# Optimizing a Trainium2 kernel written in Bass

```python
import jax, jax.numpy as jnp
from jax import lax
import numpy as np

D_MODEL = 1024
BATCH = 1
SEQ = 512
DEPTH = 2

MEM_LEN = 256
HEAD_DIM = 64
DIL_HEADS = 6
DIL_PATTERNS = ((128, 1), (512, 4), (2048, 16))
DIL_BLOCK = 128
SGU_GROUPS = 4
SGU_GROUP_DIM = 64
SGU_CHUNK = 128
RET_HEADS = 6
RET_CHUNK = 128
ROPE_BASE = 10000.0
A_WIDTH = DIL_HEADS * HEAD_DIM
B_WIDTH = SGU_GROUPS * SGU_GROUP_DIM
C_WIDTH = RET_HEADS * HEAD_DIM
MIX_WIDTH = A_WIDTH + B_WIDTH + C_WIDTH
IN_SPLITS = (A_WIDTH, A_WIDTH, A_WIDTH, B_WIDTH, B_WIDTH, C_WIDTH, C_WIDTH, C_WIDTH, C_WIDTH)
IN_WIDTH = sum(IN_SPLITS)
X_HEADS = 4
X_HEAD_DIM = D_MODEL // X_HEADS
D_FF = 4 * D_MODEL
N_NORMS = 7
EPS = 1e-6
F32 = jnp.float32

kernel_name = "hybrid_dilated_sgu_retention_block"

def rms_norm(x, g):
    xf = x.astype(F32)
    y = xf * lax.rsqrt(jnp.mean(xf * xf, axis=-1, keepdims=True) + EPS)
    return (y * g.astype(F32)).astype(x.dtype)

def dilated_branch(q, k, v, window, dilation):
    B, S, H, E = q.shape
    L = S // dilation
    span = window // dilation
    assert span <= DIL_BLOCK
    nb = -(-L // DIL_BLOCK)
    Lp = nb * DIL_BLOCK

    def to_sub(t):
        t = t.reshape(B, L, dilation, H, E).transpose(0, 2, 1, 3, 4)
        t = jnp.pad(t, ((0, 0), (0, 0), (0, Lp - L), (0, 0), (0, 0)))
        return t.reshape(B, dilation, nb, DIL_BLOCK, H, E).astype(F32)

    def band(t):
        prev = jnp.pad(t, ((0, 0), (0, 0), (1, 0), (0, 0), (0, 0), (0, 0)))[:, :, :nb]
        return jnp.concatenate([prev, t], axis=3)

    qb = to_sub(q)
    kk = band(to_sub(k))
    vv = band(to_sub(v))
    s = jnp.einsum('brnqhe,brnkhe->brnhqk', qb, kk) * (E ** -0.5)
    qi = jnp.arange(DIL_BLOCK)[:, None] + DIL_BLOCK
    ki = jnp.arange(2 * DIL_BLOCK)[None, :]
    dist = qi - ki
    blk = jnp.arange(nb)[:, None, None]
    valid = (dist >= 0) & (dist <= span) & ((blk * DIL_BLOCK - DIL_BLOCK + ki) >= 0)
    s = jnp.where(valid[:, None], s, -jnp.inf)
    m = jnp.max(s, axis=-1, keepdims=True)
    p = jnp.exp(s - m)
    den = jnp.sum(p, axis=-1)
    den_t = den.transpose(0, 1, 2, 4, 3)
    o = jnp.einsum('brnhqk,brnkhe->brnqhe', p, vv) / den_t[..., None]
    lse = (m[..., 0] + jnp.log(den)).transpose(0, 1, 2, 4, 3)

    def from_sub(t):
        rest = t.shape[4:]
        t = t.reshape((B, dilation, Lp) + rest)[:, :, :L]
        return jnp.swapaxes(t, 1, 2).reshape((B, S) + rest)

    return from_sub(o), from_sub(lse)

def dilated_attention(q, k, v):
    outs, lses = [], []
    for window, dilation in DIL_PATTERNS:
        o, l = dilated_branch(q, k, v, window, dilation)
        outs.append(o)
        lses.append(l)
    w = jax.nn.softmax(jnp.stack(lses, 0), axis=0)
    out = jnp.sum(w[..., None] * jnp.stack(outs, 0), axis=0)
    B, S = out.shape[:2]
    return out.reshape(B, S, A_WIDTH)

def spatial_gating(u, v, w_s, b_s, ln_g, ln_b):
    B, S, _ = u.shape
    u = jax.nn.gelu(u.astype(F32))
    v = jax.nn.gelu(v.astype(F32))
    mu = jnp.mean(v, axis=-1, keepdims=True)
    var = jnp.mean(jnp.square(v - mu), axis=-1, keepdims=True)
    v = (v - mu) * lax.rsqrt(var + EPS) * ln_g.astype(F32) + ln_b.astype(F32)
    v = v.reshape(B, S // SGU_CHUNK, SGU_CHUNK, SGU_GROUPS, SGU_GROUP_DIM)
    w = w_s.astype(F32) * jnp.tril(jnp.ones((SGU_CHUNK, SGU_CHUNK), F32))
    s = jnp.einsum('gij,bnjgc->bnigc', w, v) + b_s.astype(F32).T[None, None, :, :, None]
    return u * s.reshape(B, S, B_WIDTH)

def retention(q, k, v, g, positions):
    B, S, H, E = q.shape
    half = E // 2
    inv = 1.0 / (ROPE_BASE ** jnp.linspace(0.0, 1.0, half, dtype=F32))
    ang = positions.astype(F32)[..., None] * inv
    cos = jnp.cos(ang)[:, :, None, :]
    sin = jnp.sin(ang)[:, :, None, :]

    def rot(t):
        t = t.astype(F32)
        t1, t2 = t[..., :half], t[..., half:]
        return jnp.concatenate([t1 * cos - t2 * sin, t2 * cos + t1 * sin], axis=-1)

    q = rot(q)
    k = rot(k) * (E ** -0.5)
    v = v.astype(F32)
    log_g = jnp.log1p(-jnp.power(2.0, -5.0 - jnp.arange(H, dtype=F32)))
    C = RET_CHUNK
    nc = S // C
    qc = q.reshape(B, nc, C, H, E)
    kc = k.reshape(B, nc, C, H, E)
    vc = v.reshape(B, nc, C, H, E)
    idx = jnp.arange(C, dtype=F32)
    rel = idx[:, None] - idx[None, :]
    decay = jnp.where(rel[None] >= 0,
                      jnp.exp(jnp.maximum(rel, 0.0)[None] * log_g[:, None, None]), 0.0)
    inner = jnp.einsum('bnihe,bnjhe->bnhij', qc, kc) * decay
    y_in = jnp.einsum('bnhij,bnjhe->bnihe', inner, vc)
    k_dec = jnp.exp((C - 1 - idx)[:, None] * log_g[None, :])
    kv = jnp.einsum('bnjhk,bnjhv->nbhkv', kc * k_dec[:, :, None], vc)
    chunk_decay = jnp.exp(C * log_g)[None, :, None, None]

    def step(state, kv_n):
        return chunk_decay * state + kv_n, state

    _, prev = lax.scan(step, jnp.zeros((B, H, E, E), F32), kv)
    prev = prev.transpose(1, 0, 2, 3, 4)
    q_dec = jnp.exp((idx + 1.0)[:, None] * log_g[None, :])
    y_x = jnp.einsum('bnihk,bnhkv->bnihv', qc * q_dec[:, :, None], prev)
    y = (y_in + y_x).reshape(B, S, H, E)
    mu = jnp.mean(y, axis=-1, keepdims=True)
    var = jnp.mean(jnp.square(y - mu), axis=-1, keepdims=True)
    y = (y - mu) * lax.rsqrt(var + EPS)
    return jax.nn.silu(g.astype(F32)) * y.reshape(B, S, H * E)

def memory_attention(h, m, wq, wkv, wo):
    B, S, _ = h.shape
    M = m.shape[1]
    q = (h @ wq).reshape(B, S, X_HEADS, X_HEAD_DIM).astype(F32)
    kv = (m @ wkv).reshape(B, M, 2, X_HEADS, X_HEAD_DIM).astype(F32)
    s = jnp.einsum('bshe,bmhe->bhsm', q, kv[:, :, 0]) * (X_HEAD_DIM ** -0.5)
    p = jax.nn.softmax(s, axis=-1)
    o = jnp.einsum('bhsm,bmhe->bshe', p, kv[:, :, 1]).reshape(B, S, D_MODEL)
    return o.astype(h.dtype) @ wo

def setup_inputs(seed: int = 0) -> dict:
    key = jax.random.key(seed)
    ks = jax.random.split(key, 16)
    nrm = jax.random.normal
    x = nrm(ks[0], (BATCH, SEQ, D_MODEL), F32)
    mem = nrm(ks[1], (BATCH, MEM_LEN, D_MODEL), F32)
    offset = jax.random.randint(ks[2], (BATCH, 1), 0, 4096, dtype=jnp.int32)
    positions = offset + jnp.arange(SEQ, dtype=jnp.int32)[None, :]
    norm_g = 1.0 + 0.02 * nrm(ks[3], (DEPTH, N_NORMS, D_MODEL), F32)
    w_in = nrm(ks[4], (DEPTH, D_MODEL, IN_WIDTH), F32) * D_MODEL ** -0.5
    sgu_w = nrm(ks[5], (DEPTH, SGU_GROUPS, SGU_CHUNK, SGU_CHUNK), F32) * SGU_CHUNK ** -0.5
    sgu_b = 1.0 + 0.01 * nrm(ks[6], (DEPTH, SGU_GROUPS, SGU_CHUNK), F32)
    sgu_ln_g = 1.0 + 0.02 * nrm(ks[7], (DEPTH, B_WIDTH), F32)
    sgu_ln_b = 0.01 * nrm(ks[8], (DEPTH, B_WIDTH), F32)
    w_out = nrm(ks[9], (DEPTH, MIX_WIDTH, D_MODEL), F32) * MIX_WIDTH ** -0.5
    x_wq = nrm(ks[10], (DEPTH, D_MODEL, D_MODEL), F32) * D_MODEL ** -0.5
    x_wkv = nrm(ks[11], (DEPTH, D_MODEL, 2 * D_MODEL), F32) * D_MODEL ** -0.5
    x_wo = nrm(ks[12], (DEPTH, D_MODEL, D_MODEL), F32) * D_MODEL ** -0.5
    w_up = nrm(ks[13], (DEPTH, D_MODEL, D_FF), F32) * D_MODEL ** -0.5
    w_down = nrm(ks[14], (DEPTH, D_FF, D_MODEL), F32) * D_FF ** -0.5
    return {"x": x, "mem": mem, "positions": positions, "norm_g": norm_g,
            "w_in": w_in, "sgu_w": sgu_w, "sgu_b": sgu_b, "sgu_ln_g": sgu_ln_g,
            "sgu_ln_b": sgu_ln_b, "w_out": w_out, "x_wq": x_wq, "x_wkv": x_wkv,
            "x_wo": x_wo, "w_up": w_up, "w_down": w_down}

def reference(x, mem, positions, norm_g, w_in, sgu_w, sgu_b, sgu_ln_g, sgu_ln_b,
              w_out, x_wq, x_wkv, x_wo, w_up, w_down):
    B, S, _ = x.shape
    cuts = [int(c) for c in np.cumsum(IN_SPLITS)[:-1]]
    for l in range(DEPTH):
        g = norm_g[l]
        h = rms_norm(x, g[0])
        z = h @ w_in[l]
        qa, ka, va, ub, vb, qc, kc, vc, gc = jnp.split(z, cuts, axis=-1)
        head = lambda t, n: t.reshape(B, S, n, HEAD_DIM)
        ya = dilated_attention(head(qa, DIL_HEADS), head(ka, DIL_HEADS), head(va, DIL_HEADS))
        yb = spatial_gating(ub, vb, sgu_w[l], sgu_b[l], sgu_ln_g[l], sgu_ln_b[l])
        yc = retention(head(qc, RET_HEADS), head(kc, RET_HEADS), head(vc, RET_HEADS), gc, positions)
        mix = jnp.concatenate([ya, yb, yc], axis=-1).astype(x.dtype)
        x = x + rms_norm(mix @ w_out[l], g[1])
        mem_n = rms_norm(mem, g[6])
        x = x + rms_norm(memory_attention(rms_norm(x, g[2]), mem_n, x_wq[l], x_wkv[l], x_wo[l]), g[3])
        h = rms_norm(x, g[4])
        f = jnp.square(jax.nn.relu(h @ w_up[l])) @ w_down[l]
        x = x + rms_norm(f, g[5])
    return x


_drawn_inputs = setup_inputs


def setup_inputs(seed=0):
    import zlib

    import numpy as np

    out = dict(_drawn_inputs(seed))
    spreads = {}
    factors = {}
    for name, (base, spread) in spreads.items():
        noise = np.random.default_rng([zlib.crc32(name.encode()), seed]).standard_normal(out[name].shape)
        drawn = base * np.exp(spread * noise) if base else spread * noise
        out[name] = __import__('jax').numpy.asarray(drawn.astype(out[name].dtype))
    for name, factor in factors.items():
        out[name] = (out[name] * factor).astype(out[name].dtype)
    return out
```

```python
import itertools
from contextlib import ExitStack

import concourse.bass as bass
import concourse.mybir as mybir
import numpy as np

F32 = mybir.dt.float32
F32R = mybir.dt.float32r
BF16 = mybir.dt.bfloat16
I32 = mybir.dt.int32
ALU = mybir.AluOpType
ACT = mybir.ActivationFunctionType
AX_X = mybir.AxisListType.X

P = 128
DEPTH, S, D, MEM = 2, 512, 1024, 256
HD = 64
NH = 6
PAIRS = NH // 2
G = 4
XH, XD = 4, 256
FF = 4 * D
AW, BW, CW = NH * HD, G * HD, NH * HD
PATTERNS = ((128, 1), (512, 4), (2048, 16))
EPS = 1e-6
ROPE_BASE = 10000.0
HALF = HD // 2
T = S // P
MT = MEM // P
KC = D // P
BK = 4
MASKED = -1e30

A0, U0, C0 = 0, 3 * AW, 3 * AW + 2 * BW
JOBS = [
    ("va", "w_in", A0 + 2 * AW, AW, "tok", T, AW),
    ("qa", "w_in", A0, AW, "feat", PAIRS, S),
    ("ka", "w_in", A0 + AW, AW, "feat", PAIRS, S),
    ("uv", "w_in", U0, 2 * BW, "tok", T, 2 * BW),
    ("qc", "w_in", C0, CW, "tok", T, CW),
    ("kc", "w_in", C0 + CW, CW, "tok", T, CW),
    ("vc", "w_in", C0 + 2 * CW, CW, "tok", T, CW),
    ("gc", "w_in", C0 + 3 * CW, CW, "tok", T, CW),
    ("out0", "w_out", 0, 512, "tok", T, 512),
    ("out1", "w_out", 512, 512, "tok", T, 512),
    ("km0", "x_wkv", 0, 512, "feat", 4, MEM),
    ("km1", "x_wkv", 512, 512, "feat", 4, MEM),
    ("vm0", "x_wkv", D, 512, "tok", MT, 512),
    ("vm1", "x_wkv", D + 512, 512, "tok", MT, 512),
    ("qx0", "x_wq", 0, 512, "feat", 4, S),
    ("qx1", "x_wq", 512, 512, "feat", 4, S),
    ("wo0", "x_wo", 0, 512, "tok", T, 512),
    ("wo1", "x_wo", 512, 512, "tok", T, 512),
]
KB = D // (BK * P)
JOB = {j[0]: i for i, j in enumerate(JOBS)}
FIRST_BLOCK = {j[0]: KB * i for i, j in enumerate(JOBS)}
HEAD_BLOCKS = KB * len(JOBS)
GROUPS = 4
GROUP_JOBS = ("up0", "up1", "dn0", "dn1")
GROUP_BLOCKS = KB * len(GROUP_JOBS)
BLOCKS = HEAD_BLOCKS + GROUPS * GROUP_BLOCKS
WSLOTS = 2
assert BLOCKS % WSLOTS == 0 and GROUP_BLOCKS % WSLOTS == 0 and FF == GROUPS * KB * BK * P

TILES_BEFORE = {}
_n = 0
for _j in JOBS:
    TILES_BEFORE[_j[0]] = _n
    _n += _j[5]
HEAD_TILES = _n
GROUP_TILES = 4 * KB * len(GROUP_JOBS)
UP_TILES = 8

def bank_users():
    last = [None] * 4
    users = {}
    for name, _, _, _, _, tiles, _ in JOBS:
        for t in range(tiles):
            users[name, t] = last[t]
            last[t] = TILES_BEFORE[name] + t
    return users, last
BANK_USER, HEAD_LAST = bank_users()

def stats_order():
    order = [("n1", t) for t in range(T)] + [("mem", t) for t in range(MT)]
    order += [("e1", t) for t in range(T)] + [("n2", t) for t in range(T)]
    for s in range(T + 1):
        order += [("e2", s)] if s < T else []
        order += [("n3", s - 1)] if s >= 1 else []
    return order + [("e3", t) for t in range(T)]
STATS = {k: i for i, k in enumerate(stats_order())}
NORMED = {k: i for i, k in enumerate([("n1", t) for t in range(T)] + [("mem", t) for t in range(MT)]
                                     + [("n2", t) for t in range(T)] + [("n3", t) for t in range(T)])}
BRANCHED = {(e, t): T * i + t for i, e in enumerate(("e1", "e2", "e3")) for t in range(T)}
TURNED = {k: i for i, k in enumerate(
    [("n1", t) for t in range(T)] + [("mix", t) for t in range(T)] + [("mem", t) for t in range(MT)]
    + [("n2", t) for t in range(T)] + [("n3", t) for t in range(T)])}

BLOCK_TILES = [j[5] for j in JOBS for _ in range(KB)] + [4] * (GROUPS * GROUP_BLOCKS)
LAYER_TILES = sum(BLOCK_TILES)


def done(b, t=None):
    if b < 0:
        return -sum(BLOCK_TILES[b + 1:]) if b < -1 else 0
    return sum(BLOCK_TILES[:b]) + (BLOCK_TILES[b] if t is None else t + 1)


UNITS = T * NH
STEP_BLOCK = FIRST_BLOCK["uv"]
XUNITS = XH // 2 * T
DVE_LINKS = 37
POOL_LINKS = 40

GAIN = {"n1": 0, "e1": 1, "n2": 2, "e2": 3, "n3": 4, "e3": 5, "mem": 6}
GAIN_SLOT = {"n1": 0, "mem": 1, "n2": 0, "n3": 1, "e1": 2, "e2": 2, "e3": 2}


def shape_constants():
    i = np.arange(S)[:, None]
    j = np.arange(S)[None, :]
    count = np.zeros((S, S))
    for window, dilation in PATTERNS:
        count += (i >= j) & ((i - j) % dilation == 0) & (i - j <= window)
    logs = np.where(count > 0, np.log(np.maximum(count, 1)), MASKED).astype(np.float32)
    log_count = np.concatenate([logs[t * P:(t + 1) * P, :(t + 1) * P] for t in range(T)], axis=1)
    a = np.arange(P)
    upper = (a[:, None] <= a[None, :]).astype(np.float32)
    gamma = 1.0 - 2.0 ** (-5.0 - np.arange(NH))
    pos = np.arange(S, dtype=np.float64).reshape(T, P).T[:, :, None]
    decay = np.concatenate([gamma ** (pos + 1.0), gamma ** -(pos + 1.0) * HD ** -0.5], axis=2)
    inv = 1.0 / (np.float32(ROPE_BASE) ** np.linspace(0.0, 1.0, HALF, dtype=np.float32))
    return {
        "c_ident": np.eye(P, dtype=np.float32),
        "c_logcount": log_count,
        "c_upper": upper,
        "c_decay": decay.astype(np.float32),
        "c_inv": np.tile(inv.astype(np.float32)[None, :], (P, 1)),
    }


TURN = 2.0 * np.pi


def turn_pieces():
    pieces, left = [], TURN
    for _ in range(4):
        unit = 2.0 ** (np.floor(np.log2(left)) - 7)
        pieces.append(float(np.floor(left / unit) * unit))
        left -= pieces[-1]
    return pieces


TURN_PIECES = turn_pieces()
ARENA_KIB = 53


def spread(ap, n):
    return ap.rearrange("p (a b) -> p a b", b=1).broadcast_to([ap.shape[0], ap.shape[1], n])


def again(ap, n):
    return ap.rearrange("p (b a) -> p b a", b=1).broadcast_to([ap.shape[0], n, ap.shape[1]])


def mask_offset(t):
    return P * (t * (t + 1) // 2)


def trunk(nc, x, mem, positions, norm_g, w_in, sgu_w, sgu_b, sgu_ln_g, sgu_ln_b, w_out,
          x_wq, x_wkv, x_wo, w_up, w_down, c_ident, c_logcount, c_upper, c_decay, c_inv, out):
    weights = {"w_in": w_in, "w_out": w_out, "x_wq": x_wq, "x_wkv": x_wkv, "x_wo": x_wo}
    with ExitStack() as ctx:
        def sb(name, shape, dt=F32):
            return ctx.enter_context(nc.sbuf_tensor(name, shape, dt))

        xs = sb("xs", [P, T, D])
        hT_hi = sb("hT_hi", [P, KC, S], F32R)
        hT_lo = sb("hT_lo", [P, KC, S], F32R)
        w_raw = sb("w_raw", [P, WSLOTS, BK, 512])
        w_hi = sb("w_hi", [P, WSLOTS, BK, 512], F32R)
        w_lo = sb("w_lo", [P, WSLOTS, BK, 512], F32R)
        ys = sb("ys", [P, T, D])
        gains = sb("gains", [P, 3, D])
        hs = sb("hs", [P, 2, D])
        squares = sb("squares", [P, 2, D], BF16)
        ident = sb("ident", [P, P])
        log_count = sb("log_count", [P, mask_offset(T)])
        upper = sb("upper", [P, P])
        decay = sb("decay", [P, T, 2 * NH])
        inv = sb("inv", [P, HALF])
        cos = sb("cos", [P, T, HALF])
        sin = sb("sin", [P, T, HALF])
        angle = sb("angle", [P, T, HALF])
        turns = sb("turns", [P, T, HALF])
        pos_i = sb("pos_i", [P, T], I32)
        pos_f = sb("pos_f", [P, T])
        minus_half = sb("minus_half", [P, 8])
        sumsq = sb("sumsq", [P, 2, 1])
        meansq = sb("meansq", [P, 2, 1])
        rstd = sb("rstd", [P, 4, 1])
        sgu_raw = sb("sgu_raw", [P, G, P])
        sgu_T = sb("sgu_T", [P, G, P])
        sgu_bias = sb("sgu_bias", [P, G])
        ln_gain = sb("ln_gain", [P, BW])
        ln_shift = sb("ln_shift", [P, BW])
        ln_stats = sb("ln_stats", [P, T, 6])
        ln_mv = sb("ln_mv", [P, T, 2])
        ln_ve = sb("ln_ve", [P, T])
        ln_rstd = sb("ln_rstd", [P, T])
        neg_max = sb("neg_max", [P, 2, 2])
        den = sb("den", [P, UNITS])
        rden = sb("rden", [P, UNITS])
        x_den = sb("x_den", [P, XUNITS, 2])
        x_rden = sb("x_rden", [P, XUNITS, 2])
        state = sb("state", [P, 2, PAIRS, P])
        x_neg = sb("x_neg", [P, 2, 2])
        x_top = sb("x_top", [P, 2, 2])
        gn_sum = sb("gn_sum", [P, NH])
        gn_mean = sb("gn_mean", [P, NH])
        gn_var = sb("gn_var", [P, NH])
        gn_ve = sb("gn_ve", [P, NH])
        gn_rstd = sb("gn_rstd", [P, NH])

        KIB = 1024
        arena_start = -(-nc.sbuf_base // 32) * 32
        ctx.enter_context(nc.sbuf_tensor("arena", [P, ARENA_KIB * KIB // 4], F32))

        def part(name, kib, shape, dt=F32):
            return nc.alloc_sbuf_tensor_at(name, shape, dt, offset=arena_start + int(kib * KIB))

        qaT = part("qaT", 0, [P, PAIRS, S])
        kaT = part("kaT", 6, [P, PAIRS, S])
        va = part("va", 12, [P, T, AW])
        vs = part("vs", 18, [P, T, BW])
        qkc = part("qkc", 22, [P, T, 2 * CW])
        vc = part("vc", 34, [P, T, CW])
        probs = part("probs", 40, [P, 2, S])
        probsT = part("probsT", 44, [P, 2, S])
        rot = part("rot", 48, [P, 3, 2 * NH * HALF])
        qkT = part("qkT", 0, [P, 2, CW])
        innerT = part("innerT", 3, [P, NH, P])
        yc = part("yc", 6, [P, T, CW])
        yc2 = part("yc2", 12, [P, CW])
        kmT = part("kmT", 0, [P, KC, MEM])
        vm = part("vm", 8, [P, MT, D])
        x_probs = part("x_probs", 16, [P, 2, 512])
        x_probsT = part("x_probsT", 20, [P, 2, 512])
        mem_in = part("mem_in", 40, [P, MT, D])
        memT_hi = part("memT_hi", 24, [P, KC, MEM], F32R)
        memT_lo = part("memT_lo", 32, [P, KC, MEM], F32R)
        qxT = part("qxT", 24, [P, KC, S])
        uT_hi = part("uT_hi", 0, [P, KC, S], F32R)
        uT_lo = part("uT_lo", 16, [P, KC, S], F32R)
        relu = part("relu", 32, [P, 2, S])

        proj = ctx.enter_context(nc.psum_tensor("proj", [P, 4, 512], F32))
        work = ctx.enter_context(nc.psum_tensor("work", [P, 4, 512], F32))

        per_layer, start_of = {}, {}

        def counted(name, per, start=0):
            sem = ctx.enter_context(nc.semaphore(name))
            per_layer[sem.name], start_of[sem.name] = per, start
            return sem

        def nth(sem, l, n):
            return l * per_layer[sem.name] + (n + start_of[sem.name])

        waits_passed = ctx.enter_context(nc.semaphore("waits_passed"))
        const_loaded = ctx.enter_context(nc.semaphore("const_loaded"))
        x_loaded = ctx.enter_context(nc.semaphore("x_loaded"))
        setup_done = ctx.enter_context(nc.semaphore("setup_done"))
        dve_setup = ctx.enter_context(nc.semaphore("dve_setup"))
        trig_done = ctx.enter_context(nc.semaphore("trig_done"))
        stored = ctx.enter_context(nc.semaphore("stored"))
        w_loaded = [counted(f"w_loaded{i}", 16 * BLOCKS // WSLOTS) for i in range(WSLOTS)]
        w_hi_done = counted("w_hi_done", BLOCKS)
        w_lo_done = counted("w_lo_done", BLOCKS, WSLOTS)
        gain_loaded = {k: counted(f"gain_{k}", 16) for k in GAIN}
        sgu_loaded = counted("sgu_loaded", 64)
        mem_loaded = counted("mem_loaded", 16)
        tile_done = counted("tile_done", LAYER_TILES, 4 * WSLOTS)
        emptied = counted("emptied", HEAD_TILES + GROUPS * UP_TILES, 1)
        added = counted("added", GROUPS * UP_TILES, T)
        summed = counted("summed", len(STATS))
        rooted = counted("rooted", len(STATS), 2)
        normed = counted("normed", len(NORMED), 1)
        branched = counted("branched", len(BRANCHED), 1)
        x_ready = counted("x_ready", len(BRANCHED), T)
        turned = counted("turned", 2 * len(TURNED), 1)
        turned_hi = counted("turned_hi", 2 * len(TURNED), 1)
        turned_lo = counted("turned_lo", 2 * len(TURNED), 4)
        y_zeroed = counted("y_zeroed", 1)
        hidden_sq = counted("hidden_sq", GROUPS * UP_TILES, 1)
        hidden_hi = counted("hidden_hi", GROUPS * UP_TILES, 1)
        hidden_lo = counted("hidden_lo", GROUPS * UP_TILES, 2)
        sgu_turned = counted("sgu_turned", 1)
        sgu_ready = counted("sgu_ready", 1, 1)
        gelu_done = counted("gelu_done", 1)
        ln_var = counted("ln_var", 1)
        ln_root = counted("ln_root", 1)
        ln_scaled = counted("ln_scaled", 1)
        ln_done = counted("ln_done", 1)
        gated = counted("gated", 2)
        gate_out = counted("gate_out", 1)
        scored = counted("scored", UNITS)
        masked = counted("masked", UNITS, 2)
        exped = counted("exped", UNITS)
        p_turned = counted("p_turned", UNITS, 2)
        p_copied = counted("p_copied", UNITS, 1)
        weighed = counted("weighed", UNITS, 2)
        a_out = counted("a_out", T, 1)
        rotated = counted("rotated", T)
        c_turned = counted("c_turned", T)
        c_copied = counted("c_copied", T, 1)
        c_inner = counted("c_inner", T)
        c_masked = counted("c_masked", T, 1)
        c_kv = counted("c_kv", T - 1)
        c_state = counted("c_state", T - 1, 1)
        c_y = counted("c_y", T)
        c_centred = counted("c_centred", T, 1)
        gn_var_done = counted("gn_var_done", T)
        gn_root = counted("gn_root", T)
        c_out = counted("c_out", T)
        x_scored = counted("x_scored", XUNITS)
        x_max = counted("x_max", XUNITS, 1)
        x_exped = counted("x_exped", XUNITS, 2)
        x_normed = counted("x_normed", XUNITS)
        x_turned = counted("x_turned", XUNITS, 2)
        x_copied = counted("x_copied", XUNITS, 1)
        x_weighed = counted("x_weighed", XUNITS, 2)
        x_hi = counted("x_hi", XUNITS)
        x_lo = counted("x_lo", XUNITS, 1)
        dve_link = counted("dve_link", DVE_LINKS)
        pool_link = counted("pool_link", POOL_LINKS)

        def values(eng, *counts):
            return [eng.snap(count) for count in counts]

        def start_counts(eng, *sems):
            for sem in sems:
                eng.sem_inc(sem, start_of[sem.name])

        block = ctx.enter_context(nc.Block())

        @block.sync
        def _(sp):
            for dst, src in ((ident, c_ident), (inv, c_inv), (upper, c_upper), (decay, c_decay),
                             (log_count, c_logcount), (pos_i, positions)):
                sp.dma_start(dst[:], src).then_inc(const_loaded, 16)
            for t in range(T):
                sp.dma_start(xs[:, t], x[0, t * P:(t + 1) * P]).then_inc(x_loaded, 16)

            def load_block(l, b, src):
                cols = src.shape[-1]
                sp.wait_ge(w_lo_done, nth(w_lo_done, l, b - WSLOTS + 1))
                sp.sem_inc(waits_passed, 1)
                sp.dma_start(w_raw[:, b % WSLOTS, :, 0:cols],
                             src.rearrange("a (k p) c -> p (a k) c", p=P)).then_inc(w_loaded[b % WSLOTS], 16)

            def load_gain(l, k):
                sp.dma_start(gains[:, GAIN_SLOT[k]],
                             norm_g[bass.ds(l, 1), GAIN[k]].broadcast_to([P, D])).then_inc(gain_loaded[k], 16)

            with sp.Fori(0, DEPTH) as l:
                sp.wait_ge(normed, nth(normed, l, 0))
                sp.sem_inc(waits_passed, 1)
                load_gain(l, "n1")
                for name, weight, c, cols, _, _, _ in JOBS:
                    for kb in range(KB):
                        b = FIRST_BLOCK[name] + kb
                        load_block(l, b, weights[weight][bass.ds(l, 1), kb * BK * P:(kb + 1) * BK * P, c:c + cols])
                    if name == "va":
                        sp.wait_ge(normed, nth(normed, l, 0))
                        sp.dma_start(sgu_raw[:], sgu_w[bass.ds(l, 1)].rearrange("a g i j -> i (a g) j")).then_inc(sgu_loaded, 16)
                        sp.dma_start(sgu_bias[:], sgu_b[bass.ds(l, 1)].rearrange("a i g -> i (a g)")).then_inc(sgu_loaded, 16)
                        sp.dma_start(ln_gain[:], sgu_ln_g[bass.ds(l, 1)].broadcast_to([P, BW])).then_inc(sgu_loaded, 16)
                        sp.dma_start(ln_shift[:], sgu_ln_b[bass.ds(l, 1)].broadcast_to([P, BW])).then_inc(sgu_loaded, 16)
                    if name == "kc":
                        sp.wait_ge(normed, nth(normed, l, NORMED["n1", T - 1] + 1))
                        sp.sem_inc(waits_passed, 1)
                        load_gain(l, "mem")
                        sp.wait_ge(branched, nth(branched, l, 0))
                        sp.sem_inc(waits_passed, 1)
                        load_gain(l, "e1")
                        sp.wait_ge(normed, nth(normed, l, NORMED["n1", T - 1] + 1))
                        sp.sem_inc(waits_passed, 1)
                        load_gain(l, "n2")
                    if name == "gc":
                        sp.wait_ge(weighed, nth(weighed, l, UNITS))
                        sp.dma_start(mem_in[:], mem[0].rearrange("(t p) d -> p t d", p=P)).then_inc(mem_loaded, 16)
                    if name == "qx0":
                        sp.wait_ge(normed, nth(normed, l, NORMED["mem", MT - 1] + 1))
                        sp.sem_inc(waits_passed, 1)
                        load_gain(l, "n3")
                        sp.wait_ge(branched, nth(branched, l, BRANCHED["e1", T - 1] + 1))
                        sp.sem_inc(waits_passed, 1)
                        load_gain(l, "e2")
                with sp.Fori(0, GROUPS) as g:
                    for j in range(2):
                        for kb in range(KB):
                            b = HEAD_BLOCKS + KB * j + kb
                            sp.wait_ge(w_lo_done, nth(w_lo_done, l, g * GROUP_BLOCKS + (b - WSLOTS + 1)))
                            sp.sem_inc(waits_passed, 1)
                            sp.dma_start(w_raw[:, b % WSLOTS],
                                         w_up[bass.ds(l, 1), kb * BK * P:(kb + 1) * BK * P,
                                              bass.ds(g * (FF // GROUPS) + j * 512, 512)]
                                         .rearrange("a (k p) c -> p (a k) c", p=P)).then_inc(w_loaded[b % WSLOTS], 16)
                    for j in range(2):
                        for kb in range(KB):
                            b = HEAD_BLOCKS + KB * (2 + j) + kb
                            sp.wait_ge(w_lo_done, nth(w_lo_done, l, g * GROUP_BLOCKS + (b - WSLOTS + 1)))
                            sp.sem_inc(waits_passed, 1)
                            sp.dma_start(w_raw[:, b % WSLOTS],
                                         w_down[bass.ds(l, 1), bass.ds(g * (FF // GROUPS) + kb * BK * P, BK * P),
                                                j * 512:(j + 1) * 512]
                                         .rearrange("a (k p) c -> p (a k) c", p=P)).then_inc(w_loaded[b % WSLOTS], 16)
                sp.wait_ge(branched, nth(branched, l, BRANCHED["e2", T - 1] + 1))
                sp.sem_inc(waits_passed, 1)
                load_gain(l, "e3")
            for t in range(T):
                sp.wait_ge(x_ready, nth(x_ready, DEPTH - 1, BRANCHED["e3", t] + 1))
                sp.dma_start(out[0, t * P:(t + 1) * P], xs[:, t]).then_inc(stored, 16)
            sp.wait_ge(stored, 16 * T)

        @block.tensor
        def _(pe):
            start_counts(pe, tile_done, turned, p_turned, weighed, x_turned, x_weighed)
            pe.wait_ge(const_loaded, 16 * 6)

            def three_passes(dst, l_hi, l_lo, r_hi, r_lo, first, last):
                nc.tensor.matmul(dst, l_hi, r_hi, start=first, stop=False)
                nc.tensor.matmul(dst, l_hi, r_lo, start=False, stop=False)
                return nc.tensor.matmul(dst, l_lo, r_hi, start=False, stop=last)

            def block_tile(b_slot, kb, mode, t, moving, hi, lo, cols):
                for k in range(BK):
                    c = kb * BK + k
                    first, last = c == 0, kb == KB - 1 and k == BK - 1
                    if mode == "tok":
                        r = slice(t * P, (t + 1) * P)
                        mm = three_passes(proj[:, t, 0:moving], hi[:, c, r], lo[:, c, r],
                                          w_hi[:, b_slot, k, 0:cols], w_lo[:, b_slot, k, 0:cols], first, last)
                    else:
                        r = slice(t * P, (t + 1) * P)
                        mm = three_passes(proj[:, t, 0:moving], w_hi[:, b_slot, k, r], w_lo[:, b_slot, k, r],
                                          hi[:, c, 0:moving], lo[:, c, 0:moving], first, last)
                return mm

            def turn(l, key, src):
                n = TURNED[key]
                pe.wait_ge(turned_lo, nth(turned_lo, l, 2 * n - 2))
                for half in range(2):
                    for k in range(BK):
                        c = half * BK + k
                        mm = nc.tensor.transpose(work[:, 2 * (n % 2) + half, k * P:(k + 1) * P],
                                                 src[:, c * P:(c + 1) * P], ident[:])
                    mm.then_inc(turned, 1)

            def turned_in(l, key):
                pe.wait_ge(turned_lo, nth(turned_lo, l, 2 * TURNED[key] + 2))
                pe.sem_inc(waits_passed, 1)

            def a_scores(l, u):
                t, h = divmod(u, NH)
                lo, n = HD * (h % 2), (t + 1) * P
                if u == 0:
                    pe.wait_ge(emptied, nth(emptied, l, TILES_BEFORE["uv"]))
                    pe.wait_ge(turned_lo, nth(turned_lo, l, 2 * TURNED["n1", T - 1] + 2))
                    pe.wait_ge(sgu_ready, nth(sgu_ready, l, 1))
                pe.wait_ge(masked, nth(masked, l, u - 1))
                nc.tensor.matmul(work[:, u % 2, 0:n], qaT[lo:lo + HD, h // 2, t * P:(t + 1) * P],
                                 kaT[lo:lo + HD, h // 2, 0:n], start=True, stop=True).then_inc(scored, 1)

            def a_turn(l, u):
                pe.wait_ge(exped, nth(exped, l, u + 1))
                pe.wait_ge(p_copied, nth(p_copied, l, u))
                for j in range(u // NH + 1):
                    mm = nc.tensor.transpose(work[:, 2, j * P:(j + 1) * P], probs[:, u % 2, j * P:(j + 1) * P], ident[:])
                mm.then_inc(p_turned, 1)

            def a_weigh(l, u):
                t, h = divmod(u, NH)
                pe.wait_ge(p_copied, nth(p_copied, l, u + 1))
                pe.wait_ge(a_out, nth(a_out, l, t))
                for j in range(t + 1):
                    mm = nc.tensor.matmul(work[:, 3, h * HD:(h + 1) * HD], probsT[:, u % 2, j * P:(j + 1) * P],
                                          va[:, j, h * HD:(h + 1) * HD], start=(j == 0), stop=(j == t))
                mm.then_inc(weighed, 1)

            def a_step(l, j):
                if j < UNITS:
                    a_scores(l, j)
                if 1 <= j <= UNITS:
                    a_turn(l, j - 1)
                if 2 <= j < UNITS + 2:
                    a_weigh(l, j - 2)

            def sgu_weights(l):
                pe.wait_ge(sgu_loaded, nth(sgu_loaded, l, 64))
                pe.wait_ge(turned_lo, nth(turned_lo, l, 2 * TURNED["n1", T - 1] + 2))
                for g in range(G):
                    mm = nc.tensor.transpose(work[:, 0, g * P:(g + 1) * P], sgu_raw[:, g], ident[:])
                mm.then_inc(sgu_turned, 1)

            def sgu_mix(l):
                pe.wait_ge(ln_done, nth(ln_done, l, 1))
                pe.wait_ge(masked, nth(masked, l, UNITS))
                for g in range(G):
                    mm = nc.tensor.matmul(work[:, g // 2, (g % 2) * 256:(g % 2 + 1) * 256].rearrange("p (t c) -> p t c", t=T),
                                          sgu_T[:, g], vs[:, :, g * HD:(g + 1) * HD], start=True, stop=True)
                    if g % 2:
                        mm.then_inc(gated, 1)

            def c_turn(l, c):
                if c == 0:
                    pe.wait_ge(gate_out, nth(gate_out, l, 1))
                    pe.wait_ge(a_out, nth(a_out, l, T))
                pe.wait_ge(rotated, nth(rotated, l, c + 1))
                pe.wait_ge(c_copied, nth(c_copied, l, c))
                pe.wait_ge(c_state, nth(c_state, l, c))
                for i in range(2):
                    for p in range(PAIRS):
                        mm = nc.tensor.transpose(work[:, i, p * P:(p + 1) * P],
                                                 qkc[:, c, i * CW + p * P:i * CW + (p + 1) * P], ident[:])
                mm.then_inc(c_turned, 1)

            def c_products(l, c):
                pe.wait_ge(c_copied, nth(c_copied, l, c + 1))
                pe.wait_ge(c_masked, nth(c_masked, l, c))
                pe.wait_ge(c_centred, nth(c_centred, l, c))
                for h in range(NH):
                    lo, p = HD * (h % 2), h // 2
                    mm = nc.tensor.matmul(work[:, 2 + h % 2, p * P:(p + 1) * P],
                                          qkT[lo:lo + HD, 1, p * P:(p + 1) * P],
                                          qkT[lo:lo + HD, 0, p * P:(p + 1) * P], start=True, stop=True)
                mm.then_inc(c_inner, 1)
                pe.wait_ge(emptied, nth(emptied, l, TILES_BEFORE["vc"] + c + 1))
                if c == T - 1:
                    return
                for p in range(PAIRS):
                    mm = nc.tensor.matmul(work[:, 0, p * P:(p + 1) * P], qkc[:, c, CW + p * P:CW + (p + 1) * P],
                                          vc[:, c, p * P:(p + 1) * P], start=True, stop=True)
                mm.then_inc(c_kv, 1)

            def c_read(l, c):
                pe.wait_ge(c_masked, nth(c_masked, l, c + 1))
                pe.wait_ge(c_state, nth(c_state, l, c))
                for p in range(PAIRS):
                    if c > 0:
                        nc.tensor.matmul(work[:, 2, p * P:(p + 1) * P], qkT[:, 0, p * P:(p + 1) * P], state[:, c % 2, p],
                                         start=True, stop=False, skip_group_check=True)
                    for h in (2 * p, 2 * p + 1):
                        mm = nc.tensor.matmul(work[:, 2, h * HD:(h + 1) * HD], innerT[:, h], vc[:, c, h * HD:(h + 1) * HD],
                                              start=(c == 0), stop=True, skip_group_check=True)
                mm.then_inc(c_y, 1)

            def c_slot(l, k):
                if k % 2 == 0:
                    if k >= 2:
                        c_read(l, k // 2 - 1)
                    if k < 2 * T:
                        c_turn(l, k // 2)
                elif k < 2 * T:
                    c_products(l, k // 2)

            def x_scores(l, u):
                pair, t = divmod(u, T)
                if u == 0:
                    pe.wait_ge(emptied, nth(emptied, l, TILES_BEFORE["vm0"]))
                    pe.wait_ge(turned_lo, nth(turned_lo, l, 2 * TURNED["n2", T - 1] + 2))
                pe.wait_ge(emptied, nth(emptied, l, TILES_BEFORE["qx1" if pair == 0 else "wo0"]))
                pe.wait_ge(x_exped, nth(x_exped, l, u - 1))
                for i in range(2):
                    for k in range(2):
                        c = 2 * (2 * pair + i) + k
                        mm = nc.tensor.matmul(work[:, u % 2, i * MEM:(i + 1) * MEM], qxT[:, c, t * P:(t + 1) * P],
                                              kmT[:, c, :], start=(k == 0), stop=(k == 1))
                mm.then_inc(x_scored, 1)

            def x_turn(l, u):
                pe.wait_ge(x_normed, nth(x_normed, l, u + 1))
                pe.wait_ge(x_copied, nth(x_copied, l, u))
                for j in range(2 * MT):
                    mm = nc.tensor.transpose(work[:, 2, j * P:(j + 1) * P], x_probs[:, u % 2, j * P:(j + 1) * P], ident[:])
                mm.then_inc(x_turned, 1)

            def x_weigh(l, u):
                pair = u // T
                pe.wait_ge(x_copied, nth(x_copied, l, u + 1))
                pe.wait_ge(x_lo, nth(x_lo, l, u))
                pe.wait_ge(emptied, nth(emptied, l, TILES_BEFORE["qx0"]))
                for k in range(BK):
                    i = k * P // XD
                    for j in range(MT):
                        mm = nc.tensor.matmul(work[:, 3, k * P:(k + 1) * P], vm[:, j, (pair * BK + k) * P:(pair * BK + k + 1) * P],
                                              x_probsT[:, u % 2, (i * MT + j) * P:(i * MT + j + 1) * P],
                                              start=(j == 0), stop=(j == MT - 1))
                mm.then_inc(x_weighed, 1)

            def x_step(l, j):
                if j < XUNITS:
                    x_scores(l, j)
                if 2 <= j < XUNITS + 2:
                    x_weigh(l, j - 2)
                if 1 <= j <= XUNITS:
                    x_turn(l, j - 1)

            def before_tile(l, b, t):
                if b == FIRST_BLOCK["va"]:
                    if t == 0:
                        turn_ahead(l, "n1", 0)
                        turn_ahead(l, "n1", 1)
                    turned_in(l, ("n1", t))
                if b == FIRST_BLOCK["out0"]:
                    turned_in(l, ("mix", t))
                if b in (FIRST_BLOCK["wo0"], FIRST_BLOCK["wo0"] + 1):
                    pe.wait_ge(x_lo, nth(x_lo, l, (b - FIRST_BLOCK["wo0"]) * T + t + 1))
                    pe.sem_inc(waits_passed, 1)

            def turn_ahead(l, phase, t):
                if phase == "n1":
                    pe.wait_ge(normed, nth(normed, l, NORMED["n1", t] + 1))
                    turn(l, ("n1", t), hs[:, t % 2])
                else:
                    pe.wait_ge(c_out, nth(c_out, l, t + 1))
                    if t == 1:
                        pe.wait_ge(c_centred, nth(c_centred, l, T))
                    turn(l, ("mix", t), ys[:, t])

            def after_tile(l, b, t):
                if b == FIRST_BLOCK["ka"] + 1 and t == 0:
                    sgu_weights(l)
                j = (b - STEP_BLOCK) * T + t
                if 0 <= j < UNITS + 2:
                    a_step(l, j)
                if j == UNITS + 2:
                    sgu_mix(l)
                k = (b - FIRST_BLOCK["gc"]) * T + t + 2
                if 0 <= k <= 2 * T:
                    c_slot(l, k)
                if b == FIRST_BLOCK["va"] and t < T - 2:
                    turn_ahead(l, "n1", t + 2)
                if b == FIRST_BLOCK["out0"] - 1 and t >= T - 2:
                    turn_ahead(l, "mix", t - T + 2)
                if b == FIRST_BLOCK["out0"] and t < T - 2:
                    turn_ahead(l, "mix", t + 2)
                if b == FIRST_BLOCK["out0"] + 1 and t < MT:
                    pe.wait_ge(normed, nth(normed, l, NORMED["mem", t] + 1))
                    turn(l, ("mem", t), hs[:, t])
                if b == FIRST_BLOCK["qx1"] + 1 and t % 2:
                    x_step(l, t // 2)
                if b == FIRST_BLOCK["wo0"]:
                    x_step(l, XUNITS - 2 + t)

            def after_block(l, b):
                if b == FIRST_BLOCK["qx1"] + 1:
                    for j in range(2, XUNITS - 2):
                        x_step(l, j)
                t = b - (FIRST_BLOCK["km0"] + 1)
                if 0 <= t < T:
                    pe.wait_ge(normed, nth(normed, l, NORMED["n2", t] + 1))
                    turn(l, ("n2", t), hs[:, t % 2])
                if b == HEAD_BLOCKS - 1:
                    for t in range(T):
                        pe.wait_ge(normed, nth(normed, l, NORMED["n3", t] + 1))
                        turn(l, ("n3", t), hs[:, t % 2])

            def mlp_group(l, g):
                for i, name in enumerate(GROUP_JOBS):
                    for kb in range(KB):
                        b = HEAD_BLOCKS + KB * i + kb
                        pe.wait_ge(w_lo_done, nth(w_lo_done, l, g * GROUP_BLOCKS + (b + 1)))
                        for t in range(4):
                            if kb == 0:
                                if name == "up0":
                                    pe.wait_ge(emptied, nth(emptied, l, HEAD_TILES))
                                    pe.wait_ge(added, nth(added, l, g * UP_TILES + (t + 1 - T)))
                                elif name in ("up1", "dn0"):
                                    pe.wait_ge(emptied, nth(emptied, l, g * UP_TILES + (HEAD_TILES + 4 * (i - 1) + t + 1)))
                                else:
                                    pe.wait_ge(added, nth(added, l, g * UP_TILES + (t + 1)))
                            if name == "dn0" and t == 0:
                                pe.wait_ge(hidden_lo, nth(hidden_lo, l, g * UP_TILES + 4 * (kb + 1)))
                            if i < 2:
                                mm = block_tile(b % WSLOTS, kb, "feat", t, S, hT_hi, hT_lo, 512)
                            else:
                                mm = block_tile(b % WSLOTS, kb, "tok", t, 512, uT_hi, uT_lo, 512)
                            mm.then_inc(tile_done, 1)

            with pe.Fori(0, DEPTH) as l:
                for name, _, _, cols, mode, tiles, moving in JOBS:
                    if name == "km0":
                        turned_in(l, ("mem", MT - 1))
                    if name == "qx0":
                        turned_in(l, ("n2", T - 1))
                    hi, lo = (memT_hi, memT_lo) if name[1:2] == "m" and name[0] in "kv" else (hT_hi, hT_lo)
                    for kb in range(KB):
                        b = FIRST_BLOCK[name] + kb
                        for t in range(tiles):
                            before_tile(l, b, t)
                            if t == 0:
                                pe.wait_ge(w_lo_done, nth(w_lo_done, l, b + 1))
                            if kb == 0:
                                user = BANK_USER[name, t]
                                if user is None:
                                    pe.wait_ge(added, nth(added, l, t + 1 - T))
                                else:
                                    pe.wait_ge(emptied, nth(emptied, l, user + 1))
                            mm = block_tile(b % WSLOTS, kb, mode, t, moving, hi, lo, cols)
                            mm.then_inc(tile_done, 1)
                            after_tile(l, b, t)
                        after_block(l, b)
                turned_in(l, ("n3", T - 1))
                with pe.Fori(0, GROUPS) as g:
                    mlp_group(l, g)

        @block.scalar
        def _(act):
            start_counts(act, emptied, turned_hi, hidden_hi, p_copied, c_copied, x_exped, x_copied)
            act.wait_ge(trig_done, 1)
            nc.scalar.activation(sin[:], angle[:], ACT.Sin)
            nc.scalar.activation(cos[:], turns[:], ACT.Sin).then_inc(trig_done, 1)

            def split_hi(l, b, cols=512, g=0, of_next=False):
                slot, at = b % WSLOTS, (GROUP_BLOCKS if of_next else 0) + b
                act.wait_ge(w_loaded[slot], nth(w_loaded[slot], l, g * (16 * GROUP_BLOCKS // WSLOTS) + 16 * (at // WSLOTS + 1)))
                act.wait_ge(tile_done, nth(tile_done, l, g * GROUP_TILES + done(at - WSLOTS)))
                nc.scalar.activation(w_hi[:, slot, :, 0:cols], w_raw[:, slot, :, 0:cols], ACT.Copy).then_inc(w_hi_done, 1)

            def head_split(l, b):
                split_hi(l, b, JOBS[b // KB][3] if b < HEAD_BLOCKS else 512)

            def sum_squares(l, key, src):
                r = STATS[key]
                act.wait_ge(rooted, nth(rooted, l, r - 1))
                nc.scalar.activation(squares[:, r % 2], src, ACT.Square, accum_out=sumsq[:, r % 2]).then_inc(summed, 1)

            def turn_hi(l, key, dst, t):
                n = TURNED[key]
                for half in range(2):
                    act.wait_ge(turned, nth(turned, l, 2 * n + half + 1))
                    nc.scalar.activation(dst[:, half * BK:(half + 1) * BK, t * P:(t + 1) * P],
                                         work[:, 2 * (n % 2) + half].rearrange("p (k c) -> p k c", k=BK),
                                         ACT.Copy).then_inc(turned_hi, 1)

            def empty(l, b, t):
                name, _, _, cols, _, _, moving = JOBS[b // KB]
                src = proj[:, t, 0:moving]
                act.wait_ge(tile_done, nth(tile_done, l, done(b, t)))
                func, scale = ACT.Copy, 1.0
                if name == "va":
                    dst = va[:, t]
                elif name == "qa":
                    dst, scale = qaT[:, t], HD ** -0.5
                elif name == "ka":
                    dst = kaT[:, t]
                elif name == "uv":
                    nc.scalar.activation(ys[:, t, AW:AW + BW], proj[:, t, 0:BW], func)
                    src, dst = proj[:, t, BW:2 * BW], vs[:, t]
                elif name in ("qc", "kc"):
                    lo = CW * (name == "kc")
                    dst = qkc[:, t, lo:lo + CW]
                elif name == "vc":
                    dst = vc[:, t]
                elif name == "gc":
                    dst, func = ys[:, t, AW + BW:D], ACT.Silu
                elif name in ("out0", "out1", "wo0", "wo1"):
                    lo = 512 * int(name[-1])
                    dst = ys[:, t, lo:lo + 512]
                elif name in ("km0", "km1"):
                    dst = kmT[:, 4 * int(name[-1]) + t]
                elif name in ("vm0", "vm1"):
                    lo = 512 * int(name[-1])
                    dst = vm[:, t, lo:lo + 512]
                else:
                    dst, scale = qxT[:, 4 * int(name[-1]) + t], XD ** -0.5
                nc.scalar.activation(dst, src, func, scale=scale).then_inc(emptied, 1)

            def a_step(l, j):
                if j < UNITS:
                    n = (j // NH + 1) * P
                    act.wait_ge(masked, nth(masked, l, j + 1))
                    nc.scalar.activation(probs[:, j % 2, 0:n], probs[:, j % 2, 0:n], ACT.Exp, scale=-1.0,
                                         bias=neg_max[:, j % 2, 0:1], accum_out=den[:, j:j + 1]).then_inc(exped, 1)
                if 1 <= j <= UNITS:
                    u = j - 1
                    n = (u // NH + 1) * P
                    act.wait_ge(p_turned, nth(p_turned, l, u + 1))
                    act.wait_ge(weighed, nth(weighed, l, u - 1))
                    nc.scalar.copy(probsT[:, u % 2, 0:n], work[:, 2, 0:n]).then_inc(p_copied, 1)

            def c_copy(l, c):
                act.wait_ge(c_turned, nth(c_turned, l, c + 1))
                nc.scalar.copy(qkT[:], work[:, 0:2, 0:CW]).then_inc(c_copied, 1)

            def x_step(l, j):
                if j < XUNITS:
                    act.wait_ge(x_max, nth(x_max, l, j + 1))
                    act.wait_ge(x_turned, nth(x_turned, l, j - 1))
                    for i in range(2):
                        last = nc.scalar.activation(x_probs[:, j % 2, i * MEM:(i + 1) * MEM], work[:, j % 2, i * MEM:(i + 1) * MEM],
                                                    ACT.Exp, bias=x_neg[:, j % 2, i:i + 1], accum_out=x_den[:, j, i:i + 1])
                    last.then_inc(x_exped, 1)
                if j >= 2:
                    pair, t = divmod(j - 2, T)
                    act.wait_ge(x_weighed, nth(x_weighed, l, j - 1))
                    nc.scalar.activation(hT_hi[:, pair * BK:(pair + 1) * BK, t * P:(t + 1) * P],
                                         work[:, 3].rearrange("p (k c) -> p k c", k=BK), ACT.Copy).then_inc(x_hi, 1)
                if 1 <= j <= XUNITS:
                    u = j - 1
                    act.wait_ge(x_turned, nth(x_turned, l, u + 1))
                    act.wait_ge(x_weighed, nth(x_weighed, l, u - 1))
                    nc.scalar.copy(x_probsT[:, u % 2], work[:, 2]).then_inc(x_copied, 1)

            def after_tile(l, b, t):
                if b == FIRST_BLOCK["out0"] - 1 and t >= T - 2:
                    turn_hi(l, ("mix", t - T + 2), hT_hi, t - T + 2)
                if b == FIRST_BLOCK["out0"] and t < T - 2:
                    turn_hi(l, ("mix", t + 2), hT_hi, t + 2)
                if b == FIRST_BLOCK["out0"] + 1 and t < MT:
                    turn_hi(l, ("mem", t), memT_hi, t)
                if b == FIRST_BLOCK["out1"] + 1:
                    act.wait_ge(emptied, nth(emptied, l, TILES_BEFORE["out1"] + t + 1))
                    sum_squares(l, ("e1", t), ys[:, t])
                j = (b - STEP_BLOCK) * T + t
                if 0 <= j < UNITS + 2:
                    a_step(l, j)
                k = (b - FIRST_BLOCK["gc"]) * T + t + 2
                if 0 <= k < 2 * T and k % 2 == 0:
                    c_copy(l, k // 2)
                if b == FIRST_BLOCK["qx1"] + 1 and t % 2:
                    x_step(l, t // 2)
                if b == FIRST_BLOCK["wo0"]:
                    x_step(l, XUNITS - 2 + t)

            def before_block(l, b):
                if b == FIRST_BLOCK["qc"]:
                    act.wait_ge(emptied, nth(emptied, l, TILES_BEFORE["qc"]))
                    nc.scalar.activation(ys[:, :, AW:AW + BW], ys[:, :, AW:AW + BW], ACT.Gelu_apprx_tanh)
                    nc.scalar.activation(vs[:], vs[:], ACT.Gelu_apprx_tanh).then_inc(gelu_done, 1)
                if b == FIRST_BLOCK["km0"]:
                    for t in (0, 1):
                        act.wait_ge(x_ready, nth(x_ready, l, BRANCHED["e1", t] + 1))
                        sum_squares(l, ("n2", t), xs[:, t])
                if b == FIRST_BLOCK["km0"] + 1:
                    for t in (2, 3):
                        act.wait_ge(x_ready, nth(x_ready, l, BRANCHED["e1", t] + 1))
                        sum_squares(l, ("n2", t), xs[:, t])
                t = b - (FIRST_BLOCK["km0"] + 2)
                if 0 <= t < T:
                    turn_hi(l, ("n2", t), hT_hi, t)

            def mlp_group(l, g, last):
                for i in range(GROUP_BLOCKS):
                    b = HEAD_BLOCKS + i
                    if i < GROUP_BLOCKS - 1 or not last:
                        split_hi(l, b + 1, g=g)
                    if i in (1, 3):
                        for t in range(5):
                            m = 2 * (i - 1) + t
                            if t < 4:
                                act.wait_ge(tile_done, nth(tile_done, l, g * GROUP_TILES + done(b, t)))
                                act.wait_ge(hidden_lo, nth(hidden_lo, l, g * UP_TILES + (m - 1)))
                                nc.scalar.activation(relu[:, m % 2], proj[:, t], ACT.Relu).then_inc(emptied, 1)
                            if t >= 1:
                                act.wait_ge(hidden_sq, nth(hidden_sq, l, g * UP_TILES + m))
                                nc.scalar.activation(uT_hi[:, m - 1], relu[:, (m - 1) % 2], ACT.Copy).then_inc(hidden_hi, 1)

            with act.Fori(0, DEPTH) as l:
                head_split(l, 0)
                for s in range(T + 1):
                    if s < T:
                        act.wait_ge(x_ready, nth(x_ready, l, s + 1 - T))
                        sum_squares(l, ("n1", s), xs[:, s])
                    if s >= 1:
                        turn_hi(l, ("n1", s - 1), hT_hi, s - 1)
                for b in range(HEAD_BLOCKS):
                    head_split(l, b + 1)
                    before_block(l, b)
                    tiles = JOBS[b // KB][5]
                    if b < HEAD_BLOCKS - 1:
                        for t in range(tiles):
                            if b % KB == KB - 1:
                                empty(l, b, t)
                            after_tile(l, b, t)
                    if b == FIRST_BLOCK["out0"]:
                        for t in range(MT):
                            act.wait_ge(mem_loaded, nth(mem_loaded, l, 16))
                            sum_squares(l, ("mem", t), mem_in[:, t])
                    if b == FIRST_BLOCK["qx1"] + 1:
                        for j in range(2, XUNITS - 2):
                            x_step(l, j)
                for s in range(T + 2):
                    if s < T:
                        empty(l, HEAD_BLOCKS - 1, s)
                        act.wait_ge(emptied, nth(emptied, l, TILES_BEFORE["wo1"] + s + 1))
                        sum_squares(l, ("e2", s), ys[:, s])
                    if 1 <= s <= T:
                        act.wait_ge(x_ready, nth(x_ready, l, BRANCHED["e2", s - 1] + 1))
                        sum_squares(l, ("n3", s - 1), xs[:, s - 1])
                    if s >= 2:
                        turn_hi(l, ("n3", s - 2), hT_hi, s - 2)
                with act.Fori(0, GROUPS - 1) as g:
                    mlp_group(l, g, False)
                mlp_group(l, GROUPS - 1, True)
                for t in range(T):
                    act.wait_ge(added, nth(added, l, GROUPS * UP_TILES - T + t + 1))
                    sum_squares(l, ("e3", t), ys[:, t])

        @block.vector
        def _(dve):
            start_counts(dve, w_lo_done, added, normed, branched, turned_lo, hidden_sq, hidden_lo, sgu_ready,
                         masked, a_out, c_masked, c_state, c_centred, x_max, x_lo)
            steps = [0]

            def setup(ins):
                steps[0] += 1
                ins.then_inc(dve_setup, 1)
                dve.wait_ge(dve_setup, steps[0])

            dve.wait_ge(const_loaded, 16 * 6)
            setup(nc.vector.tensor_copy(pos_f[:], pos_i[:]))
            setup(nc.vector.memset(state[:], 0.0))
            for t in range(T):
                setup(nc.vector.tensor_scalar(angle[:, t], inv[:], pos_f[:, t:t + 1], None, ALU.mult))
            round_up = 1.5 * 2.0 ** 23
            setup(nc.vector.tensor_scalar(turns[:], angle[:], 1.0 / TURN, round_up, ALU.mult, ALU.add))
            setup(nc.vector.tensor_scalar(turns[:], turns[:], -round_up, None, ALU.add))
            for piece in TURN_PIECES:
                setup(nc.vector.scalar_tensor_tensor(out=angle[:], in0=turns[:], scalar=-piece, in1=angle[:],
                                                     op0=ALU.mult, op1=ALU.add))
            pi = float(np.nextafter(np.float32(np.pi), np.float32(0)))
            setup(nc.vector.tensor_scalar(angle[:], angle[:], pi, -pi, ALU.min, ALU.max))
            setup(nc.vector.scalar_tensor_tensor(out=turns[:], in0=angle[:], scalar=-1.0, in1=angle[:],
                                                 op0=ALU.mult, op1=ALU.max))
            setup(nc.vector.tensor_scalar(turns[:], turns[:], -1.0, float(np.float32(np.pi / 2)), ALU.mult, ALU.add))
            dve.sem_inc(trig_done, 1)

            def split_lo(l, b, cols=512, g=0):
                slot = b % WSLOTS
                dve.wait_ge(w_hi_done, nth(w_hi_done, l, g * GROUP_BLOCKS + (b + 1)))
                nc.vector.tensor_tensor(w_lo[:, slot, :, 0:cols], w_raw[:, slot, :, 0:cols],
                                        w_hi[:, slot, :, 0:cols].bitcast(F32), ALU.subtract).then_inc(w_lo_done, 1)

            def head_split(l, b):
                split_lo(l, b, JOBS[b // KB][3] if b < HEAD_BLOCKS else 512)

            def norm(l, key, src):
                n, t = NORMED[key], key[1]
                r = STATS[key]
                before = [k for k in NORMED if NORMED[k] < n and k[1] % 2 == t % 2]
                free = 2 * TURNED[before[-1]] + 2 if before else 0
                at0, at1, at2 = values(dve, nth(rooted, l, r + 1), nth(gain_loaded[key[0]], l, 16), nth(turned, l, free))
                dve.wait_ge(rooted, at0)
                dve.wait_ge(gain_loaded[key[0]], at1)
                dve.wait_ge(turned, at2)
                nc.vector.scalar_tensor_tensor(out=hs[:, t % 2], in0=src, scalar=rstd[:, r % 4],
                                               in1=gains[:, GAIN_SLOT[key[0]]], op0=ALU.mult,
                                               op1=ALU.mult).then_inc(normed, 1)

            def branch(l, key):
                t, r = key[1], STATS[key]
                at0, at1 = values(dve, nth(rooted, l, r + 1), nth(gain_loaded[key[0]], l, 16))
                dve.wait_ge(rooted, at0)
                dve.wait_ge(gain_loaded[key[0]], at1)
                nc.vector.scalar_tensor_tensor(out=ys[:, t], in0=ys[:, t], scalar=rstd[:, r % 4],
                                               in1=gains[:, GAIN_SLOT[key[0]]], op0=ALU.mult,
                                               op1=ALU.mult).then_inc(branched, 1)

            def turn_lo(l, key, hi, lo, t):
                n = TURNED[key]
                for half in range(2):
                    dve.wait_ge(turned_hi, nth(turned_hi, l, 2 * n + half + 1))
                    at = (slice(None), slice(half * BK, (half + 1) * BK), slice(t * P, (t + 1) * P))
                    nc.vector.tensor_tensor(lo[at], work[:, 2 * (n % 2) + half].rearrange("p (k c) -> p k c", k=BK),
                                            hi[at].bitcast(F32), ALU.subtract).then_inc(turned_lo, 1)

            def a_step(l, links, j):
                if j < UNITS:
                    t = j // NH
                    n = (t + 1) * P
                    at0, at1 = values(dve, nth(scored, l, j + 1), nth(p_turned, l, j - 1))
                    dve.wait_ge(scored, at0)
                    dve.wait_ge(p_turned, at1)
                    dve.sem_inc(waits_passed, 1)
                    nc.vector.tensor_tensor_reduce(out=probs[:, j % 2, 0:n], in0=work[:, j % 2, 0:n],
                                                   in1=log_count[:, mask_offset(t):mask_offset(t) + n],
                                                   scale=-1.0, scalar=3e38, op0=ALU.add, op1=ALU.min,
                                                   accum_out=neg_max[:, j % 2, 0:1]).then_inc(masked, 1)
                if j >= 2 and (j - 2) % NH == NH - 1:
                    t = (j - 2) // NH
                    heads = slice(t * NH, (t + 1) * NH)
                    dve.wait_ge(exped, nth(exped, l, (t + 1) * NH))
                    nc.vector.reciprocal(rden[:, heads], den[:, heads]).then_inc(dve_link, 1)
                    dve.wait_ge(dve_link, nth(dve_link, l, next(links)))
                    dve.sem_inc(waits_passed, 1)
                    dve.wait_ge(weighed, nth(weighed, l, (t + 1) * NH))
                    nc.vector.tensor_tensor(ys[:, t, 0:AW].rearrange("p (h e) -> p h e", h=NH),
                                            work[:, 3, 0:AW].rearrange("p (h e) -> p h e", h=NH),
                                            spread(rden[:, heads], HD), ALU.mult).then_inc(a_out, 1)

            def layer_norm(l, links):
                dve.wait_ge(gelu_done, nth(gelu_done, l, 1))
                for t in range(T):
                    last = nc.vector.bn_stats(ln_stats[:, t], vs[:, t])
                last.then_inc(dve_link, 1)
                dve.wait_ge(dve_link, nth(dve_link, l, next(links)))
                dve.sem_inc(waits_passed, 1)
                for t in range(T):
                    last = nc.vector.bn_aggr(ln_mv[:, t], ln_stats[:, t])
                last.then_inc(ln_var, 1)

            def layer_norm_scale(l):
                dve.wait_ge(ln_root, nth(ln_root, l, 1))
                for t in range(T):
                    last = nc.vector.tensor_scalar(vs[:, t], vs[:, t], ln_mv[:, t, 0:1], ln_rstd[:, t:t + 1],
                                                   ALU.subtract, ALU.mult)
                last.then_inc(ln_scaled, 1)

            def gate(l):
                for g in range(G):
                    dve.wait_ge(gated, nth(gated, l, g // 2 + 1))
                    dst = ys[:, :, AW + g * HD:AW + (g + 1) * HD]
                    last = nc.vector.scalar_tensor_tensor(
                        out=dst, in0=work[:, g // 2, (g % 2) * 256:(g % 2 + 1) * 256].rearrange("p (t c) -> p t c", t=T),
                        scalar=sgu_bias[:, g:g + 1], in1=dst, op0=ALU.add, op1=ALU.mult)
                last.then_inc(gate_out, 1)

            def c_mask(l, c):
                dve.wait_ge(c_inner, nth(c_inner, l, c + 1))
                for i in range(2):
                    last = nc.vector.tensor_tensor(innerT[:, i:NH:2],
                                                   work[:, 2 + i, 0:CW].rearrange("p (h c) -> p h c", h=3),
                                                   again(upper[:], 3), ALU.mult)
                last.then_inc(c_masked, 1)
                if c == T - 1:
                    return
                at0, at1 = values(dve, nth(c_kv, l, c + 1), nth(c_state, l, c))
                dve.wait_ge(c_kv, at0)
                dve.wait_ge(c_state, at1)
                if c:
                    dve.wait_ge(c_y, nth(c_y, l, c))
                for lo in (0, HD):
                    at = (slice(lo, lo + HD), slice(None), slice(lo, lo + HD))
                    kv = work[:, 0, 0:CW].rearrange("p (h c) -> p h c", h=PAIRS)[at]
                    new, old = state[:, (c + 1) % 2][at], state[:, c % 2][at]
                    if c == 0:
                        last = nc.vector.tensor_copy(new, kv)
                    else:
                        last = nc.vector.tensor_tensor(new, kv, old, ALU.add)
                last.then_inc(c_state, 1)

            def group_norm(l, links, c):
                dve.wait_ge(c_y, nth(c_y, l, c + 1))
                y = work[:, 2, 0:CW].rearrange("p (h e) -> p h e", h=NH)
                ych = yc[:, c].rearrange("p (h e) -> p h e", h=NH)
                nc.vector.reduce_sum(gn_sum[:], y, AX_X).then_inc(dve_link, 1)
                dve.wait_ge(dve_link, nth(dve_link, l, next(links)))
                dve.sem_inc(waits_passed, 1)
                nc.vector.tensor_scalar(gn_mean[:], gn_sum[:], 1.0 / HD, None, ALU.mult).then_inc(dve_link, 1)
                dve.wait_ge(dve_link, nth(dve_link, l, next(links)))
                dve.sem_inc(waits_passed, 1)
                nc.vector.tensor_tensor(ych, y, spread(gn_mean[:], HD), ALU.subtract).then_inc(c_centred, 1)
                dve.wait_ge(c_centred, nth(c_centred, l, c + 1))
                nc.vector.tensor_tensor(yc2[:], yc[:, c], yc[:, c], ALU.mult).then_inc(dve_link, 1)
                dve.wait_ge(dve_link, nth(dve_link, l, next(links)))
                dve.sem_inc(waits_passed, 1)
                nc.vector.reduce_sum(gn_var[:], yc2[:].rearrange("p (h e) -> p h e", h=NH), AX_X).then_inc(gn_var_done, 1)
                dve.wait_ge(gn_root, nth(gn_root, l, c + 1))
                nc.vector.tensor_tensor(ych, ych, spread(gn_rstd[:], HD), ALU.mult).then_inc(dve_link, 1)
                dve.wait_ge(dve_link, nth(dve_link, l, next(links)))
                dve.sem_inc(waits_passed, 1)

            def c_gate(l, c):
                dve.wait_ge(emptied, nth(emptied, l, TILES_BEFORE["gc"] + c + 1))
                nc.vector.tensor_tensor(ys[:, c, AW + BW:D], ys[:, c, AW + BW:D], yc[:, c], ALU.mult).then_inc(c_out, 1)

            def x_step(l, links, j):
                if 1 <= j <= XUNITS:
                    u = j - 1
                    dve.wait_ge(x_exped, nth(x_exped, l, u + 1))
                    nc.vector.reciprocal(x_rden[:, u], x_den[:, u]).then_inc(dve_link, 1)
                    dve.wait_ge(dve_link, nth(dve_link, l, next(links)))
                    dve.sem_inc(waits_passed, 1)
                    two = x_probs[:, u % 2].rearrange("p (h m) -> p h m", h=2)
                    nc.vector.tensor_tensor(two, two, spread(x_rden[:, u], MEM), ALU.mult).then_inc(x_normed, 1)
                if j < XUNITS:
                    dve.wait_ge(x_scored, nth(x_scored, l, j + 1))
                    nc.vector.reduce_max(x_top[:, j % 2], work[:, j % 2].rearrange("p (h m) -> p h m", h=2), AX_X).then_inc(dve_link, 1)
                    dve.wait_ge(dve_link, nth(dve_link, l, next(links)))
                    dve.sem_inc(waits_passed, 1)
                    dve.wait_ge(x_exped, nth(x_exped, l, j - 1))
                    nc.vector.tensor_scalar(x_neg[:, j % 2], x_top[:, j % 2], -1.0, None, ALU.mult).then_inc(x_max, 1)
                if j >= 2:
                    pair, t = divmod(j - 2, T)
                    at = (slice(None), slice(pair * BK, (pair + 1) * BK), slice(t * P, (t + 1) * P))
                    dve.wait_ge(x_hi, nth(x_hi, l, j - 1))
                    nc.vector.tensor_tensor(hT_lo[at], work[:, 3].rearrange("p (k c) -> p k c", k=BK),
                                            hT_hi[at].bitcast(F32), ALU.subtract).then_inc(x_lo, 1)

            def after_tile(l, links, b, t):
                if b == FIRST_BLOCK["out0"] and t < T - 2:
                    turn_lo(l, ("mix", t + 2), hT_hi, hT_lo, t + 2)
                if b == FIRST_BLOCK["out0"] + 1 and t < MT:
                    turn_lo(l, ("mem", t), memT_hi, memT_lo, t)
                if b == FIRST_BLOCK["out1"] + 1:
                    branch(l, ("e1", t))
                if b == FIRST_BLOCK["ka"] + 1 and t == 0:
                    dve.wait_ge(sgu_turned, nth(sgu_turned, l, 1))
                    nc.vector.tensor_tensor(sgu_T[:], work[:, 0].rearrange("p (g i) -> p g i", g=G),
                                            again(upper[:], G),
                                            ALU.mult).then_inc(sgu_ready, 1)
                j = (b - STEP_BLOCK) * T + t
                if 0 <= j < UNITS + 2:
                    a_step(l, links, j)
                if j == UNITS + 3:
                    gate(l)
                k = (b - FIRST_BLOCK["gc"]) * T + t + 2
                if 0 <= k < 2 * T:
                    if k % 2:
                        c_mask(l, k // 2)
                    elif k >= 2:
                        group_norm(l, links, k // 2 - 1)
                if k == 2 * T - 1:
                    c_gate(l, 0)
                if k == 2 * T:
                    c_gate(l, 1)
                    turn_lo(l, ("mix", 0), hT_hi, hT_lo, 0)
                    group_norm(l, links, T - 1)
                if k == 2 * T + 1:
                    c_gate(l, 2)
                    turn_lo(l, ("mix", 1), hT_hi, hT_lo, 1)
                    c_gate(l, 3)
                if b == FIRST_BLOCK["qx1"] + 1 and t % 2:
                    x_step(l, links, t // 2)
                if b == FIRST_BLOCK["wo0"]:
                    x_step(l, links, XUNITS - 2 + t)

            def before_block(l, links, b):
                first = FIRST_BLOCK["km0"]
                if b == FIRST_BLOCK["qc"]:
                    layer_norm(l, links)
                if b == FIRST_BLOCK["qc"] + 1:
                    layer_norm_scale(l)
                if b == first:
                    norm(l, ("n2", 0), xs[:, 0])
                    norm(l, ("n2", 1), xs[:, 1])
                if b == first + 1:
                    norm(l, ("n2", 2), xs[:, 2])
                if first + 2 <= b < first + 2 + T:
                    turn_lo(l, ("n2", b - first - 2), hT_hi, hT_lo, b - first - 2)
                if b == first + 2:
                    norm(l, ("n2", 3), xs[:, 3])

            def mlp_group(l, g, last):
                for i in range(GROUP_BLOCKS):
                    b = HEAD_BLOCKS + i
                    if i < GROUP_BLOCKS - 1 or not last:
                        split_lo(l, b + 1, g=g)
                    if i in (1, 3):
                        for t in range(5):
                            m = 2 * (i - 1) + t
                            if t < 4:
                                dve.wait_ge(emptied, nth(emptied, l, g * UP_TILES + (HEAD_TILES + m + 1)))
                                nc.vector.tensor_tensor(relu[:, m % 2], relu[:, m % 2], relu[:, m % 2],
                                                        ALU.mult).then_inc(hidden_sq, 1)
                            if t >= 1:
                                dve.wait_ge(hidden_hi, nth(hidden_hi, l, g * UP_TILES + m))
                                nc.vector.tensor_tensor(uT_lo[:, m - 1], relu[:, (m - 1) % 2], uT_hi[:, m - 1].bitcast(F32),
                                                        ALU.subtract).then_inc(hidden_lo, 1)
                    if i in (5, 7):
                        for t in range(T):
                            j = (i - 5) // 2
                            at0, at1 = values(dve, nth(tile_done, l, g * GROUP_TILES + done(b, t)), nth(y_zeroed, l, 1))
                            dve.wait_ge(tile_done, at0)
                            dve.wait_ge(y_zeroed, at1)
                            part_y = ys[:, t, j * 512:(j + 1) * 512]
                            nc.vector.tensor_tensor(part_y, proj[:, t], part_y, ALU.add).then_inc(added, 1)

            with dve.Fori(0, DEPTH) as l:
                links = itertools.count(1)
                head_split(l, 0)
                for s in range(T + 1):
                    if s < T:
                        norm(l, ("n1", s), xs[:, s])
                    if s >= 1:
                        turn_lo(l, ("n1", s - 1), hT_hi, hT_lo, s - 1)
                for b in range(HEAD_BLOCKS):
                    head_split(l, b + 1)
                    before_block(l, links, b)
                    if b == HEAD_BLOCKS - 1:
                        continue
                    for t in range(JOBS[b // KB][5]):
                        after_tile(l, links, b, t)
                    if b == FIRST_BLOCK["out0"]:
                        for t in range(MT):
                            norm(l, ("mem", t), mem_in[:, t])
                    if b == FIRST_BLOCK["qx1"] + 1:
                        for j in range(2, XUNITS - 2):
                            x_step(l, links, j)
                for s in range(T + 2):
                    if s < T:
                        branch(l, ("e2", s))
                    if 1 <= s <= T:
                        norm(l, ("n3", s - 1), xs[:, s - 1])
                    if s >= 2:
                        turn_lo(l, ("n3", s - 2), hT_hi, hT_lo, s - 2)
                with dve.Fori(0, GROUPS - 1) as g:
                    mlp_group(l, g, False)
                mlp_group(l, GROUPS - 1, True)
                for t in range(T):
                    branch(l, ("e3", t))
                assert next(links) == DVE_LINKS + 1

        @block.gpsimd
        def _(pool):
            nc.gpsimd.memset(minus_half[:], -0.5).then_inc(setup_done, 1)
            pool.wait_ge(setup_done, 1)
            pool.wait_ge(const_loaded, 16 * 6)
            pool.wait_ge(x_loaded, 16 * T)
            start_counts(pool, x_ready, rooted)

            def root(l, links, key):
                r = STATS[key]
                pool.wait_ge(summed, nth(summed, l, r + 1))
                pool.sem_inc(waits_passed, 1)
                nc.gpsimd.tensor_scalar(meansq[:, r % 2], sumsq[:, r % 2], 1.0 / D, EPS, ALU.mult, ALU.add).then_inc(pool_link, 1)
                pool.wait_ge(pool_link, nth(pool_link, l, next(links)))
                pool.sem_inc(waits_passed, 1)
                nc.gpsimd.tensor_tensor(rstd[:, r % 4], meansq[:, r % 2], minus_half[:, 0:1], ALU.pow).then_inc(rooted, 1)

            def add_branch(l, key):
                t = key[1]
                pool.wait_ge(branched, nth(branched, l, BRANCHED[key] + 1))
                nc.gpsimd.tensor_tensor(xs[:, t], xs[:, t], ys[:, t], ALU.add).then_inc(x_ready, 1)

            def rotate(l, links, t):
                pool.wait_ge(emptied, nth(emptied, l, TILES_BEFORE["kc"] + t + 1))
                x12 = qkc[:, t].rearrange("p (h s e) -> p h s e", s=2, e=HALF)
                x1, x2 = x12[:, :, 0], x12[:, :, 1]
                a, b_, c = (rot[:, i].rearrange("p (h e) -> p h e", e=HALF) for i in range(3))
                cs = again(cos[:, t], 2 * NH)
                sn = again(sin[:, t], 2 * NH)
                nc.gpsimd.tensor_tensor(a, x1, cs, ALU.mult)
                nc.gpsimd.tensor_tensor(b_, x2, sn, ALU.mult)
                nc.gpsimd.tensor_tensor(c, x1, sn, ALU.mult)
                nc.gpsimd.tensor_tensor(x2, x2, cs, ALU.mult).then_inc(pool_link, 1)
                pool.wait_ge(pool_link, nth(pool_link, l, next(links)))
                nc.gpsimd.tensor_tensor(x1, a, b_, ALU.subtract)
                nc.gpsimd.tensor_tensor(x2, x2, c, ALU.add).then_inc(pool_link, 1)
                pool.wait_ge(pool_link, nth(pool_link, l, next(links)))
                every = qkc[:, t].rearrange("p (h e) -> p h e", e=HD)
                nc.gpsimd.tensor_tensor(every, every, spread(decay[:, t], HD),
                                        ALU.mult).then_inc(rotated, 1)

            with pool.Fori(0, DEPTH) as l:
                links = itertools.count(1)
                for t in range(T):
                    root(l, links, ("n1", t))
                pool.wait_ge(ln_var, nth(ln_var, l, 1))
                pool.sem_inc(waits_passed, 1)
                nc.gpsimd.tensor_scalar(ln_ve[:], ln_mv[:, :, 1], EPS, None, ALU.add).then_inc(pool_link, 1)
                pool.wait_ge(pool_link, nth(pool_link, l, next(links)))
                pool.sem_inc(waits_passed, 1)
                nc.gpsimd.tensor_tensor(ln_rstd[:], ln_ve[:], minus_half[:, 0:T], ALU.pow).then_inc(ln_root, 1)
                pool.wait_ge(ln_scaled, nth(ln_scaled, l, 1))
                pool.wait_ge(sgu_loaded, nth(sgu_loaded, l, 64))
                g4 = again(ln_gain[:], T)
                s4 = again(ln_shift[:], T)
                nc.gpsimd.tensor_tensor(vs[:], vs[:], g4, ALU.mult).then_inc(pool_link, 1)
                pool.wait_ge(pool_link, nth(pool_link, l, next(links)))
                pool.sem_inc(waits_passed, 1)
                nc.gpsimd.tensor_tensor(vs[:], vs[:], s4, ALU.add).then_inc(ln_done, 1)
                pool.wait_ge(trig_done, 2)
                for t in range(T):
                    rotate(l, links, t)
                for c in range(T):
                    pool.wait_ge(gn_var_done, nth(gn_var_done, l, c + 1))
                    pool.sem_inc(waits_passed, 1)
                    nc.gpsimd.tensor_scalar(gn_ve[:], gn_var[:], 1.0 / HD, EPS, ALU.mult, ALU.add).then_inc(pool_link, 1)
                    pool.wait_ge(pool_link, nth(pool_link, l, next(links)))
                    pool.sem_inc(waits_passed, 1)
                    nc.gpsimd.tensor_tensor(gn_rstd[:], gn_ve[:], minus_half[:, 0:NH], ALU.pow).then_inc(gn_root, 1)
                for t in range(MT):
                    root(l, links, ("mem", t))
                for t in range(T + 1):
                    if t < T:
                        root(l, links, ("e1", t))
                    if t >= 1:
                        add_branch(l, ("e1", t - 1))
                for t in range(T):
                    root(l, links, ("n2", t))
                for s in range(T + 1):
                    if s < T:
                        root(l, links, ("e2", s))
                        add_branch(l, ("e2", s))
                    if s >= 1:
                        root(l, links, ("n3", s - 1))
                pool.wait_ge(x_ready, nth(x_ready, l, BRANCHED["e2", T - 1] + 1))
                pool.sem_inc(waits_passed, 1)
                nc.gpsimd.memset(ys[:], 0.0).then_inc(y_zeroed, 1)
                for t in range(T):
                    root(l, links, ("e3", t))
                    add_branch(l, ("e3", t))
                assert next(links) == POOL_LINKS + 1


NAMES = ["x", "mem", "positions", "norm_g", "w_in", "sgu_w", "sgu_b", "sgu_ln_g", "sgu_ln_b", "w_out",
         "x_wq", "x_wkv", "x_wo", "w_up", "w_down"]


def kernel(**inputs):
    import numpy as _np
    import concourse.bacc as _bacc
    from concourse import mybir as _mybir
    from concourse.bass_utils import run_bass_kernel_spmd as _run

    nc = _bacc.Bacc("TRN2", target_bir_lowering=False, num_devices=1)
    given = {name: _np.ascontiguousarray(inputs[name]) for name in NAMES} | shape_constants()
    given["positions"] = _np.ascontiguousarray(given["positions"].reshape(T, P).T)
    given["sgu_b"] = _np.ascontiguousarray(given["sgu_b"].transpose(0, 2, 1))
    arrays, args = {}, []
    for name, a in given.items():
        arrays[f"in_{name}_dram"] = a
        args.append(nc.dram_tensor(f"in_{name}_dram", a.shape, _mybir.dt.from_np(a.dtype), kind="ExternalInput").ap())
    args.append(nc.dram_tensor("out_dram", (1, S, D), _mybir.dt.float32, kind="ExternalOutput").ap())
    trunk(nc, *args)
    r = _run(nc, [arrays], core_ids=[0])
    return r.results[0]["out_dram"]
```

```python
import itertools
from contextlib import ExitStack

import concourse.bass as bass
import concourse.mybir as mybir
import numpy as np

F32 = mybir.dt.float32
F32R = mybir.dt.float32r
BF16 = mybir.dt.bfloat16
I32 = mybir.dt.int32
ALU = mybir.AluOpType
ACT = mybir.ActivationFunctionType
AX_X = mybir.AxisListType.X

P = 128
DEPTH, S, D, MEM = 2, 512, 1024, 256
HD = 64
NH = 6
PAIRS = NH // 2
G = 4
XH, XD = 4, 256
FF = 4 * D
AW, BW, CW = NH * HD, G * HD, NH * HD
PATTERNS = ((128, 1), (512, 4), (2048, 16))
EPS = 1e-6
ROPE_BASE = 10000.0
HALF = HD // 2
T = S // P
MT = MEM // P
KC = D // P
BK = 4
MASKED = -1e30

A0, U0, C0 = 0, 3 * AW, 3 * AW + 2 * BW
JOBS = [
    ("va", "w_in", A0 + 2 * AW, AW, "tok", T, AW),
    ("qa", "w_in", A0, AW, "feat", PAIRS, S),
    ("ka", "w_in", A0 + AW, AW, "feat", PAIRS, S),
    ("uv", "w_in", U0, 2 * BW, "tok", T, 2 * BW),
    ("qc", "w_in", C0, CW, "tok", T, CW),
    ("kc", "w_in", C0 + CW, CW, "tok", T, CW),
    ("vc", "w_in", C0 + 2 * CW, CW, "tok", T, CW),
    ("gc", "w_in", C0 + 3 * CW, CW, "tok", T, CW),
    ("out0", "w_out", 0, 512, "tok", T, 512),
    ("out1", "w_out", 512, 512, "tok", T, 512),
    ("km0", "x_wkv", 0, 512, "feat", 4, MEM),
    ("km1", "x_wkv", 512, 512, "feat", 4, MEM),
    ("vm0", "x_wkv", D, 512, "tok", MT, 512),
    ("vm1", "x_wkv", D + 512, 512, "tok", MT, 512),
    ("qx0", "x_wq", 0, 512, "feat", 4, S),
    ("qx1", "x_wq", 512, 512, "feat", 4, S),
    ("wo0", "x_wo", 0, 512, "tok", T, 512),
    ("wo1", "x_wo", 512, 512, "tok", T, 512),
]
KB = D // (BK * P)
JOB = {j[0]: i for i, j in enumerate(JOBS)}
FIRST_BLOCK = {j[0]: KB * i for i, j in enumerate(JOBS)}
HEAD_BLOCKS = KB * len(JOBS)
GROUPS = 4
GROUP_JOBS = ("up0", "up1", "dn0", "dn1")
GROUP_BLOCKS = KB * len(GROUP_JOBS)
BLOCKS = HEAD_BLOCKS + GROUPS * GROUP_BLOCKS
WSLOTS = 2
assert BLOCKS % WSLOTS == 0 and GROUP_BLOCKS % WSLOTS == 0 and FF == GROUPS * KB * BK * P

BRANCH_JOBS = ("out0", "out1", "wo0", "wo1")
TILES_BEFORE = {}
_n = 0
for _j in JOBS:
    TILES_BEFORE[_j[0]] = _n
    _n += 0 if _j[0] in BRANCH_JOBS else _j[5]
HEAD_TILES = _n
GROUP_TILES = 4 * KB * len(GROUP_JOBS)
UP_TILES = 8


def bank_users():
    last = [None] * 4
    users = {}
    for name, _, _, _, _, tiles, _ in JOBS:
        for t in range(tiles):
            users[name, t] = last[t]
            if name in BRANCH_JOBS:
                last[t] = (True, T * BRANCH_JOBS.index(name) + t)
            else:
                last[t] = (False, TILES_BEFORE[name] + t)
    return users
BANK_USER = bank_users()

def steps(text):
    return [(step[0], int(step[1])) for step in text.split()]


N1_ACT = steps("x0 x1 w0 h0 x2 h1 x3 h2 h3")
N1_DVE = steps("n0 n1 w0 h0 n2 h1 n3 h2 h3")
N3_ACT = steps("e0 e1 x0 x1 w0 h0 e2 h1 x2 e3 w1 x3 h2 h3")
N3_DVE = steps("e0 x0 e1 x1 n0 n1 w0 h0 h1 e2 x2 e3 x3 w1 n2 n3 h2 h3")


def stats_order():
    order = [("n1", t) for t in range(T)] + [("mem", t) for t in range(MT)]
    order += [("e1", t) for t in range(T)] + [("n2", t) for t in range(T)]
    order += [("e2" if what == "e" else "n3", t) for what, t in N3_ACT if what in "ex"]
    return order + [("e3", t) for t in range(T)]
STATS = {k: i for i, k in enumerate(stats_order())}
NORMED = {k: i for i, k in enumerate([("n1", t) for t in range(T)] + [("mem", t) for t in range(MT)]
                                     + [("n2", t) for t in range(T)] + [("n3", t) for t in range(T)])}
BRANCHED = {(e, t): T * i + t for i, e in enumerate(("e1", "e2", "e3")) for t in range(T)}
GAINED = {(e, half, t): 2 * T * i + T * half + t for i, e in enumerate(("e1", "e2", "e3"))
          for half in range(2) for t in range(T)}
TURNED = {k: i for i, k in enumerate(
    [("n1", t) for t in range(T)] + [("mix", t) for t in range(T)] + [("mem", t) for t in range(MT)]
    + [("n2", t) for t in range(T)] + [("n3", t) for t in range(T)])}

BLOCK_TILES = [j[5] for j in JOBS for _ in range(KB)] + [4] * (GROUPS * GROUP_BLOCKS)
LAYER_TILES = sum(BLOCK_TILES)


BY_BLOCK = [(kb, t) for kb in range(KB) for t in range(4)]
EARLY_PAIR = [(0, 0), (0, 1), (1, 0), (1, 1), (0, 2), (0, 3), (1, 2), (1, 3)]


def done(b, t=None):
    if b < 0:
        return -sum(BLOCK_TILES[b + 1:]) if b < -1 else 0
    first = FIRST_BLOCK["wo1"]
    if first <= b < first + KB:
        return sum(BLOCK_TILES[:first]) + EARLY_PAIR.index((b - first, T - 1 if t is None else t)) + 1
    return sum(BLOCK_TILES[:b]) + (BLOCK_TILES[b] if t is None else t + 1)


UNITS = T * NH
STEP_BLOCK = FIRST_BLOCK["uv"]
XUNITS = XH // 2 * T


def unit_step(b, t):
    j = (b - STEP_BLOCK) * T + t
    pause = (FIRST_BLOCK["qc"] - STEP_BLOCK) * T
    if j < 0 or pause <= j < pause + 2:
        return -1
    return j if j < pause else j - 2


DVE_LINKS = 37
POOL_LINKS = 43

GAIN = {"n1": 0, "e1": 1, "n2": 2, "e2": 3, "n3": 4, "e3": 5, "mem": 6}
GAIN_SLOT = {"n1": 0, "mem": 1, "n2": 0, "n3": 1, "e1": 2, "e2": 2, "e3": 2}


def shape_constants():
    i = np.arange(S)[:, None]
    j = np.arange(S)[None, :]
    count = np.zeros((S, S))
    for window, dilation in PATTERNS:
        count += (i >= j) & ((i - j) % dilation == 0) & (i - j <= window)
    logs = np.where(count > 0, np.log(np.maximum(count, 1)), MASKED).astype(np.float32)
    log_count = np.concatenate([logs[t * P:(t + 1) * P, :(t + 1) * P] for t in range(T)], axis=1)
    a = np.arange(P)
    upper = (a[:, None] <= a[None, :]).astype(np.float32)
    gamma = 1.0 - 2.0 ** (-5.0 - np.arange(NH))
    pos = np.arange(S, dtype=np.float64).reshape(T, P).T[:, :, None]
    decay = np.concatenate([gamma ** (pos + 1.0), gamma ** -(pos + 1.0) * HD ** -0.5], axis=2)
    inv = 1.0 / (np.float32(ROPE_BASE) ** np.linspace(0.0, 1.0, HALF, dtype=np.float32))
    return {
        "c_ident": np.eye(P, dtype=np.float32),
        "c_logcount": log_count,
        "c_upper": upper,
        "c_decay": decay.astype(np.float32),
        "c_inv": np.tile(inv.astype(np.float32)[None, :], (P, 1)),
    }


TURN = 2.0 * np.pi


def turn_pieces():
    pieces, left = [], TURN
    for _ in range(4):
        unit = 2.0 ** (np.floor(np.log2(left)) - 7)
        pieces.append(float(np.floor(left / unit) * unit))
        left -= pieces[-1]
    return pieces


TURN_PIECES = turn_pieces()
ARENA_KIB = 53


def spread(ap, n):
    return ap.rearrange("p (a b) -> p a b", b=1).broadcast_to([ap.shape[0], ap.shape[1], n])


def again(ap, n):
    return ap.rearrange("p (b a) -> p b a", b=1).broadcast_to([ap.shape[0], n, ap.shape[1]])


def mask_offset(t):
    return P * (t * (t + 1) // 2)


def trunk(nc, x, mem, positions, norm_g, w_in, sgu_w, sgu_b, sgu_ln_g, sgu_ln_b, w_out,
          x_wq, x_wkv, x_wo, w_up, w_down, c_ident, c_logcount, c_upper, c_decay, c_inv, out):
    weights = {"w_in": w_in, "w_out": w_out, "x_wq": x_wq, "x_wkv": x_wkv, "x_wo": x_wo}
    with ExitStack() as ctx:
        def sb(name, shape, dt=F32):
            return ctx.enter_context(nc.sbuf_tensor(name, shape, dt))

        xs = sb("xs", [P, T, D])
        hT_hi = sb("hT_hi", [P, KC, S], F32R)
        hT_lo = sb("hT_lo", [P, KC, S], F32R)
        w_raw = sb("w_raw", [P, WSLOTS, BK, 512])
        w_hi = sb("w_hi", [P, WSLOTS, BK, 512], F32R)
        w_lo = sb("w_lo", [P, WSLOTS, BK, 512], F32R)
        ys = sb("ys", [P, T, D])
        gains = sb("gains", [P, 3, D])
        hs = sb("hs", [P, 2, D])
        squares = sb("squares", [P, 2, D], BF16)
        ident = sb("ident", [P, P])
        log_count = sb("log_count", [P, mask_offset(T)])
        upper = sb("upper", [P, P])
        decay = sb("decay", [P, T, 2 * NH])
        inv = sb("inv", [P, HALF])
        cos = sb("cos", [P, T, HALF])
        sin = sb("sin", [P, T, HALF])
        angle = sb("angle", [P, T, HALF])
        turns = sb("turns", [P, T, HALF])
        pos_i = sb("pos_i", [P, T], I32)
        pos_f = sb("pos_f", [P, T])
        minus_half = sb("minus_half", [P, 8])
        sumsq = sb("sumsq", [P, 2, 1])
        meansq = sb("meansq", [P, 2, 1])
        rstd = sb("rstd", [P, len(STATS), 1])
        half_sum = sb("half_sum", [P, T])
        half_mean = sb("half_mean", [P, T])
        sgu_raw = sb("sgu_raw", [P, G, P])
        sgu_T = sb("sgu_T", [P, G, P])
        sgu_bias = sb("sgu_bias", [P, G])
        ln_gain = sb("ln_gain", [P, BW])
        ln_shift = sb("ln_shift", [P, BW])
        ln_stats = sb("ln_stats", [P, T, 6])
        ln_mv = sb("ln_mv", [P, T, 2])
        ln_ve = sb("ln_ve", [P, T])
        ln_rstd = sb("ln_rstd", [P, T])
        neg_max = sb("neg_max", [P, 2, 2])
        den = sb("den", [P, UNITS])
        rden = sb("rden", [P, UNITS])
        x_den = sb("x_den", [P, XUNITS, 2])
        x_rden = sb("x_rden", [P, XUNITS, 2])
        state = sb("state", [P, 2, PAIRS, P])
        x_neg = sb("x_neg", [P, 2, 2])
        x_top = sb("x_top", [P, 2, 2])
        gn_sum = sb("gn_sum", [P, NH])
        gn_mean = sb("gn_mean", [P, NH])
        gn_var = sb("gn_var", [P, NH])
        gn_ve = sb("gn_ve", [P, NH])
        gn_rstd = sb("gn_rstd", [P, NH])

        KIB = 1024
        arena_start = -(-nc.sbuf_base // 32) * 32
        ctx.enter_context(nc.sbuf_tensor("arena", [P, ARENA_KIB * KIB // 4], F32))

        def part(name, kib, shape, dt=F32):
            return nc.alloc_sbuf_tensor_at(name, shape, dt, offset=arena_start + int(kib * KIB))

        qaT = part("qaT", 0, [P, PAIRS, S])
        kaT = part("kaT", 6, [P, PAIRS, S])
        va = part("va", 12, [P, T, AW])
        vs = part("vs", 18, [P, T, BW])
        qkc = part("qkc", 22, [P, T, 2 * CW])
        vc = part("vc", 34, [P, T, CW])
        probs = part("probs", 40, [P, 2, S])
        probsT = part("probsT", 44, [P, 2, S])
        rot = part("rot", 48, [P, 3, 2 * NH * HALF])
        qkT = part("qkT", 0, [P, 2, CW])
        innerT = part("innerT", 3, [P, NH, P])
        yc = part("yc", 6, [P, T, CW])
        yc2 = part("yc2", 12, [P, CW])
        kmT = part("kmT", 0, [P, KC, MEM])
        vm = part("vm", 8, [P, MT, D])
        x_probs = part("x_probs", 16, [P, 2, 512])
        x_probsT = part("x_probsT", 20, [P, 2, 512])
        mem_in = part("mem_in", 40, [P, MT, D])
        memT_hi = part("memT_hi", 24, [P, KC, MEM], F32R)
        memT_lo = part("memT_lo", 32, [P, KC, MEM], F32R)
        qxT = part("qxT", 24, [P, KC, S])
        half_squares = part("half_squares", 48, [P, T, 512], BF16)
        uT_hi = part("uT_hi", 0, [P, KC, S], F32R)
        uT_lo = part("uT_lo", 16, [P, KC, S], F32R)
        relu = part("relu", 32, [P, 2, S])

        proj = ctx.enter_context(nc.psum_tensor("proj", [P, 4, 512], F32))
        work = ctx.enter_context(nc.psum_tensor("work", [P, 4, 512], F32))

        per_layer, start_of = {}, {}

        def counted(name, per, start=0):
            sem = ctx.enter_context(nc.semaphore(name))
            per_layer[sem.name], start_of[sem.name] = per, start
            return sem

        def nth(sem, l, n):
            return l * per_layer[sem.name] + (n + start_of[sem.name])

        waits_passed = ctx.enter_context(nc.semaphore("waits_passed"))
        first_loaded = ctx.enter_context(nc.semaphore("first_loaded"))
        const_loaded = ctx.enter_context(nc.semaphore("const_loaded"))
        x_loaded = [ctx.enter_context(nc.semaphore(f"x_loaded{t}")) for t in range(T)]
        setup_done = ctx.enter_context(nc.semaphore("setup_done"))
        dve_setup = ctx.enter_context(nc.semaphore("dve_setup"))
        trig_done = ctx.enter_context(nc.semaphore("trig_done"))
        stored = ctx.enter_context(nc.semaphore("stored"))
        w_loaded = [counted(f"w_loaded{i}", 16 * BLOCKS // WSLOTS) for i in range(WSLOTS)]
        w_hi_done = counted("w_hi_done", BLOCKS)
        w_lo_done = counted("w_lo_done", BLOCKS, WSLOTS)
        gain_loaded = {k: counted(f"gain_{k}", 16) for k in GAIN}
        sgu_loaded = counted("sgu_loaded", 64)
        mem_loaded = counted("mem_loaded", 16)
        tile_done = counted("tile_done", LAYER_TILES, 4 * WSLOTS)
        emptied = counted("emptied", HEAD_TILES + GROUPS * UP_TILES, 1)
        added = counted("added", GROUPS * UP_TILES, T)
        summed = counted("summed", len(STATS))
        rooted = counted("rooted", len(STATS), 2)
        normed = counted("normed", len(NORMED), 1)
        half_summed = counted("half_summed", len(BRANCHED))
        gained = counted("gained", len(GAINED), 1)
        x_ready = counted("x_ready", len(BRANCHED), T)
        turned = counted("turned", 2 * len(TURNED), 1)
        turned_hi = counted("turned_hi", 2 * len(TURNED), 1)
        turned_lo = counted("turned_lo", 2 * len(TURNED), 4)
        y_zeroed = counted("y_zeroed", 1)
        hidden_sq = counted("hidden_sq", GROUPS * UP_TILES, 1)
        hidden_hi = counted("hidden_hi", GROUPS * UP_TILES, 1)
        hidden_lo = counted("hidden_lo", GROUPS * UP_TILES, 2)
        sgu_turned = counted("sgu_turned", 1)
        sgu_ready = counted("sgu_ready", 1, 1)
        gelu_done = counted("gelu_done", 1)
        ln_var = counted("ln_var", 1)
        ln_root = counted("ln_root", 1)
        ln_scaled = counted("ln_scaled", 1)
        ln_done = counted("ln_done", 1)
        gated = counted("gated", 2)
        gate_out = counted("gate_out", 1)
        scored = counted("scored", UNITS)
        masked = counted("masked", UNITS, 2)
        exped = counted("exped", UNITS)
        p_turned = counted("p_turned", UNITS, 2)
        p_copied = counted("p_copied", UNITS, 1)
        weighed = counted("weighed", UNITS, 2)
        a_out = counted("a_out", T, 1)
        rotated = counted("rotated", T)
        c_turned = counted("c_turned", T)
        c_copied = counted("c_copied", T, 1)
        c_inner = counted("c_inner", T)
        c_masked = counted("c_masked", T, 1)
        c_kv = counted("c_kv", T - 1)
        c_state = counted("c_state", T - 1, 1)
        c_y = counted("c_y", T)
        c_centred = counted("c_centred", T, 1)
        gn_var_done = counted("gn_var_done", T)
        gn_root = counted("gn_root", T)
        c_out = counted("c_out", T)
        x_scored = counted("x_scored", XUNITS)
        x_max = counted("x_max", XUNITS, 1)
        x_exped = counted("x_exped", XUNITS, 2)
        x_normed = counted("x_normed", XUNITS)
        x_turned = counted("x_turned", XUNITS, 2)
        x_copied = counted("x_copied", XUNITS, 1)
        x_weighed = counted("x_weighed", XUNITS, 2)
        x_hi = counted("x_hi", XUNITS)
        x_lo = counted("x_lo", XUNITS, 1)
        dve_link = counted("dve_link", DVE_LINKS)
        pool_link = counted("pool_link", POOL_LINKS)

        def values(eng, *counts):
            return [eng.snap(count) for count in counts]

        def start_counts(eng, *sems):
            for sem in sems:
                eng.sem_inc(sem, start_of[sem.name])

        block = ctx.enter_context(nc.Block())

        @block.sync
        def _(sp):
            for dst, src in ((pos_i, positions), (inv, c_inv)):
                sp.dma_start(dst[:], src).then_inc(first_loaded, 16)
            sp.dma_start(xs[:, 0], x[0, 0:P]).then_inc(x_loaded[0], 16)

            def load_block(l, b, src):
                cols = src.shape[-1]
                sp.wait_ge(w_lo_done, nth(w_lo_done, l, b - WSLOTS + 1))
                sp.sem_inc(waits_passed, 1)
                sp.dma_start(w_raw[:, b % WSLOTS, :, 0:cols],
                             src.rearrange("a (k p) c -> p (a k) c", p=P)).then_inc(w_loaded[b % WSLOTS], 16)

            def load_gain(l, k):
                sp.dma_start(gains[:, GAIN_SLOT[k]],
                             norm_g[bass.ds(l, 1), GAIN[k]].broadcast_to([P, D])).then_inc(gain_loaded[k], 16)

            with sp.Fori(0, DEPTH) as l:
                sp.wait_ge(normed, nth(normed, l, 0))
                sp.sem_inc(waits_passed, 1)
                load_gain(l, "n1")
                for name, weight, c, cols, _, _, _ in JOBS:
                    for kb in range(KB):
                        b = FIRST_BLOCK[name] + kb
                        load_block(l, b, weights[weight][bass.ds(l, 1), kb * BK * P:(kb + 1) * BK * P, c:c + cols])
                    if name == "va":
                        sp.wait_ge(normed, nth(normed, l, 0))
                        sp.dma_start(sgu_raw[:], sgu_w[bass.ds(l, 1)].rearrange("a g i j -> i (a g) j")).then_inc(sgu_loaded, 16)
                        sp.dma_start(sgu_bias[:], sgu_b[bass.ds(l, 1)].rearrange("a i g -> i (a g)")).then_inc(sgu_loaded, 16)
                        sp.dma_start(ln_gain[:], sgu_ln_g[bass.ds(l, 1)].broadcast_to([P, BW])).then_inc(sgu_loaded, 16)
                        sp.dma_start(ln_shift[:], sgu_ln_b[bass.ds(l, 1)].broadcast_to([P, BW])).then_inc(sgu_loaded, 16)
                    if name == "kc":
                        sp.wait_ge(normed, nth(normed, l, NORMED["n1", T - 1] + 1))
                        sp.sem_inc(waits_passed, 1)
                        load_gain(l, "mem")
                        sp.wait_ge(gained, nth(gained, l, 0))
                        sp.sem_inc(waits_passed, 1)
                        load_gain(l, "e1")
                        sp.wait_ge(normed, nth(normed, l, NORMED["n1", T - 1] + 1))
                        sp.sem_inc(waits_passed, 1)
                        load_gain(l, "n2")
                    if name == "gc":
                        sp.wait_ge(weighed, nth(weighed, l, UNITS))
                        sp.dma_start(mem_in[:], mem[0].rearrange("(t p) d -> p t d", p=P)).then_inc(mem_loaded, 16)
                    if name == "qx0":
                        sp.wait_ge(normed, nth(normed, l, NORMED["mem", MT - 1] + 1))
                        sp.sem_inc(waits_passed, 1)
                        load_gain(l, "n3")
                        sp.wait_ge(gained, nth(gained, l, GAINED["e1", 1, T - 1] + 1))
                        sp.sem_inc(waits_passed, 1)
                        load_gain(l, "e2")
                with sp.Fori(0, GROUPS) as g:
                    for j in range(2):
                        for kb in range(KB):
                            b = HEAD_BLOCKS + KB * j + kb
                            sp.wait_ge(w_lo_done, nth(w_lo_done, l, g * GROUP_BLOCKS + (b - WSLOTS + 1)))
                            sp.sem_inc(waits_passed, 1)
                            sp.dma_start(w_raw[:, b % WSLOTS],
                                         w_up[bass.ds(l, 1), kb * BK * P:(kb + 1) * BK * P,
                                              bass.ds(g * (FF // GROUPS) + j * 512, 512)]
                                         .rearrange("a (k p) c -> p (a k) c", p=P)).then_inc(w_loaded[b % WSLOTS], 16)
                    for j in range(2):
                        for kb in range(KB):
                            b = HEAD_BLOCKS + KB * (2 + j) + kb
                            sp.wait_ge(w_lo_done, nth(w_lo_done, l, g * GROUP_BLOCKS + (b - WSLOTS + 1)))
                            sp.sem_inc(waits_passed, 1)
                            sp.dma_start(w_raw[:, b % WSLOTS],
                                         w_down[bass.ds(l, 1), bass.ds(g * (FF // GROUPS) + kb * BK * P, BK * P),
                                                j * 512:(j + 1) * 512]
                                         .rearrange("a (k p) c -> p (a k) c", p=P)).then_inc(w_loaded[b % WSLOTS], 16)
                sp.wait_ge(gained, nth(gained, l, GAINED["e2", 1, T - 1] + 1))
                sp.sem_inc(waits_passed, 1)
                load_gain(l, "e3")
            for t in range(T):
                sp.wait_ge(x_ready, nth(x_ready, DEPTH - 1, BRANCHED["e3", t] + 1))
                sp.dma_start(out[0, t * P:(t + 1) * P], xs[:, t]).then_inc(stored, 16)
            sp.wait_ge(stored, 16 * T)

        @block.tensor
        def _(pe):
            start_counts(pe, tile_done, turned, p_turned, weighed, x_turned, x_weighed)
            pe.wait_ge(first_loaded, 16 * 3)

            def three_passes(dst, l_hi, l_lo, r_hi, r_lo, first, last):
                nc.tensor.matmul(dst, l_hi, r_hi, start=first, stop=False)
                nc.tensor.matmul(dst, l_hi, r_lo, start=False, stop=False)
                return nc.tensor.matmul(dst, l_lo, r_hi, start=False, stop=last)

            def block_tile(b_slot, kb, mode, t, moving, hi, lo, cols, at=0):
                for k in range(BK):
                    c = kb * BK + k
                    first, last = c == 0, kb == KB - 1 and k == BK - 1
                    if mode == "tok":
                        r = slice(t * P, (t + 1) * P)
                        mm = three_passes(proj[:, t, 0:moving], hi[:, c, r], lo[:, c, r],
                                          w_hi[:, b_slot, k, 0:cols], w_lo[:, b_slot, k, 0:cols], first, last)
                    else:
                        r = slice(t * P, (t + 1) * P)
                        tokens = slice(at, at + moving)
                        mm = three_passes(proj[:, t, tokens], w_hi[:, b_slot, k, r], w_lo[:, b_slot, k, r],
                                          hi[:, c, tokens], lo[:, c, tokens], first, last)
                return mm

            def turn(l, key, src):
                n = TURNED[key]
                pe.wait_ge(turned_lo, nth(turned_lo, l, 2 * n - 2))
                for half in range(2):
                    for k in range(BK):
                        c = half * BK + k
                        mm = nc.tensor.transpose(work[:, 2 * (n % 2) + half, k * P:(k + 1) * P],
                                                 src[:, c * P:(c + 1) * P], ident[:])
                    mm.then_inc(turned, 1)

            def turned_in(l, key):
                pe.wait_ge(turned_lo, nth(turned_lo, l, 2 * TURNED[key] + 2))
                pe.sem_inc(waits_passed, 1)

            def a_scores(l, u):
                t, h = divmod(u, NH)
                lo, n = HD * (h % 2), (t + 1) * P
                if u == 0:
                    pe.wait_ge(emptied, nth(emptied, l, TILES_BEFORE["uv"]))
                    pe.wait_ge(turned_lo, nth(turned_lo, l, 2 * TURNED["n1", T - 1] + 2))
                    pe.wait_ge(sgu_ready, nth(sgu_ready, l, 1))
                pe.wait_ge(masked, nth(masked, l, u - 1))
                nc.tensor.matmul(work[:, u % 2, 0:n], qaT[lo:lo + HD, h // 2, t * P:(t + 1) * P],
                                 kaT[lo:lo + HD, h // 2, 0:n], start=True, stop=True).then_inc(scored, 1)

            def a_turn(l, u):
                pe.wait_ge(exped, nth(exped, l, u + 1))
                pe.wait_ge(p_copied, nth(p_copied, l, u))
                for j in range(u // NH + 1):
                    mm = nc.tensor.transpose(work[:, 2, j * P:(j + 1) * P], probs[:, u % 2, j * P:(j + 1) * P], ident[:])
                mm.then_inc(p_turned, 1)

            def a_weigh(l, u):
                t, h = divmod(u, NH)
                pe.wait_ge(p_copied, nth(p_copied, l, u + 1))
                pe.wait_ge(a_out, nth(a_out, l, t))
                for j in range(t + 1):
                    mm = nc.tensor.matmul(work[:, 3, h * HD:(h + 1) * HD], probsT[:, u % 2, j * P:(j + 1) * P],
                                          va[:, j, h * HD:(h + 1) * HD], start=(j == 0), stop=(j == t))
                mm.then_inc(weighed, 1)

            def a_step(l, j):
                if j < UNITS:
                    a_scores(l, j)
                if 1 <= j <= UNITS:
                    a_turn(l, j - 1)
                if 2 <= j < UNITS + 2:
                    a_weigh(l, j - 2)

            def sgu_weights(l):
                pe.wait_ge(sgu_loaded, nth(sgu_loaded, l, 64))
                pe.wait_ge(turned_lo, nth(turned_lo, l, 2 * TURNED["n1", T - 1] + 2))
                for g in range(G):
                    mm = nc.tensor.transpose(work[:, 0, g * P:(g + 1) * P], sgu_raw[:, g], ident[:])
                mm.then_inc(sgu_turned, 1)

            def sgu_mix(l):
                pe.wait_ge(ln_done, nth(ln_done, l, 1))
                pe.wait_ge(masked, nth(masked, l, UNITS))
                for g in range(G):
                    mm = nc.tensor.matmul(work[:, g // 2, (g % 2) * 256:(g % 2 + 1) * 256].rearrange("p (t c) -> p t c", t=T),
                                          sgu_T[:, g], vs[:, :, g * HD:(g + 1) * HD], start=True, stop=True)
                    if g % 2:
                        mm.then_inc(gated, 1)

            def c_turn(l, c):
                if c == 0:
                    pe.wait_ge(gate_out, nth(gate_out, l, 1))
                    pe.wait_ge(a_out, nth(a_out, l, T))
                pe.wait_ge(rotated, nth(rotated, l, c + 1))
                pe.wait_ge(c_copied, nth(c_copied, l, c))
                pe.wait_ge(c_state, nth(c_state, l, c))
                for i in range(2):
                    for p in range(PAIRS):
                        mm = nc.tensor.transpose(work[:, i, p * P:(p + 1) * P],
                                                 qkc[:, c, i * CW + p * P:i * CW + (p + 1) * P], ident[:])
                mm.then_inc(c_turned, 1)

            def c_products(l, c):
                pe.wait_ge(c_copied, nth(c_copied, l, c + 1))
                pe.wait_ge(c_masked, nth(c_masked, l, c))
                pe.wait_ge(c_centred, nth(c_centred, l, c))
                for h in range(NH):
                    lo, p = HD * (h % 2), h // 2
                    mm = nc.tensor.matmul(work[:, 2 + h % 2, p * P:(p + 1) * P],
                                          qkT[lo:lo + HD, 1, p * P:(p + 1) * P],
                                          qkT[lo:lo + HD, 0, p * P:(p + 1) * P], start=True, stop=True)
                mm.then_inc(c_inner, 1)
                pe.wait_ge(emptied, nth(emptied, l, TILES_BEFORE["vc"] + c + 1))
                if c == T - 1:
                    return
                for p in range(PAIRS):
                    mm = nc.tensor.matmul(work[:, 0, p * P:(p + 1) * P], qkc[:, c, CW + p * P:CW + (p + 1) * P],
                                          vc[:, c, p * P:(p + 1) * P], start=True, stop=True)
                mm.then_inc(c_kv, 1)

            def c_read(l, c):
                pe.wait_ge(c_masked, nth(c_masked, l, c + 1))
                pe.wait_ge(c_state, nth(c_state, l, c))
                for p in range(PAIRS):
                    if c > 0:
                        nc.tensor.matmul(work[:, 2, p * P:(p + 1) * P], qkT[:, 0, p * P:(p + 1) * P], state[:, c % 2, p],
                                         start=True, stop=False, skip_group_check=True)
                    for h in (2 * p, 2 * p + 1):
                        mm = nc.tensor.matmul(work[:, 2, h * HD:(h + 1) * HD], innerT[:, h], vc[:, c, h * HD:(h + 1) * HD],
                                              start=(c == 0), stop=True, skip_group_check=True)
                mm.then_inc(c_y, 1)

            def c_slot(l, k):
                if k % 2 == 0:
                    if k >= 2:
                        c_read(l, k // 2 - 1)
                    if k < 2 * T:
                        c_turn(l, k // 2)
                elif k < 2 * T:
                    c_products(l, k // 2)

            def x_scores(l, u):
                pair, t = divmod(u, T)
                if u == 0:
                    pe.wait_ge(emptied, nth(emptied, l, TILES_BEFORE["vm0"]))
                    pe.wait_ge(turned_lo, nth(turned_lo, l, 2 * TURNED["n2", T - 1] + 2))
                pe.wait_ge(emptied, nth(emptied, l, TILES_BEFORE["qx1" if pair == 0 else "wo0"]))
                pe.wait_ge(x_exped, nth(x_exped, l, u - 1))
                for i in range(2):
                    for k in range(2):
                        c = 2 * (2 * pair + i) + k
                        mm = nc.tensor.matmul(work[:, u % 2, i * MEM:(i + 1) * MEM], qxT[:, c, t * P:(t + 1) * P],
                                              kmT[:, c, :], start=(k == 0), stop=(k == 1))
                mm.then_inc(x_scored, 1)

            def x_turn(l, u):
                pe.wait_ge(x_normed, nth(x_normed, l, u + 1))
                pe.wait_ge(x_copied, nth(x_copied, l, u))
                for j in range(2 * MT):
                    mm = nc.tensor.transpose(work[:, 2, j * P:(j + 1) * P], x_probs[:, u % 2, j * P:(j + 1) * P], ident[:])
                mm.then_inc(x_turned, 1)

            def x_weigh(l, u):
                pair = u // T
                pe.wait_ge(x_copied, nth(x_copied, l, u + 1))
                pe.wait_ge(x_lo, nth(x_lo, l, u))
                pe.wait_ge(emptied, nth(emptied, l, TILES_BEFORE["qx0"]))
                for k in range(BK):
                    i = k * P // XD
                    for j in range(MT):
                        mm = nc.tensor.matmul(work[:, 3, k * P:(k + 1) * P], vm[:, j, (pair * BK + k) * P:(pair * BK + k + 1) * P],
                                              x_probsT[:, u % 2, (i * MT + j) * P:(i * MT + j + 1) * P],
                                              start=(j == 0), stop=(j == MT - 1))
                mm.then_inc(x_weighed, 1)

            def x_step(l, j):
                if j < XUNITS:
                    x_scores(l, j)
                if 2 <= j < XUNITS + 2:
                    x_weigh(l, j - 2)
                if 1 <= j <= XUNITS:
                    x_turn(l, j - 1)

            def before_tile(l, b, t):
                if b == FIRST_BLOCK["va"]:
                    if t == 0:
                        turn_ahead(l, "n1", 0)
                        turn_ahead(l, "n1", 1)
                    turned_in(l, ("n1", t))
                if b == FIRST_BLOCK["out0"]:
                    turned_in(l, ("mix", t))
                if b in (FIRST_BLOCK["wo0"], FIRST_BLOCK["wo0"] + 1):
                    pe.wait_ge(x_lo, nth(x_lo, l, (b - FIRST_BLOCK["wo0"]) * T + t + 1))
                    pe.sem_inc(waits_passed, 1)

            def turn_ahead(l, phase, t):
                if phase == "n1":
                    pe.wait_ge(normed, nth(normed, l, NORMED["n1", t] + 1))
                    turn(l, ("n1", t), hs[:, t % 2])
                else:
                    pe.wait_ge(c_out, nth(c_out, l, t + 1))
                    if t == 1:
                        pe.wait_ge(c_centred, nth(c_centred, l, T))
                    turn(l, ("mix", t), ys[:, t])

            def after_tile(l, b, t):
                if b == FIRST_BLOCK["ka"] + 1 and t == 0:
                    sgu_weights(l)
                j = unit_step(b, t)
                if 0 <= j < UNITS + 2:
                    a_step(l, j)
                if j == UNITS + 2:
                    sgu_mix(l)
                k = (b - FIRST_BLOCK["gc"]) * T + t + 2
                if 0 <= k <= 2 * T:
                    c_slot(l, k)
                if b == FIRST_BLOCK["va"] and t < T - 2:
                    turn_ahead(l, "n1", t + 2)
                if b == FIRST_BLOCK["out0"] - 1 and t >= T - 2:
                    turn_ahead(l, "mix", t - T + 2)
                if b == FIRST_BLOCK["wo1"] and t == 3:
                    turn_n3(l, 0)
                if b == FIRST_BLOCK["wo1"] + 1 and t == 2:
                    turn_n3(l, 1)
                if b == FIRST_BLOCK["out0"] and t < T - 2:
                    turn_ahead(l, "mix", t + 2)
                if b == FIRST_BLOCK["out0"] + 1 and t < MT:
                    pe.wait_ge(normed, nth(normed, l, NORMED["mem", t] + 1))
                    turn(l, ("mem", t), hs[:, t])
                if b == FIRST_BLOCK["qx1"] + 1 and t % 2:
                    x_step(l, t // 2)
                if b == FIRST_BLOCK["wo0"]:
                    x_step(l, XUNITS - 2 + t)

            def after_block(l, b):
                if b == FIRST_BLOCK["qx1"] + 1:
                    for j in range(2, XUNITS - 2):
                        x_step(l, j)
                t = b - (FIRST_BLOCK["km0"] + 1)
                if 0 <= t < T:
                    pe.wait_ge(normed, nth(normed, l, NORMED["n2", t] + 1))
                    turn(l, ("n2", t), hs[:, t % 2])

            def turn_n3(l, t):
                pe.wait_ge(normed, nth(normed, l, NORMED["n3", t] + 1))
                turn(l, ("n3", t), hs[:, t % 2])

            N3_SLOTS = ((1, 0), (1, 1))

            def first_up(l):
                for half in range(2):
                    turned_in(l, ("n3", 2 * half + 1))
                    for kb in range(KB):
                        b = HEAD_BLOCKS + kb
                        if half == 0:
                            pe.wait_ge(w_lo_done, nth(w_lo_done, l, b + 1))
                        for t in range(4):
                            if half == 0 and kb == 0:
                                pe.wait_ge(gained, nth(gained, l, GAINED["e2", 1, t] + 1))
                            mm = block_tile(b % WSLOTS, kb, "feat", t, S // 2, hT_hi, hT_lo, 512, at=half * (S // 2))
                            if half:
                                mm.then_inc(tile_done, 1)
                            if half == 0 and (kb, t) in N3_SLOTS:
                                turn_n3(l, 2 + N3_SLOTS.index((kb, t)))

            def mlp_group(l, g, jobs=GROUP_JOBS):
                for name in jobs:
                    i = GROUP_JOBS.index(name)
                    for kb in range(KB):
                        b = HEAD_BLOCKS + KB * i + kb
                        pe.wait_ge(w_lo_done, nth(w_lo_done, l, g * GROUP_BLOCKS + (b + 1)))
                        for t in range(4):
                            if kb == 0:
                                if name == "up0":
                                    pe.wait_ge(added, nth(added, l, g * UP_TILES + (t + 1 - T)))
                                elif name in ("up1", "dn0"):
                                    pe.wait_ge(emptied, nth(emptied, l, g * UP_TILES + (HEAD_TILES + 4 * (i - 1) + t + 1)))
                                else:
                                    pe.wait_ge(added, nth(added, l, g * UP_TILES + (t + 1)))
                            if name == "dn0" and t == 0:
                                pe.wait_ge(hidden_lo, nth(hidden_lo, l, g * UP_TILES + 4 * (kb + 1)))
                            if i < 2:
                                mm = block_tile(b % WSLOTS, kb, "feat", t, S, hT_hi, hT_lo, 512)
                            else:
                                mm = block_tile(b % WSLOTS, kb, "tok", t, 512, uT_hi, uT_lo, 512)
                            mm.then_inc(tile_done, 1)

            with pe.Fori(0, DEPTH) as l:
                for name, _, _, cols, mode, tiles, moving in JOBS:
                    if name == "km0":
                        turned_in(l, ("mem", MT - 1))
                    if name == "qx0":
                        turned_in(l, ("n2", T - 1))
                    hi, lo = (memT_hi, memT_lo) if name[1:2] == "m" and name[0] in "kv" else (hT_hi, hT_lo)
                    for kb, t in EARLY_PAIR if name == "wo1" else BY_BLOCK:
                        b = FIRST_BLOCK[name] + kb
                        if t < tiles:
                            before_tile(l, b, t)
                            if t == 0:
                                pe.wait_ge(w_lo_done, nth(w_lo_done, l, b + 1))
                            if kb == 0:
                                user = BANK_USER[name, t]
                                if user is None:
                                    pe.wait_ge(added, nth(added, l, t + 1 - T))
                                elif user[0]:
                                    pe.wait_ge(gained, nth(gained, l, user[1] + 1))
                                else:
                                    pe.wait_ge(emptied, nth(emptied, l, user[1] + 1))
                            mm = block_tile(b % WSLOTS, kb, mode, t, moving, hi, lo, cols)
                            mm.then_inc(tile_done, 1)
                            after_tile(l, b, t)
                        if t == tiles - 1:
                            after_block(l, b)
                first_up(l)
                mlp_group(l, 0, GROUP_JOBS[1:])
                with pe.Fori(1, GROUPS) as g:
                    mlp_group(l, g)

        @block.scalar
        def _(act):
            start_counts(act, emptied, turned_hi, hidden_hi, p_copied, c_copied, x_exped, x_copied)
            act.dma_start(ident[:], c_ident).then_inc(first_loaded, 16)
            act.dma_start(xs[:, 1], x[0, P:2 * P]).then_inc(x_loaded[1], 16)
            act.wait_ge(x_loaded[0], 16)
            for t in range(2, T):
                act.dma_start(xs[:, t], x[0, t * P:(t + 1) * P]).then_inc(x_loaded[t], 16)
            for dst, src in ((upper, c_upper), (decay, c_decay), (log_count, c_logcount)):
                act.dma_start(dst[:], src).then_inc(const_loaded, 16)
            act.wait_ge(trig_done, 1)
            nc.scalar.activation(sin[:], angle[:], ACT.Sin)
            nc.scalar.activation(cos[:], turns[:], ACT.Sin).then_inc(trig_done, 1)

            def split_hi(l, b, cols=512, g=0, of_next=False):
                slot, at = b % WSLOTS, (GROUP_BLOCKS if of_next else 0) + b
                act.wait_ge(w_loaded[slot], nth(w_loaded[slot], l, g * (16 * GROUP_BLOCKS // WSLOTS) + 16 * (at // WSLOTS + 1)))
                act.wait_ge(tile_done, nth(tile_done, l, g * GROUP_TILES + done(at - WSLOTS)))
                nc.scalar.activation(w_hi[:, slot, :, 0:cols], w_raw[:, slot, :, 0:cols], ACT.Copy).then_inc(w_hi_done, 1)

            def head_split(l, b):
                split_hi(l, b, JOBS[b // KB][3] if b < HEAD_BLOCKS else 512)

            def sum_squares(l, key, src):
                r = STATS[key]
                act.wait_ge(rooted, nth(rooted, l, r - 1))
                nc.scalar.activation(squares[:, r % 2], src, ACT.Square, accum_out=sumsq[:, r % 2]).then_inc(summed, 1)

            def branch_squares(l, e, half, t, src):
                if half == 0:
                    nc.scalar.activation(half_squares[:, t], src, ACT.Square, scale=D ** -0.5,
                                         accum_out=half_sum[:, t:t + 1]).then_inc(half_summed, 1)
                    return
                r = STATS[e, t]
                act.wait_ge(rooted, nth(rooted, l, r - 1))
                nc.scalar.activation(squares[:, r % 2, 0:512], src, ACT.Square, scale=D ** -0.5,
                                     accum_out=sumsq[:, r % 2]).then_inc(summed, 1)

            def turn_hi(l, key, dst, t):
                n = TURNED[key]
                for half in range(2):
                    act.wait_ge(turned, nth(turned, l, 2 * n + half + 1))
                    nc.scalar.activation(dst[:, half * BK:(half + 1) * BK, t * P:(t + 1) * P],
                                         work[:, 2 * (n % 2) + half].rearrange("p (k c) -> p k c", k=BK),
                                         ACT.Copy).then_inc(turned_hi, 1)

            def empty(l, b, t):
                name, _, _, cols, _, _, moving = JOBS[b // KB]
                src = proj[:, t, 0:moving]
                act.wait_ge(tile_done, nth(tile_done, l, done(b, t)))
                if name in BRANCH_JOBS:
                    branch_squares(l, "e1" if name[0] == "o" else "e2", int(name[-1]), t, src)
                    return
                func, scale = ACT.Copy, 1.0
                if name == "va":
                    dst = va[:, t]
                elif name == "qa":
                    dst, scale = qaT[:, t], HD ** -0.5
                elif name == "ka":
                    dst = kaT[:, t]
                elif name == "uv":
                    nc.scalar.activation(ys[:, t, AW:AW + BW], proj[:, t, 0:BW], func)
                    src, dst = proj[:, t, BW:2 * BW], vs[:, t]
                elif name in ("qc", "kc"):
                    lo = CW * (name == "kc")
                    dst = qkc[:, t, lo:lo + CW]
                elif name == "vc":
                    dst = vc[:, t]
                elif name == "gc":
                    dst, func = ys[:, t, AW + BW:D], ACT.Silu
                elif name in ("km0", "km1"):
                    dst = kmT[:, 4 * int(name[-1]) + t]
                elif name in ("vm0", "vm1"):
                    lo = 512 * int(name[-1])
                    dst = vm[:, t, lo:lo + 512]
                else:
                    dst, scale = qxT[:, 4 * int(name[-1]) + t], XD ** -0.5
                nc.scalar.activation(dst, src, func, scale=scale).then_inc(emptied, 1)

            def a_step(l, j):
                if j < UNITS:
                    n = (j // NH + 1) * P
                    act.wait_ge(masked, nth(masked, l, j + 1))
                    nc.scalar.activation(probs[:, j % 2, 0:n], probs[:, j % 2, 0:n], ACT.Exp, scale=-1.0,
                                         bias=neg_max[:, j % 2, 0:1], accum_out=den[:, j:j + 1]).then_inc(exped, 1)
                if 1 <= j <= UNITS:
                    u = j - 1
                    n = (u // NH + 1) * P
                    act.wait_ge(p_turned, nth(p_turned, l, u + 1))
                    act.wait_ge(weighed, nth(weighed, l, u - 1))
                    nc.scalar.copy(probsT[:, u % 2, 0:n], work[:, 2, 0:n]).then_inc(p_copied, 1)

            def c_copy(l, c):
                act.wait_ge(c_turned, nth(c_turned, l, c + 1))
                nc.scalar.copy(qkT[:], work[:, 0:2, 0:CW]).then_inc(c_copied, 1)

            def x_step(l, j):
                if j < XUNITS:
                    act.wait_ge(x_max, nth(x_max, l, j + 1))
                    act.wait_ge(x_turned, nth(x_turned, l, j - 1))
                    for i in range(2):
                        last = nc.scalar.activation(x_probs[:, j % 2, i * MEM:(i + 1) * MEM], work[:, j % 2, i * MEM:(i + 1) * MEM],
                                                    ACT.Exp, bias=x_neg[:, j % 2, i:i + 1], accum_out=x_den[:, j, i:i + 1])
                    last.then_inc(x_exped, 1)
                if j >= 2:
                    pair, t = divmod(j - 2, T)
                    act.wait_ge(x_weighed, nth(x_weighed, l, j - 1))
                    nc.scalar.activation(hT_hi[:, pair * BK:(pair + 1) * BK, t * P:(t + 1) * P],
                                         work[:, 3].rearrange("p (k c) -> p k c", k=BK), ACT.Copy).then_inc(x_hi, 1)
                if 1 <= j <= XUNITS:
                    u = j - 1
                    act.wait_ge(x_turned, nth(x_turned, l, u + 1))
                    act.wait_ge(x_weighed, nth(x_weighed, l, u - 1))
                    nc.scalar.copy(x_probsT[:, u % 2], work[:, 2]).then_inc(x_copied, 1)

            def after_tile(l, b, t):
                if b == FIRST_BLOCK["out0"] - 1 and t >= T - 2:
                    turn_hi(l, ("mix", t - T + 2), hT_hi, t - T + 2)
                if b == FIRST_BLOCK["out0"] and t < T - 2:
                    turn_hi(l, ("mix", t + 2), hT_hi, t + 2)
                if b == FIRST_BLOCK["out0"] + 1 and t < MT:
                    turn_hi(l, ("mem", t), memT_hi, t)
                j = unit_step(b, t)
                if 0 <= j < UNITS + 2:
                    a_step(l, j)
                k = (b - FIRST_BLOCK["gc"]) * T + t + 2
                if 0 <= k < 2 * T and k % 2 == 0:
                    c_copy(l, k // 2)
                if b == FIRST_BLOCK["qx1"] + 1 and t % 2:
                    x_step(l, t // 2)
                if b == FIRST_BLOCK["wo0"]:
                    x_step(l, XUNITS - 2 + t)

            def before_block(l, b):
                if b == FIRST_BLOCK["qc"]:
                    act.wait_ge(emptied, nth(emptied, l, TILES_BEFORE["qc"]))
                    nc.scalar.activation(ys[:, :, AW:AW + BW], ys[:, :, AW:AW + BW], ACT.Gelu_apprx_tanh)
                    nc.scalar.activation(vs[:], vs[:], ACT.Gelu_apprx_tanh).then_inc(gelu_done, 1)
                if b == FIRST_BLOCK["km0"]:
                    for t in (0, 1):
                        act.wait_ge(x_ready, nth(x_ready, l, BRANCHED["e1", t] + 1))
                        sum_squares(l, ("n2", t), xs[:, t])
                if b == FIRST_BLOCK["km0"] + 1:
                    for t in (2, 3):
                        act.wait_ge(x_ready, nth(x_ready, l, BRANCHED["e1", t] + 1))
                        sum_squares(l, ("n2", t), xs[:, t])
                t = b - (FIRST_BLOCK["km0"] + 2)
                if 0 <= t < T:
                    turn_hi(l, ("n2", t), hT_hi, t)

            def mlp_group(l, g, last):
                for i in range(GROUP_BLOCKS):
                    b = HEAD_BLOCKS + i
                    if i > 0 and (i < GROUP_BLOCKS - 1 or not last):
                        split_hi(l, b + 1, g=g)
                    if last and i in (5, 7):
                        for t in range(T):
                            half = (i - 5) // 2
                            act.wait_ge(added, nth(added, l, g * UP_TILES + (T * half + t + 1)))
                            branch_squares(l, "e3", half, t, ys[:, t, half * 512:(half + 1) * 512])
                    if i in (1, 3):
                        for t in range(5):
                            m = 2 * (i - 1) + t
                            if t < 4:
                                act.wait_ge(tile_done, nth(tile_done, l, g * GROUP_TILES + done(b, t)))
                                act.wait_ge(hidden_lo, nth(hidden_lo, l, g * UP_TILES + (m - 1)))
                                nc.scalar.activation(relu[:, m % 2], proj[:, t], ACT.Relu).then_inc(emptied, 1)
                            if t >= 1:
                                act.wait_ge(hidden_sq, nth(hidden_sq, l, g * UP_TILES + m))
                                nc.scalar.activation(uT_hi[:, m - 1], relu[:, (m - 1) % 2], ACT.Copy).then_inc(hidden_hi, 1)

            with act.Fori(0, DEPTH) as l:
                for what, t in N1_ACT:
                    if what == "x":
                        act.wait_ge(x_loaded[t], 16)
                        act.wait_ge(x_ready, nth(x_ready, l, t + 1 - T))
                        sum_squares(l, ("n1", t), xs[:, t])
                    elif what == "h":
                        turn_hi(l, ("n1", t), hT_hi, t)
                    else:
                        head_split(l, 0)
                for b in range(HEAD_BLOCKS):
                    if b < HEAD_BLOCKS - 1:
                        head_split(l, b + 1)
                    before_block(l, b)
                    tiles = JOBS[b // KB][5]
                    if b < HEAD_BLOCKS - 1:
                        for t in range(tiles):
                            if b % KB == KB - 1:
                                empty(l, b, t)
                            after_tile(l, b, t)
                    if b == FIRST_BLOCK["out0"]:
                        for t in range(MT):
                            act.wait_ge(mem_loaded, nth(mem_loaded, l, 16))
                            sum_squares(l, ("mem", t), mem_in[:, t])
                    if b == FIRST_BLOCK["qx1"] + 1:
                        for j in range(2, XUNITS - 2):
                            x_step(l, j)
                for what, t in N3_ACT:
                    if what == "e":
                        empty(l, HEAD_BLOCKS - 1, t)
                    elif what == "x":
                        act.wait_ge(x_ready, nth(x_ready, l, BRANCHED["e2", t] + 1))
                        sum_squares(l, ("n3", t), xs[:, t])
                    elif what == "h":
                        turn_hi(l, ("n3", t), hT_hi, t)
                    else:
                        split_hi(l, HEAD_BLOCKS + t)
                with act.Fori(0, GROUPS - 1) as g:
                    mlp_group(l, g, False)
                    split_hi(l, HEAD_BLOCKS + GROUP_BLOCKS + 1, g=g)
                mlp_group(l, GROUPS - 1, True)

        @block.vector
        def _(dve):
            start_counts(dve, w_lo_done, added, normed, gained, turned_lo, hidden_sq, hidden_lo, sgu_ready,
                         masked, a_out, c_masked, c_state, c_centred, x_max, x_lo)
            steps = [0]

            def setup(ins):
                steps[0] += 1
                ins.then_inc(dve_setup, 1)
                dve.wait_ge(dve_setup, steps[0])

            dve.wait_ge(first_loaded, 16 * 3)
            setup(nc.vector.tensor_copy(pos_f[:], pos_i[:]))
            setup(nc.vector.memset(state[:], 0.0))
            for t in range(T):
                setup(nc.vector.tensor_scalar(angle[:, t], inv[:], pos_f[:, t:t + 1], None, ALU.mult))
            round_up = 1.5 * 2.0 ** 23
            setup(nc.vector.tensor_scalar(turns[:], angle[:], 1.0 / TURN, round_up, ALU.mult, ALU.add))
            setup(nc.vector.tensor_scalar(turns[:], turns[:], -round_up, None, ALU.add))
            for piece in TURN_PIECES:
                setup(nc.vector.scalar_tensor_tensor(out=angle[:], in0=turns[:], scalar=-piece, in1=angle[:],
                                                     op0=ALU.mult, op1=ALU.add))
            pi = float(np.nextafter(np.float32(np.pi), np.float32(0)))
            setup(nc.vector.tensor_scalar(angle[:], angle[:], pi, -pi, ALU.min, ALU.max))
            setup(nc.vector.scalar_tensor_tensor(out=turns[:], in0=angle[:], scalar=-1.0, in1=angle[:],
                                                 op0=ALU.mult, op1=ALU.max))
            setup(nc.vector.tensor_scalar(turns[:], turns[:], -1.0, float(np.float32(np.pi / 2)), ALU.mult, ALU.add))
            dve.sem_inc(trig_done, 1)

            def split_lo(l, b, cols=512, g=0):
                slot = b % WSLOTS
                dve.wait_ge(w_hi_done, nth(w_hi_done, l, g * GROUP_BLOCKS + (b + 1)))
                nc.vector.tensor_tensor(w_lo[:, slot, :, 0:cols], w_raw[:, slot, :, 0:cols],
                                        w_hi[:, slot, :, 0:cols].bitcast(F32), ALU.subtract).then_inc(w_lo_done, 1)

            def head_split(l, b):
                split_lo(l, b, JOBS[b // KB][3] if b < HEAD_BLOCKS else 512)

            def norm(l, key, src):
                n, t = NORMED[key], key[1]
                r = STATS[key]
                before = [k for k in NORMED if NORMED[k] < n and k[1] % 2 == t % 2]
                free = 2 * TURNED[before[-1]] + 2 if before else 0
                at0, at1, at2 = values(dve, nth(rooted, l, r + 1), nth(gain_loaded[key[0]], l, 16), nth(turned, l, free))
                dve.wait_ge(rooted, at0)
                dve.wait_ge(gain_loaded[key[0]], at1)
                dve.wait_ge(turned, at2)
                nc.vector.scalar_tensor_tensor(out=hs[:, t % 2], in0=src, scalar=rstd[:, r],
                                               in1=gains[:, GAIN_SLOT[key[0]]], op0=ALU.mult,
                                               op1=ALU.mult).then_inc(normed, 1)

            def gain(l, e, half, t):
                h = slice(half * 512, (half + 1) * 512)
                if half:
                    at0, at1 = values(dve, nth(summed, l, STATS[e, t] + 1), nth(gain_loaded[e], l, 16))
                    dve.wait_ge(summed, at0)
                else:
                    at0, at1 = values(dve, nth(half_summed, l, BRANCHED[e, t] + 1), nth(gain_loaded[e], l, 16))
                    dve.wait_ge(half_summed, at0)
                dve.wait_ge(gain_loaded[e], at1)
                nc.vector.tensor_tensor(ys[:, t, h], ys[:, t, h] if e == "e3" else proj[:, t],
                                        gains[:, GAIN_SLOT[e], h], ALU.mult).then_inc(gained, 1)

            def update(l, e, t):
                at0, at1 = values(dve, nth(rooted, l, STATS[e, t] + 1), nth(gained, l, GAINED[e, 1, t] + 1))
                dve.wait_ge(rooted, at0)
                dve.wait_ge(gained, at1)
                nc.vector.scalar_tensor_tensor(out=xs[:, t], in0=ys[:, t], scalar=rstd[:, STATS[e, t]], in1=xs[:, t],
                                               op0=ALU.mult, op1=ALU.add).then_inc(x_ready, 1)

            def turn_lo(l, key, hi, lo, t):
                n = TURNED[key]
                for half in range(2):
                    dve.wait_ge(turned_hi, nth(turned_hi, l, 2 * n + half + 1))
                    at = (slice(None), slice(half * BK, (half + 1) * BK), slice(t * P, (t + 1) * P))
                    nc.vector.tensor_tensor(lo[at], work[:, 2 * (n % 2) + half].rearrange("p (k c) -> p k c", k=BK),
                                            hi[at].bitcast(F32), ALU.subtract).then_inc(turned_lo, 1)

            def a_step(l, links, j):
                if j < UNITS:
                    t = j // NH
                    n = (t + 1) * P
                    at0, at1 = values(dve, nth(scored, l, j + 1), nth(p_turned, l, j - 1))
                    dve.wait_ge(scored, at0)
                    dve.wait_ge(p_turned, at1)
                    dve.sem_inc(waits_passed, 1)
                    nc.vector.tensor_tensor_reduce(out=probs[:, j % 2, 0:n], in0=work[:, j % 2, 0:n],
                                                   in1=log_count[:, mask_offset(t):mask_offset(t) + n],
                                                   scale=-1.0, scalar=3e38, op0=ALU.add, op1=ALU.min,
                                                   accum_out=neg_max[:, j % 2, 0:1]).then_inc(masked, 1)
                if j >= 2 and (j - 2) % NH == NH - 1:
                    t = (j - 2) // NH
                    heads = slice(t * NH, (t + 1) * NH)
                    dve.wait_ge(exped, nth(exped, l, (t + 1) * NH))
                    nc.vector.reciprocal(rden[:, heads], den[:, heads]).then_inc(dve_link, 1)
                    dve.wait_ge(dve_link, nth(dve_link, l, next(links)))
                    dve.sem_inc(waits_passed, 1)
                    dve.wait_ge(weighed, nth(weighed, l, (t + 1) * NH))
                    nc.vector.tensor_tensor(ys[:, t, 0:AW].rearrange("p (h e) -> p h e", h=NH),
                                            work[:, 3, 0:AW].rearrange("p (h e) -> p h e", h=NH),
                                            spread(rden[:, heads], HD), ALU.mult).then_inc(a_out, 1)

            def layer_norm(l, links):
                dve.wait_ge(gelu_done, nth(gelu_done, l, 1))
                for t in range(T):
                    last = nc.vector.bn_stats(ln_stats[:, t], vs[:, t])
                last.then_inc(dve_link, 1)
                dve.wait_ge(dve_link, nth(dve_link, l, next(links)))
                dve.sem_inc(waits_passed, 1)
                for t in range(T):
                    last = nc.vector.bn_aggr(ln_mv[:, t], ln_stats[:, t])
                last.then_inc(ln_var, 1)

            def layer_norm_scale(l):
                dve.wait_ge(ln_root, nth(ln_root, l, 1))
                for t in range(T):
                    last = nc.vector.tensor_scalar(vs[:, t], vs[:, t], ln_mv[:, t, 0:1], ln_rstd[:, t:t + 1],
                                                   ALU.subtract, ALU.mult)
                last.then_inc(ln_scaled, 1)

            def gate(l):
                for g in range(G):
                    dve.wait_ge(gated, nth(gated, l, g // 2 + 1))
                    dst = ys[:, :, AW + g * HD:AW + (g + 1) * HD]
                    last = nc.vector.scalar_tensor_tensor(
                        out=dst, in0=work[:, g // 2, (g % 2) * 256:(g % 2 + 1) * 256].rearrange("p (t c) -> p t c", t=T),
                        scalar=sgu_bias[:, g:g + 1], in1=dst, op0=ALU.add, op1=ALU.mult)
                last.then_inc(gate_out, 1)

            def c_mask(l, c):
                dve.wait_ge(c_inner, nth(c_inner, l, c + 1))
                for i in range(2):
                    last = nc.vector.tensor_tensor(innerT[:, i:NH:2],
                                                   work[:, 2 + i, 0:CW].rearrange("p (h c) -> p h c", h=3),
                                                   again(upper[:], 3), ALU.mult)
                last.then_inc(c_masked, 1)
                if c == T - 1:
                    return
                at0, at1 = values(dve, nth(c_kv, l, c + 1), nth(c_state, l, c))
                dve.wait_ge(c_kv, at0)
                dve.wait_ge(c_state, at1)
                if c:
                    dve.wait_ge(c_y, nth(c_y, l, c))
                for lo in (0, HD):
                    at = (slice(lo, lo + HD), slice(None), slice(lo, lo + HD))
                    kv = work[:, 0, 0:CW].rearrange("p (h c) -> p h c", h=PAIRS)[at]
                    new, old = state[:, (c + 1) % 2][at], state[:, c % 2][at]
                    if c == 0:
                        last = nc.vector.tensor_copy(new, kv)
                    else:
                        last = nc.vector.tensor_tensor(new, kv, old, ALU.add)
                last.then_inc(c_state, 1)

            def group_norm(l, links, c):
                dve.wait_ge(c_y, nth(c_y, l, c + 1))
                y = work[:, 2, 0:CW].rearrange("p (h e) -> p h e", h=NH)
                ych = yc[:, c].rearrange("p (h e) -> p h e", h=NH)
                nc.vector.reduce_sum(gn_sum[:], y, AX_X).then_inc(dve_link, 1)
                dve.wait_ge(dve_link, nth(dve_link, l, next(links)))
                dve.sem_inc(waits_passed, 1)
                nc.vector.tensor_scalar(gn_mean[:], gn_sum[:], 1.0 / HD, None, ALU.mult).then_inc(dve_link, 1)
                dve.wait_ge(dve_link, nth(dve_link, l, next(links)))
                dve.sem_inc(waits_passed, 1)
                nc.vector.tensor_tensor(ych, y, spread(gn_mean[:], HD), ALU.subtract).then_inc(c_centred, 1)
                dve.wait_ge(c_centred, nth(c_centred, l, c + 1))
                nc.vector.tensor_tensor(yc2[:], yc[:, c], yc[:, c], ALU.mult).then_inc(dve_link, 1)
                dve.wait_ge(dve_link, nth(dve_link, l, next(links)))
                dve.sem_inc(waits_passed, 1)
                nc.vector.reduce_sum(gn_var[:], yc2[:].rearrange("p (h e) -> p h e", h=NH), AX_X).then_inc(gn_var_done, 1)

            def group_scale(l, links, c):
                ych = yc[:, c].rearrange("p (h e) -> p h e", h=NH)
                dve.wait_ge(gn_root, nth(gn_root, l, c + 1))
                nc.vector.tensor_tensor(ych, ych, spread(gn_rstd[:], HD), ALU.mult).then_inc(dve_link, 1)
                dve.wait_ge(dve_link, nth(dve_link, l, next(links)))
                dve.sem_inc(waits_passed, 1)

            def c_gate(l, c):
                dve.wait_ge(emptied, nth(emptied, l, TILES_BEFORE["gc"] + c + 1))
                nc.vector.tensor_tensor(ys[:, c, AW + BW:D], ys[:, c, AW + BW:D], yc[:, c], ALU.mult).then_inc(c_out, 1)

            def x_step(l, links, j):
                if 1 <= j <= XUNITS:
                    u = j - 1
                    dve.wait_ge(x_exped, nth(x_exped, l, u + 1))
                    nc.vector.reciprocal(x_rden[:, u], x_den[:, u]).then_inc(dve_link, 1)
                    dve.wait_ge(dve_link, nth(dve_link, l, next(links)))
                    dve.sem_inc(waits_passed, 1)
                    two = x_probs[:, u % 2].rearrange("p (h m) -> p h m", h=2)
                    nc.vector.tensor_tensor(two, two, spread(x_rden[:, u], MEM), ALU.mult).then_inc(x_normed, 1)
                if j < XUNITS:
                    dve.wait_ge(x_scored, nth(x_scored, l, j + 1))
                    nc.vector.reduce_max(x_top[:, j % 2], work[:, j % 2].rearrange("p (h m) -> p h m", h=2), AX_X).then_inc(dve_link, 1)
                    dve.wait_ge(dve_link, nth(dve_link, l, next(links)))
                    dve.sem_inc(waits_passed, 1)
                    dve.wait_ge(x_exped, nth(x_exped, l, j - 1))
                    nc.vector.tensor_scalar(x_neg[:, j % 2], x_top[:, j % 2], -1.0, None, ALU.mult).then_inc(x_max, 1)
                if j >= 2:
                    pair, t = divmod(j - 2, T)
                    at = (slice(None), slice(pair * BK, (pair + 1) * BK), slice(t * P, (t + 1) * P))
                    dve.wait_ge(x_hi, nth(x_hi, l, j - 1))
                    nc.vector.tensor_tensor(hT_lo[at], work[:, 3].rearrange("p (k c) -> p k c", k=BK),
                                            hT_hi[at].bitcast(F32), ALU.subtract).then_inc(x_lo, 1)

            def after_tile(l, links, b, t):
                if b == FIRST_BLOCK["out0"] and t < T - 2:
                    turn_lo(l, ("mix", t + 2), hT_hi, hT_lo, t + 2)
                if b == FIRST_BLOCK["out0"] + 1:
                    gain(l, "e1", 0, t)
                    if t < MT:
                        turn_lo(l, ("mem", t), memT_hi, memT_lo, t)
                if b == FIRST_BLOCK["wo0"] + 1:
                    gain(l, "e2", 0, t)
                if b == FIRST_BLOCK["out1"] + 1:
                    gain(l, "e1", 1, t)
                    update(l, "e1", t)
                if b == FIRST_BLOCK["ka"] + 1 and t == 0:
                    dve.wait_ge(const_loaded, 16 * 3)
                    dve.wait_ge(sgu_turned, nth(sgu_turned, l, 1))
                    nc.vector.tensor_tensor(sgu_T[:], work[:, 0].rearrange("p (g i) -> p g i", g=G),
                                            again(upper[:], G),
                                            ALU.mult).then_inc(sgu_ready, 1)
                j = unit_step(b, t)
                if 0 <= j < UNITS + 2:
                    a_step(l, links, j)
                if j == UNITS + 3:
                    gate(l)
                k = (b - FIRST_BLOCK["gc"]) * T + t + 2
                if 0 <= k < 2 * T:
                    if k % 2:
                        c_mask(l, k // 2)
                        if k >= 3:
                            group_scale(l, links, k // 2 - 1)
                    elif k >= 2:
                        group_norm(l, links, k // 2 - 1)
                if k == 2 * T - 1:
                    c_gate(l, 0)
                if k == 2 * T:
                    c_gate(l, 1)
                    group_norm(l, links, T - 1)
                    turn_lo(l, ("mix", 0), hT_hi, hT_lo, 0)
                if k == 2 * T + 1:
                    c_gate(l, 2)
                    turn_lo(l, ("mix", 1), hT_hi, hT_lo, 1)
                    group_scale(l, links, T - 1)
                    c_gate(l, 3)
                if b == FIRST_BLOCK["qx1"] + 1 and t % 2:
                    x_step(l, links, t // 2)
                if b == FIRST_BLOCK["wo0"]:
                    x_step(l, links, XUNITS - 2 + t)

            def before_block(l, links, b):
                first = FIRST_BLOCK["km0"]
                if b == FIRST_BLOCK["qc"]:
                    layer_norm(l, links)
                if b == FIRST_BLOCK["qc"] + 1:
                    layer_norm_scale(l)
                if b == first:
                    norm(l, ("n2", 0), xs[:, 0])
                    norm(l, ("n2", 1), xs[:, 1])
                if b == first + 1:
                    norm(l, ("n2", 2), xs[:, 2])
                if first + 2 <= b < first + 2 + T:
                    turn_lo(l, ("n2", b - first - 2), hT_hi, hT_lo, b - first - 2)
                if b == first + 2:
                    norm(l, ("n2", 3), xs[:, 3])

            def mlp_group(l, g, last):
                for i in range(GROUP_BLOCKS):
                    b = HEAD_BLOCKS + i
                    if i > 0 and (i < GROUP_BLOCKS - 1 or not last):
                        split_lo(l, b + 1, g=g)
                    if i in (1, 3):
                        for t in range(5):
                            m = 2 * (i - 1) + t
                            if t < 4:
                                dve.wait_ge(emptied, nth(emptied, l, g * UP_TILES + (HEAD_TILES + m + 1)))
                                nc.vector.tensor_tensor(relu[:, m % 2], relu[:, m % 2], relu[:, m % 2],
                                                        ALU.mult).then_inc(hidden_sq, 1)
                            if t >= 1:
                                dve.wait_ge(hidden_hi, nth(hidden_hi, l, g * UP_TILES + m))
                                nc.vector.tensor_tensor(uT_lo[:, m - 1], relu[:, (m - 1) % 2], uT_hi[:, m - 1].bitcast(F32),
                                                        ALU.subtract).then_inc(hidden_lo, 1)
                    if i in (5, 7):
                        for t in range(T):
                            j = (i - 5) // 2
                            at0, at1 = values(dve, nth(tile_done, l, g * GROUP_TILES + done(b, t)), nth(y_zeroed, l, 1))
                            dve.wait_ge(tile_done, at0)
                            dve.wait_ge(y_zeroed, at1)
                            part_y = ys[:, t, j * 512:(j + 1) * 512]
                            nc.vector.tensor_tensor(part_y, proj[:, t], part_y, ALU.add).then_inc(added, 1)
                            if last and j == 1 and t >= 1:
                                gain(l, "e3", 1, t - 1)
                                update(l, "e3", t - 1)
                        if last and j == 1:
                            gain(l, "e3", 1, T - 1)
                            update(l, "e3", T - 1)
                    if last and i == 6:
                        for t in range(T):
                            gain(l, "e3", 0, t)

            with dve.Fori(0, DEPTH) as l:
                links = itertools.count(1)
                for what, t in N1_DVE:
                    if what == "n":
                        norm(l, ("n1", t), xs[:, t])
                    elif what == "h":
                        turn_lo(l, ("n1", t), hT_hi, hT_lo, t)
                    else:
                        head_split(l, 0)
                for b in range(HEAD_BLOCKS):
                    if b < HEAD_BLOCKS - 1:
                        head_split(l, b + 1)
                    before_block(l, links, b)
                    if b == HEAD_BLOCKS - 1:
                        continue
                    for t in range(JOBS[b // KB][5]):
                        after_tile(l, links, b, t)
                    if b == FIRST_BLOCK["out0"]:
                        for t in range(MT):
                            norm(l, ("mem", t), mem_in[:, t])
                    if b == FIRST_BLOCK["qx1"] + 1:
                        for j in range(2, XUNITS - 2):
                            x_step(l, links, j)
                for what, t in N3_DVE:
                    if what == "e":
                        gain(l, "e2", 1, t)
                    elif what == "x":
                        update(l, "e2", t)
                    elif what == "n":
                        norm(l, ("n3", t), xs[:, t])
                    elif what == "h":
                        turn_lo(l, ("n3", t), hT_hi, hT_lo, t)
                    else:
                        split_lo(l, HEAD_BLOCKS + t)
                with dve.Fori(0, GROUPS - 1) as g:
                    mlp_group(l, g, False)
                    split_lo(l, HEAD_BLOCKS + GROUP_BLOCKS + 1, g=g)
                mlp_group(l, GROUPS - 1, True)
                assert next(links) == DVE_LINKS + 1

        @block.gpsimd
        def _(pool):
            nc.gpsimd.memset(minus_half[:], -0.5).then_inc(setup_done, 1)
            pool.wait_ge(setup_done, 1)
            start_counts(pool, rooted, x_ready)

            def root(l, links, key):
                r = STATS[key]
                pool.wait_ge(summed, nth(summed, l, r + 1))
                pool.sem_inc(waits_passed, 1)
                nc.gpsimd.tensor_scalar(meansq[:, r % 2], sumsq[:, r % 2], 1.0 / D, EPS, ALU.mult, ALU.add).then_inc(pool_link, 1)
                pool.wait_ge(pool_link, nth(pool_link, l, next(links)))
                pool.sem_inc(waits_passed, 1)
                nc.gpsimd.tensor_tensor(rstd[:, r], meansq[:, r % 2], minus_half[:, 0:1], ALU.pow).then_inc(rooted, 1)

            def branch_halves(l, links, e):
                pool.wait_ge(half_summed, nth(half_summed, l, BRANCHED[e, T - 1] + 1))
                pool.sem_inc(waits_passed, 1)
                nc.gpsimd.tensor_scalar(half_mean[:], half_sum[:], EPS, None, ALU.add).then_inc(pool_link, 1)
                pool.wait_ge(pool_link, nth(pool_link, l, next(links)))
                pool.sem_inc(waits_passed, 1)

            def branch_root(l, links, e, t):
                r = STATS[e, t]
                pool.wait_ge(summed, nth(summed, l, r + 1))
                pool.sem_inc(waits_passed, 1)
                nc.gpsimd.tensor_tensor(meansq[:, r % 2], sumsq[:, r % 2], half_mean[:, t:t + 1], ALU.add).then_inc(pool_link, 1)
                pool.wait_ge(pool_link, nth(pool_link, l, next(links)))
                pool.sem_inc(waits_passed, 1)
                nc.gpsimd.tensor_tensor(rstd[:, r], meansq[:, r % 2], minus_half[:, 0:1], ALU.pow).then_inc(rooted, 1)

            def rotate(l, links, t):
                pool.wait_ge(emptied, nth(emptied, l, TILES_BEFORE["kc"] + t + 1))
                x12 = qkc[:, t].rearrange("p (h s e) -> p h s e", s=2, e=HALF)
                x1, x2 = x12[:, :, 0], x12[:, :, 1]
                a, b_, c = (rot[:, i].rearrange("p (h e) -> p h e", e=HALF) for i in range(3))
                cs = again(cos[:, t], 2 * NH)
                sn = again(sin[:, t], 2 * NH)
                nc.gpsimd.tensor_tensor(a, x1, cs, ALU.mult)
                nc.gpsimd.tensor_tensor(b_, x2, sn, ALU.mult)
                nc.gpsimd.tensor_tensor(c, x1, sn, ALU.mult)
                nc.gpsimd.tensor_tensor(x2, x2, cs, ALU.mult).then_inc(pool_link, 1)
                pool.wait_ge(pool_link, nth(pool_link, l, next(links)))
                nc.gpsimd.tensor_tensor(x1, a, b_, ALU.subtract)
                nc.gpsimd.tensor_tensor(x2, x2, c, ALU.add).then_inc(pool_link, 1)
                pool.wait_ge(pool_link, nth(pool_link, l, next(links)))
                every = qkc[:, t].rearrange("p (h e) -> p h e", e=HD)
                nc.gpsimd.tensor_tensor(every, every, spread(decay[:, t], HD),
                                        ALU.mult).then_inc(rotated, 1)

            with pool.Fori(0, DEPTH) as l:
                links = itertools.count(1)
                for t in range(T):
                    root(l, links, ("n1", t))
                pool.wait_ge(ln_var, nth(ln_var, l, 1))
                pool.sem_inc(waits_passed, 1)
                nc.gpsimd.tensor_scalar(ln_ve[:], ln_mv[:, :, 1], EPS, None, ALU.add).then_inc(pool_link, 1)
                pool.wait_ge(pool_link, nth(pool_link, l, next(links)))
                pool.sem_inc(waits_passed, 1)
                nc.gpsimd.tensor_tensor(ln_rstd[:], ln_ve[:], minus_half[:, 0:T], ALU.pow).then_inc(ln_root, 1)
                pool.wait_ge(ln_scaled, nth(ln_scaled, l, 1))
                pool.wait_ge(sgu_loaded, nth(sgu_loaded, l, 64))
                g4 = again(ln_gain[:], T)
                s4 = again(ln_shift[:], T)
                nc.gpsimd.tensor_tensor(vs[:], vs[:], g4, ALU.mult).then_inc(pool_link, 1)
                pool.wait_ge(pool_link, nth(pool_link, l, next(links)))
                pool.sem_inc(waits_passed, 1)
                nc.gpsimd.tensor_tensor(vs[:], vs[:], s4, ALU.add).then_inc(ln_done, 1)
                pool.wait_ge(trig_done, 2)
                pool.wait_ge(const_loaded, 16 * 3)
                for t in range(T):
                    rotate(l, links, t)
                for c in range(T):
                    pool.wait_ge(gn_var_done, nth(gn_var_done, l, c + 1))
                    pool.sem_inc(waits_passed, 1)
                    nc.gpsimd.tensor_scalar(gn_ve[:], gn_var[:], 1.0 / HD, EPS, ALU.mult, ALU.add).then_inc(pool_link, 1)
                    pool.wait_ge(pool_link, nth(pool_link, l, next(links)))
                    pool.sem_inc(waits_passed, 1)
                    nc.gpsimd.tensor_tensor(gn_rstd[:], gn_ve[:], minus_half[:, 0:NH], ALU.pow).then_inc(gn_root, 1)
                for t in range(MT):
                    root(l, links, ("mem", t))
                branch_halves(l, links, "e1")
                for t in range(T):
                    branch_root(l, links, "e1", t)
                for t in range(T):
                    root(l, links, ("n2", t))
                branch_halves(l, links, "e2")
                for what, t in N3_ACT:
                    if what == "e":
                        branch_root(l, links, "e2", t)
                    elif what == "x":
                        root(l, links, ("n3", t))
                pool.wait_ge(x_ready, nth(x_ready, l, BRANCHED["e2", T - 1] + 1))
                pool.sem_inc(waits_passed, 1)
                nc.gpsimd.memset(ys[:], 0.0).then_inc(y_zeroed, 1)
                branch_halves(l, links, "e3")
                for t in range(T):
                    branch_root(l, links, "e3", t)
                assert next(links) == POOL_LINKS + 1


NAMES = ["x", "mem", "positions", "norm_g", "w_in", "sgu_w", "sgu_b", "sgu_ln_g", "sgu_ln_b", "w_out",
         "x_wq", "x_wkv", "x_wo", "w_up", "w_down"]


def kernel(**inputs):
    import numpy as _np
    import concourse.bacc as _bacc
    from concourse import mybir as _mybir
    from concourse.bass_utils import run_bass_kernel_spmd as _run

    nc = _bacc.Bacc("TRN2", target_bir_lowering=False, num_devices=1)
    given = {name: _np.ascontiguousarray(inputs[name]) for name in NAMES} | shape_constants()
    given["positions"] = _np.ascontiguousarray(given["positions"].reshape(T, P).T)
    given["sgu_b"] = _np.ascontiguousarray(given["sgu_b"].transpose(0, 2, 1))
    arrays, args = {}, []
    for name, a in given.items():
        arrays[f"in_{name}_dram"] = a
        args.append(nc.dram_tensor(f"in_{name}_dram", a.shape, _mybir.dt.from_np(a.dtype), kind="ExternalInput").ap())
    args.append(nc.dram_tensor("out_dram", (1, S, D), _mybir.dt.float32, kind="ExternalOutput").ap())
    trunk(nc, *args)
    r = _run(nc, [arrays], core_ids=[0])
    return r.results[0]["out_dram"]
```

```python
import itertools
from contextlib import ExitStack

import concourse.bass as bass
import concourse.mybir as mybir
import numpy as np

F32 = mybir.dt.float32
F32R = mybir.dt.float32r
BF16 = mybir.dt.bfloat16
I32 = mybir.dt.int32
ALU = mybir.AluOpType
ACT = mybir.ActivationFunctionType
AX_X = mybir.AxisListType.X

P = 128
DEPTH, S, D, MEM = 2, 512, 1024, 256
HD = 64
NH = 6
PAIRS = NH // 2
G = 4
XH, XD = 4, 256
FF = 4 * D
AW, BW, CW = NH * HD, G * HD, NH * HD
PATTERNS = ((128, 1), (512, 4), (2048, 16))
EPS = 1e-6
ROPE_BASE = 10000.0
HALF = HD // 2
T = S // P
MT = MEM // P
KC = D // P
BK = 4
MASKED = -1e30

A0, U0, C0 = 0, 3 * AW, 3 * AW + 2 * BW
JOBS = [
    ("km0", "x_wkv", 0, 512, "feat", 4, MEM),
    ("km1", "x_wkv", 512, 512, "feat", 4, MEM),
    ("va", "w_in", A0 + 2 * AW, AW, "tok", T, AW),
    ("qa", "w_in", A0, AW, "feat", PAIRS, S),
    ("ka", "w_in", A0 + AW, AW, "feat", PAIRS, S),
    ("uv", "w_in", U0, 2 * BW, "tok", T, 2 * BW),
    ("qc", "w_in", C0, CW, "tok", T, CW),
    ("kc", "w_in", C0 + CW, CW, "tok", T, CW),
    ("vc", "w_in", C0 + 2 * CW, CW, "tok", T, CW),
    ("gc", "w_in", C0 + 3 * CW, CW, "tok", T, CW),
    ("out0", "w_out", 0, 512, "tok", T, 512),
    ("out1", "w_out", 512, 512, "tok", T, 512),
    ("vm0", "x_wkv", D, 512, "tok", MT, 512),
    ("vm1", "x_wkv", D + 512, 512, "tok", MT, 512),
    ("qx0", "x_wq", 0, 512, "feat", 4, S),
    ("qx1", "x_wq", 512, 512, "feat", 4, S),
    ("wo0", "x_wo", 0, 512, "tok", T, 512),
    ("wo1", "x_wo", 512, 512, "tok", T, 512),
]
KB = D // (BK * P)
FIRST_BLOCK = {j[0]: KB * i for i, j in enumerate(JOBS)}
HEAD_BLOCKS = KB * len(JOBS)
GROUPS = 4
GROUP_JOBS = ("up0", "up1", "dn0", "dn1")
GROUP_BLOCKS = KB * len(GROUP_JOBS)
BLOCKS = HEAD_BLOCKS + GROUPS * GROUP_BLOCKS
WSLOTS = 2
assert BLOCKS % WSLOTS == 0 and GROUP_BLOCKS % WSLOTS == 0 and FF == GROUPS * KB * BK * P

BRANCH_JOBS = ("out0", "out1", "wo0", "wo1")
TILES_BEFORE = {}
_n = 0
for _j in JOBS:
    TILES_BEFORE[_j[0]] = _n
    _n += 0 if _j[0] in BRANCH_JOBS else _j[5]
HEAD_TILES = _n
GROUP_TILES = 4 * KB * len(GROUP_JOBS)
UP_TILES = 8


def bank_users():
    last = [None] * 4
    users = {}
    for name, _, _, _, _, tiles, _ in JOBS:
        for t in range(tiles):
            users[name, t] = last[t]
            if name in BRANCH_JOBS:
                last[t] = (True, T * BRANCH_JOBS.index(name) + t)
            else:
                last[t] = (False, TILES_BEFORE[name] + t)
    return users
BANK_USER = bank_users()

def steps(text):
    return [(step[0], int(step[1])) for step in text.split()]


N3_ACT = steps("e0 e1 x0 x1 w0 h0 e2 h1 x2 e3 w1 x3 h2 h3")
N3_DVE = steps("e0 x0 e1 x1 n0 n1 w0 h0 h1 e2 x2 e3 x3 w1 n2 n3 h2 h3")


def stats_order():
    order = [("n1", t) for t in range(T)]
    order += [("e1", t) for t in range(T)] + [("n2", t) for t in range(T)]
    order += [("e2" if what == "e" else "n3", t) for what, t in N3_ACT if what in "ex"]
    return order + [("e3", t) for t in range(T)]
STATS = {k: i for i, k in enumerate(stats_order())}
NORMED = {k: i for i, k in enumerate([("n1", t) for t in range(T)] + [("memv", t) for t in range(MT)]
                                     + [("n2", t) for t in range(T)] + [("n3", t) for t in range(T)]
                                     + [("memk", t) for t in range(MT)])}
BRANCHED = {(e, t): T * i + t for i, e in enumerate(("e1", "e2", "e3")) for t in range(T)}
GAINED = {(e, half, t): 2 * T * i + T * half + t for i, e in enumerate(("e1", "e2", "e3"))
          for half in range(2) for t in range(T)}
TURNED = {k: i for i, k in enumerate(
    [("n1", t) for t in range(T)] + [("mix", t) for t in range(T)] + [("memv", t) for t in range(MT)]
    + [("n2", t) for t in range(T)] + [("n3", t) for t in range(T)] + [("memk", t) for t in range(MT)])}
PROLOGUE = -1

FILLED = {"n1": "km0", "n2": "vm0"}
MEMORY_JOBS = ("km0", "km1", "vm0", "vm1")


def fill_slots(tiles):
    return [(1, tiles // 2 - 1), (1, tiles - 1), (2, tiles - 1), (3, tiles // 2 - 1)]


FILL_SQUARES = {0: (0, 1), 1: (2,), 2: (3,)}
FILL_HI = {1: (0,), 2: (1,), 3: (2, 3)}

BLOCK_TILES = [j[5] for j in JOBS for _ in range(KB)] + [4] * (GROUPS * GROUP_BLOCKS)
LAYER_TILES = sum(BLOCK_TILES)


BY_BLOCK = [(kb, t) for kb in range(KB) for t in range(4)]
EARLY_PAIR = [(0, 0), (0, 1), (1, 0), (1, 1), (0, 2), (0, 3), (1, 2), (1, 3)]


def done(b, t=None):
    if b < 0:
        return -sum(BLOCK_TILES[b + 1:]) if b < -1 else 0
    first = FIRST_BLOCK["wo1"]
    if first <= b < first + KB:
        return sum(BLOCK_TILES[:first]) + EARLY_PAIR.index((b - first, T - 1 if t is None else t)) + 1
    return sum(BLOCK_TILES[:b]) + (BLOCK_TILES[b] if t is None else t + 1)


UNITS = T * NH
STEP_BLOCK = FIRST_BLOCK["uv"]
XUNITS = XH // 2 * T


def unit_step(b, t):
    j = (b - STEP_BLOCK) * T + t
    pause = (FIRST_BLOCK["qc"] - STEP_BLOCK) * T
    if j < 0 or pause <= j < pause + 2:
        return -1
    return j if j < pause else j - 2


DVE_LINKS = 37
POOL_LINKS = 41

GAIN = {"n1": 0, "e1": 1, "n2": 2, "e2": 3, "n3": 4, "e3": 5, "mem": 6}
GAIN_SLOT = {"n1": 0, "mem": 1, "n2": 0, "n3": 1, "e1": 2, "e2": 2, "e3": 2}


def shape_constants():
    i = np.arange(S)[:, None]
    j = np.arange(S)[None, :]
    count = np.zeros((S, S))
    for window, dilation in PATTERNS:
        count += (i >= j) & ((i - j) % dilation == 0) & (i - j <= window)
    logs = np.where(count > 0, np.log(np.maximum(count, 1)), MASKED).astype(np.float32)
    log_count = np.ascontiguousarray(logs[(T - 1) * P:])
    a = np.arange(P)
    upper = (a[:, None] <= a[None, :]).astype(np.float32)
    gamma = 1.0 - 2.0 ** (-5.0 - np.arange(NH))
    pos = np.arange(S, dtype=np.float64).reshape(T, P).T[:, :, None]
    decay = np.concatenate([gamma ** (pos + 1.0), gamma ** -(pos + 1.0) * HD ** -0.5], axis=2)
    inv = 1.0 / (np.float32(ROPE_BASE) ** np.linspace(0.0, 1.0, HALF, dtype=np.float32))
    return {
        "c_ident": np.eye(P, dtype=np.float32),
        "c_logcount": log_count,
        "c_upper": upper,
        "c_decay": decay.astype(np.float32),
        "c_inv": np.tile(inv.astype(np.float32)[None, :], (P, 1)),
    }


TURN = 2.0 * np.pi


def turn_pieces():
    pieces, left = [], TURN
    for _ in range(4):
        unit = 2.0 ** (np.floor(np.log2(left)) - 7)
        pieces.append(float(np.floor(left / unit) * unit))
        left -= pieces[-1]
    return pieces


TURN_PIECES = turn_pieces()
ARENA_KIB = 56


def spread(ap, n):
    return ap.rearrange("p (a b) -> p a b", b=1).broadcast_to([ap.shape[0], ap.shape[1], n])


def again(ap, n):
    return ap.rearrange("p (b a) -> p b a", b=1).broadcast_to([ap.shape[0], n, ap.shape[1]])


def trunk(nc, x, mem, positions, norm_g, w_in, sgu_w, sgu_b, sgu_ln_g, sgu_ln_b, w_out,
          x_wq, x_wkv, x_wo, w_up, w_down, c_ident, c_logcount, c_upper, c_decay, c_inv, out):
    weights = {"w_in": w_in, "w_out": w_out, "x_wq": x_wq, "x_wkv": x_wkv, "x_wo": x_wo}
    with ExitStack() as ctx:
        def sb(name, shape, dt=F32):
            return ctx.enter_context(nc.sbuf_tensor(name, shape, dt))

        xs = sb("xs", [P, T, D])
        hT_hi = sb("hT_hi", [P, KC, S], F32R)
        hT_lo = sb("hT_lo", [P, KC, S], F32R)
        w_raw = sb("w_raw", [P, WSLOTS, BK, 512])
        w_hi = sb("w_hi", [P, WSLOTS, BK, 512], F32R)
        w_lo = sb("w_lo", [P, WSLOTS, BK, 512], F32R)
        ys = sb("ys", [P, T, D])
        gains = sb("gains", [P, 3, D])
        hs_start = nc.sbuf_base
        hs = sb("hs", [P, 2, D])
        squares = sb("squares", [P, 2, D], BF16)
        ident = sb("ident", [P, P])
        log_count = sb("log_count", [P, S])
        upper = sb("upper", [P, P])
        decay = sb("decay", [P, T, 2 * NH])
        inv = sb("inv", [P, HALF])
        cos = sb("cos", [P, T, HALF])
        sin = sb("sin", [P, T, HALF])
        angle = sb("angle", [P, T, HALF])
        turns = sb("turns", [P, T, HALF])
        pos_i = sb("pos_i", [P, T], I32)
        pos_f = sb("pos_f", [P, T])
        minus_half = sb("minus_half", [P, 8])
        sumsq = sb("sumsq", [P, 2, 1])
        mem_sumsq = sb("mem_sumsq", [P, MT])
        mem_meansq = sb("mem_meansq", [P, MT])
        mem_rstd = sb("mem_rstd", [P, MT])
        meansq = sb("meansq", [P, 2, 1])
        rstd = sb("rstd", [P, len(STATS), 1])
        half_sum = sb("half_sum", [P, T])
        half_mean = sb("half_mean", [P, T])
        sgu_raw = sb("sgu_raw", [P, G, P])
        sgu_T = sb("sgu_T", [P, G, P])
        sgu_bias = sb("sgu_bias", [P, G])
        ln_gain = sb("ln_gain", [P, BW])
        ln_shift = sb("ln_shift", [P, BW])
        ln_stats = sb("ln_stats", [P, T, 6])
        ln_mv = sb("ln_mv", [P, T, 2])
        ln_ve = sb("ln_ve", [P, T])
        ln_rstd = sb("ln_rstd", [P, T])
        neg_max = sb("neg_max", [P, 2, 2])
        den = sb("den", [P, UNITS])
        rden = sb("rden", [P, UNITS])
        x_den = sb("x_den", [P, XUNITS, 2])
        x_rden = sb("x_rden", [P, XUNITS, 2])
        state = sb("state", [P, 2, PAIRS, P])
        x_neg = sb("x_neg", [P, 2, 2])
        x_top = sb("x_top", [P, 2, 2])
        exp_table = sb("exp_table", [P, 1])
        gn_sum = sb("gn_sum", [P, NH])
        gn_mean = sb("gn_mean", [P, NH])
        gn_var = sb("gn_var", [P, NH])
        gn_ve = sb("gn_ve", [P, NH])
        gn_rstd = sb("gn_rstd", [P, NH])

        KIB = 1024
        arena_start = -(-nc.sbuf_base // 32) * 32
        ctx.enter_context(nc.sbuf_tensor("arena", [P, ARENA_KIB * KIB // 4], F32))

        def part(name, kib, shape, dt=F32):
            return nc.alloc_sbuf_tensor_at(name, shape, dt, offset=arena_start + int(kib * KIB))

        qaT = part("qaT", 0, [P, PAIRS, S])
        kaT = part("kaT", 6, [P, PAIRS, S])
        va = part("va", 12, [P, T, AW])
        vs = part("vs", 18, [P, T, BW])
        qkc = part("qkc", 22, [P, T, 2 * CW])
        vc = part("vc", 34, [P, T, CW])
        probs = part("probs", 40, [P, 2, S])
        probsT = part("probsT", 44, [P, 2, S])
        rot = nc.alloc_sbuf_tensor_at("rot", [P, 3, 2 * NH * HALF], F32, offset=hs_start)
        qkT = part("qkT", 0, [P, 2, CW])
        innerT = part("innerT", 3, [P, NH, P])
        yc = part("yc", 6, [P, T, CW])
        yc2 = part("yc2", 12, [P, CW])
        kmT = part("kmT", 48, [P, KC, MEM])
        vm = part("vm", 8, [P, MT, D])
        x_probs = part("x_probs", 16, [P, 2, 512])
        x_probsT = part("x_probsT", 20, [P, 2, 512])
        memT_hi = part("memT_hi", 32, [P, KC, MEM], F32R)
        memT_lo = part("memT_lo", 40, [P, KC, MEM], F32R)
        qxT = part("qxT", 24, [P, KC, S])
        half_squares = {"e1": part("half_squares", 16, [P, T, 512], BF16),
                        "e3": part("half_squares3", 48, [P, T, 512], BF16)}
        half_squares["e2"] = half_squares["e1"]
        uT_hi = part("uT_hi", 0, [P, KC, S], F32R)
        uT_lo = part("uT_lo", 16, [P, KC, S], F32R)
        relu = part("relu", 32, [P, 2, S])

        proj = ctx.enter_context(nc.psum_tensor("proj", [P, 4, 512], F32))
        work = ctx.enter_context(nc.psum_tensor("work", [P, 4, 512], F32))

        per_layer, start_of = {}, {}

        def counted(name, per, start=0):
            sem = ctx.enter_context(nc.semaphore(name))
            per_layer[sem.name], start_of[sem.name] = per, start
            return sem

        def nth(sem, l, n):
            return l * per_layer[sem.name] + (n + start_of[sem.name])

        waits_passed = ctx.enter_context(nc.semaphore("waits_passed"))
        first_loaded = ctx.enter_context(nc.semaphore("first_loaded"))
        const_loaded = ctx.enter_context(nc.semaphore("const_loaded"))
        x_loaded = [ctx.enter_context(nc.semaphore(f"x_loaded{t}")) for t in range(T)]
        setup_done = ctx.enter_context(nc.semaphore("setup_done"))
        dve_setup = ctx.enter_context(nc.semaphore("dve_setup"))
        trig_done = ctx.enter_context(nc.semaphore("trig_done"))
        stored = ctx.enter_context(nc.semaphore("stored"))
        w_loaded = [counted(f"w_loaded{i}", 16 * BLOCKS // WSLOTS) for i in range(WSLOTS)]
        w_hi_done = counted("w_hi_done", BLOCKS)
        w_lo_done = counted("w_lo_done", BLOCKS, WSLOTS)
        gain_loaded = {k: counted(f"gain_{k}", 16, 16 if k == "mem" else 0) for k in GAIN}
        sgu_loaded = counted("sgu_loaded", 64)
        mem_loaded = counted("mem_loaded", 32 * MT, 16 * MT)
        mem_summed = ctx.enter_context(nc.semaphore("mem_summed"))
        mem_rooted = ctx.enter_context(nc.semaphore("mem_rooted"))
        tile_done = counted("tile_done", LAYER_TILES, 4 * WSLOTS)
        emptied = counted("emptied", HEAD_TILES + GROUPS * UP_TILES, 1)
        added = counted("added", GROUPS * UP_TILES, T)
        summed = counted("summed", len(STATS))
        rooted = counted("rooted", len(STATS), 2)
        normed = counted("normed", len(NORMED), MT)
        half_summed = counted("half_summed", len(BRANCHED))
        gained = counted("gained", len(GAINED), 1)
        x_ready = counted("x_ready", len(BRANCHED), T)
        turned = counted("turned", 2 * len(TURNED), 2 * MT)
        turned_hi = counted("turned_hi", 2 * len(TURNED), 2 * MT)
        turned_lo = counted("turned_lo", 2 * len(TURNED), 2 * MT)
        y_zeroed = counted("y_zeroed", 1)
        hidden_sq = counted("hidden_sq", GROUPS * UP_TILES, 1)
        hidden_hi = counted("hidden_hi", GROUPS * UP_TILES, 1)
        hidden_lo = counted("hidden_lo", GROUPS * UP_TILES, 2)
        sgu_turned = counted("sgu_turned", 1)
        sgu_ready = counted("sgu_ready", 1, 1)
        gelu_done = counted("gelu_done", 1)
        ln_var = counted("ln_var", 1)
        ln_root = counted("ln_root", 1)
        ln_scaled = counted("ln_scaled", 1)
        ln_done = counted("ln_done", 1)
        gated = counted("gated", 2)
        gate_out = counted("gate_out", 1)
        scored = counted("scored", UNITS)
        masked = counted("masked", UNITS, 2)
        exped = counted("exped", UNITS)
        p_turned = counted("p_turned", UNITS, 2)
        p_copied = counted("p_copied", UNITS, 1)
        weighed = counted("weighed", UNITS, 2)
        a_out = counted("a_out", T, 1)
        rotated = counted("rotated", T)
        c_turned = counted("c_turned", T)
        c_copied = counted("c_copied", T, 1)
        c_inner = counted("c_inner", T)
        c_masked = counted("c_masked", T, 1)
        c_kv = counted("c_kv", T - 1)
        c_state = counted("c_state", T - 1, 1)
        c_y = counted("c_y", T)
        c_centred = counted("c_centred", T, 1)
        gn_var_done = counted("gn_var_done", T)
        gn_root = counted("gn_root", T)
        c_out = counted("c_out", T)
        x_scored = counted("x_scored", XUNITS)
        x_max = counted("x_max", XUNITS, 1)
        x_exped = counted("x_exped", XUNITS, 2)
        x_normed = counted("x_normed", XUNITS)
        x_turned = counted("x_turned", XUNITS, 2)
        x_copied = counted("x_copied", XUNITS, 1)
        x_weighed = counted("x_weighed", XUNITS, 2)
        x_hi = counted("x_hi", XUNITS)
        x_lo = counted("x_lo", XUNITS, 1)
        dve_link = counted("dve_link", DVE_LINKS)
        pool_link = counted("pool_link", POOL_LINKS)

        def values(eng, *counts):
            return [eng.snap(count) for count in counts]

        def start_counts(eng, *sems):
            for sem in sems:
                eng.sem_inc(sem, start_of[sem.name])

        block = ctx.enter_context(nc.Block())

        @block.sync
        def _(sp):
            def load_block(l, b, src):
                cols = src.shape[-1]
                if l is not PROLOGUE:
                    sp.wait_ge(w_lo_done, nth(w_lo_done, l, b - WSLOTS + 1))
                    sp.sem_inc(waits_passed, 1)
                sp.dma_start(w_raw[:, b % WSLOTS, :, 0:cols],
                             src.rearrange("a (k p) c -> p (a k) c", p=P)).then_inc(w_loaded[b % WSLOTS], 16)

            def load_gain(l, k):
                sp.dma_start(gains[:, GAIN_SLOT[k]],
                             norm_g[bass.ds(l, 1), GAIN[k]].broadcast_to([P, D])).then_inc(gain_loaded[k], 16)

            for dst, src in ((pos_i, positions), (inv, c_inv)):
                sp.dma_start(dst[:], src).then_inc(first_loaded, 16)
            for t in range(MT):
                sp.dma_start(hs[:, t], mem[0, t * P:(t + 1) * P]).then_inc(mem_loaded, 16)
            load_gain(0, "mem")
            load_block(PROLOGUE, BLOCKS, x_wkv[0:1, 0:BK * P, 0:512])
            sp.dma_start(xs[:, 0], x[0, 0:P]).then_inc(x_loaded[0], 16)

            with sp.Fori(0, DEPTH) as l:
                sp.wait_ge(normed, nth(normed, l, 0))
                sp.sem_inc(waits_passed, 1)
                load_gain(l, "n1")
                for name, weight, c, cols, _, _, _ in JOBS:
                    for kb in range(KB):
                        b = FIRST_BLOCK[name] + kb
                        if b > 0:
                            load_block(l, b, weights[weight][bass.ds(l, 1), kb * BK * P:(kb + 1) * BK * P, c:c + cols])
                    if name == "va":
                        sp.wait_ge(normed, nth(normed, l, 0))
                        sp.dma_start(sgu_raw[:], sgu_w[bass.ds(l, 1)].rearrange("a g i j -> i (a g) j")).then_inc(sgu_loaded, 16)
                        sp.dma_start(sgu_bias[:], sgu_b[bass.ds(l, 1)].rearrange("a i g -> i (a g)")).then_inc(sgu_loaded, 16)
                        sp.dma_start(ln_gain[:], sgu_ln_g[bass.ds(l, 1)].broadcast_to([P, BW])).then_inc(sgu_loaded, 16)
                        sp.dma_start(ln_shift[:], sgu_ln_b[bass.ds(l, 1)].broadcast_to([P, BW])).then_inc(sgu_loaded, 16)
                    if name == "kc":
                        sp.wait_ge(gained, nth(gained, l, 0))
                        sp.sem_inc(waits_passed, 1)
                        load_gain(l, "e1")
                        sp.wait_ge(normed, nth(normed, l, NORMED["n1", T - 1] + 1))
                        sp.sem_inc(waits_passed, 1)
                        load_gain(l, "n2")
                    if name == "gc":
                        sp.wait_ge(rotated, nth(rotated, l, T))
                        for t in range(MT):
                            sp.dma_start(hs[:, t], mem[0, t * P:(t + 1) * P]).then_inc(mem_loaded, 16)
                    if name == "qx0":
                        sp.wait_ge(normed, nth(normed, l, NORMED["memv", MT - 1] + 1))
                        sp.sem_inc(waits_passed, 1)
                        load_gain(l, "n3")
                        sp.wait_ge(gained, nth(gained, l, GAINED["e1", 1, T - 1] + 1))
                        sp.sem_inc(waits_passed, 1)
                        load_gain(l, "e2")
                with sp.Fori(0, GROUPS) as g:
                    for j in range(2):
                        for kb in range(KB):
                            b = HEAD_BLOCKS + KB * j + kb
                            sp.wait_ge(w_lo_done, nth(w_lo_done, l, g * GROUP_BLOCKS + (b - WSLOTS + 1)))
                            sp.sem_inc(waits_passed, 1)
                            sp.dma_start(w_raw[:, b % WSLOTS],
                                         w_up[bass.ds(l, 1), kb * BK * P:(kb + 1) * BK * P,
                                              bass.ds(g * (FF // GROUPS) + j * 512, 512)]
                                         .rearrange("a (k p) c -> p (a k) c", p=P)).then_inc(w_loaded[b % WSLOTS], 16)
                    for j in range(2):
                        for kb in range(KB):
                            b = HEAD_BLOCKS + KB * (2 + j) + kb
                            sp.wait_ge(w_lo_done, nth(w_lo_done, l, g * GROUP_BLOCKS + (b - WSLOTS + 1)))
                            sp.sem_inc(waits_passed, 1)
                            sp.dma_start(w_raw[:, b % WSLOTS],
                                         w_down[bass.ds(l, 1), bass.ds(g * (FF // GROUPS) + kb * BK * P, BK * P),
                                                j * 512:(j + 1) * 512]
                                         .rearrange("a (k p) c -> p (a k) c", p=P)).then_inc(w_loaded[b % WSLOTS], 16)
                sp.wait_ge(gained, nth(gained, l, GAINED["e2", 1, T - 1] + 1))
                sp.sem_inc(waits_passed, 1)
                load_gain(l, "e3")
                load_block(l, BLOCKS, x_wkv[DEPTH - 1:DEPTH, 0:BK * P, 0:512])
            for t in range(T):
                sp.wait_ge(x_ready, nth(x_ready, DEPTH - 1, BRANCHED["e3", t] + 1))
                sp.dma_start(out[0, t * P:(t + 1) * P], xs[:, t]).then_inc(stored, 16)
            sp.wait_ge(stored, 16 * T)

        @block.tensor
        def _(pe):
            start_counts(pe, tile_done, p_turned, weighed, x_turned, x_weighed)
            pe.wait_ge(first_loaded, 16 * 3)

            def three_passes(dst, l_hi, l_lo, r_hi, r_lo, first, last):
                nc.tensor.matmul(dst, l_hi, r_hi, start=first, stop=False)
                nc.tensor.matmul(dst, l_hi, r_lo, start=False, stop=False)
                return nc.tensor.matmul(dst, l_lo, r_hi, start=False, stop=last)

            def block_tile(b_slot, kb, mode, t, moving, hi, lo, cols, at=0):
                for k in range(BK):
                    c = kb * BK + k
                    first, last = c == 0, kb == KB - 1 and k == BK - 1
                    if mode == "tok":
                        r = slice(t * P, (t + 1) * P)
                        mm = three_passes(proj[:, t, 0:moving], hi[:, c, r], lo[:, c, r],
                                          w_hi[:, b_slot, k, 0:cols], w_lo[:, b_slot, k, 0:cols], first, last)
                    else:
                        r = slice(t * P, (t + 1) * P)
                        tokens = slice(at, at + moving)
                        mm = three_passes(proj[:, t, tokens], w_hi[:, b_slot, k, r], w_lo[:, b_slot, k, r],
                                          hi[:, c, tokens], lo[:, c, tokens], first, last)
                return mm

            def turn(l, key, src):
                n = TURNED[key]
                if l is not PROLOGUE:
                    pe.wait_ge(turned_lo, nth(turned_lo, l, 2 * n - 2))
                for half in range(2):
                    for k in range(BK):
                        c = half * BK + k
                        mm = nc.tensor.transpose(work[:, 2 * (n % 2) + half, k * P:(k + 1) * P],
                                                 src[:, c * P:(c + 1) * P], ident[:])
                    mm.then_inc(turned, 1)

            def turned_in(l, key):
                pe.wait_ge(turned_lo, nth(turned_lo, l, 2 * TURNED[key] + 2))
                pe.sem_inc(waits_passed, 1)

            def a_scores(l, u):
                t, h = divmod(u, NH)
                lo, n = HD * (h % 2), (t + 1) * P
                if u == 0:
                    pe.wait_ge(emptied, nth(emptied, l, TILES_BEFORE["uv"]))
                    pe.wait_ge(turned_lo, nth(turned_lo, l, 2 * TURNED["n1", T - 1] + 2))
                    pe.wait_ge(sgu_ready, nth(sgu_ready, l, 1))
                pe.wait_ge(masked, nth(masked, l, u - 1))
                nc.tensor.matmul(work[:, u % 2, 0:n], qaT[lo:lo + HD, h // 2, t * P:(t + 1) * P],
                                 kaT[lo:lo + HD, h // 2, 0:n], start=True, stop=True).then_inc(scored, 1)

            def a_turn(l, u):
                pe.wait_ge(exped, nth(exped, l, u + 1))
                pe.wait_ge(p_copied, nth(p_copied, l, u))
                for j in range(u // NH + 1):
                    mm = nc.tensor.transpose(work[:, 2, j * P:(j + 1) * P], probs[:, u % 2, j * P:(j + 1) * P], ident[:])
                mm.then_inc(p_turned, 1)

            def a_weigh(l, u):
                t, h = divmod(u, NH)
                pe.wait_ge(p_copied, nth(p_copied, l, u + 1))
                pe.wait_ge(a_out, nth(a_out, l, t))
                for j in range(t + 1):
                    mm = nc.tensor.matmul(work[:, 3, h * HD:(h + 1) * HD], probsT[:, u % 2, j * P:(j + 1) * P],
                                          va[:, j, h * HD:(h + 1) * HD], start=(j == 0), stop=(j == t))
                mm.then_inc(weighed, 1)

            def a_step(l, j):
                if j < UNITS:
                    a_scores(l, j)
                if 1 <= j <= UNITS:
                    a_turn(l, j - 1)
                if 2 <= j < UNITS + 2:
                    a_weigh(l, j - 2)

            def sgu_weights(l):
                pe.wait_ge(sgu_loaded, nth(sgu_loaded, l, 64))
                pe.wait_ge(turned_lo, nth(turned_lo, l, 2 * TURNED["n1", T - 1] + 2))
                for g in range(G):
                    mm = nc.tensor.transpose(work[:, 0, g * P:(g + 1) * P], sgu_raw[:, g], ident[:])
                mm.then_inc(sgu_turned, 1)

            def sgu_mix(l):
                pe.wait_ge(ln_done, nth(ln_done, l, 1))
                pe.wait_ge(masked, nth(masked, l, UNITS))
                for g in range(G):
                    mm = nc.tensor.matmul(work[:, g // 2, (g % 2) * 256:(g % 2 + 1) * 256].rearrange("p (t c) -> p t c", t=T),
                                          sgu_T[:, g], vs[:, :, g * HD:(g + 1) * HD], start=True, stop=True)
                    if g % 2:
                        mm.then_inc(gated, 1)

            def c_turn(l, c):
                if c == 0:
                    pe.wait_ge(gate_out, nth(gate_out, l, 1))
                    pe.wait_ge(a_out, nth(a_out, l, T))
                pe.wait_ge(rotated, nth(rotated, l, c + 1))
                pe.wait_ge(c_copied, nth(c_copied, l, c))
                pe.wait_ge(c_state, nth(c_state, l, c))
                for i in range(2):
                    for p in range(PAIRS):
                        mm = nc.tensor.transpose(work[:, i, p * P:(p + 1) * P],
                                                 qkc[:, c, i * CW + p * P:i * CW + (p + 1) * P], ident[:])
                mm.then_inc(c_turned, 1)

            def c_products(l, c):
                pe.wait_ge(c_copied, nth(c_copied, l, c + 1))
                pe.wait_ge(c_masked, nth(c_masked, l, c))
                pe.wait_ge(c_centred, nth(c_centred, l, c))
                for h in range(NH):
                    lo, p = HD * (h % 2), h // 2
                    mm = nc.tensor.matmul(work[:, 2 + h % 2, p * P:(p + 1) * P],
                                          qkT[lo:lo + HD, 1, p * P:(p + 1) * P],
                                          qkT[lo:lo + HD, 0, p * P:(p + 1) * P], start=True, stop=True)
                mm.then_inc(c_inner, 1)
                pe.wait_ge(emptied, nth(emptied, l, TILES_BEFORE["vc"] + c + 1))
                if c == T - 1:
                    return
                for p in range(PAIRS):
                    mm = nc.tensor.matmul(work[:, 0, p * P:(p + 1) * P], qkc[:, c, CW + p * P:CW + (p + 1) * P],
                                          vc[:, c, p * P:(p + 1) * P], start=True, stop=True)
                mm.then_inc(c_kv, 1)

            def c_read(l, c):
                pe.wait_ge(c_masked, nth(c_masked, l, c + 1))
                pe.wait_ge(c_state, nth(c_state, l, c))
                for p in range(PAIRS):
                    if c > 0:
                        nc.tensor.matmul(work[:, 2, p * P:(p + 1) * P], qkT[:, 0, p * P:(p + 1) * P], state[:, c % 2, p],
                                         start=True, stop=False, skip_group_check=True)
                    for h in (2 * p, 2 * p + 1):
                        mm = nc.tensor.matmul(work[:, 2, h * HD:(h + 1) * HD], innerT[:, h], vc[:, c, h * HD:(h + 1) * HD],
                                              start=(c == 0), stop=True, skip_group_check=True)
                mm.then_inc(c_y, 1)

            def c_slot(l, k):
                if k % 2 == 0:
                    if k >= 2:
                        c_read(l, k // 2 - 1)
                    if k < 2 * T:
                        c_turn(l, k // 2)
                elif k < 2 * T:
                    c_products(l, k // 2)

            def x_scores(l, u):
                pair, t = divmod(u, T)
                if u == 0:
                    pe.wait_ge(turned_lo, nth(turned_lo, l, 2 * TURNED["n2", T - 1] + 2))
                pe.wait_ge(emptied, nth(emptied, l, TILES_BEFORE["qx1" if pair == 0 else "wo0"]))
                pe.wait_ge(x_exped, nth(x_exped, l, u - 1))
                for i in range(2):
                    for k in range(2):
                        c = 2 * (2 * pair + i) + k
                        mm = nc.tensor.matmul(work[:, u % 2, i * MEM:(i + 1) * MEM], qxT[:, c, t * P:(t + 1) * P],
                                              kmT[:, c, :], start=(k == 0), stop=(k == 1))
                mm.then_inc(x_scored, 1)

            def x_turn(l, u):
                pe.wait_ge(x_normed, nth(x_normed, l, u + 1))
                pe.wait_ge(x_copied, nth(x_copied, l, u))
                for j in range(2 * MT):
                    mm = nc.tensor.transpose(work[:, 2, j * P:(j + 1) * P], x_probs[:, u % 2, j * P:(j + 1) * P], ident[:])
                mm.then_inc(x_turned, 1)

            def x_weigh(l, u):
                pair = u // T
                pe.wait_ge(x_copied, nth(x_copied, l, u + 1))
                pe.wait_ge(x_lo, nth(x_lo, l, u))
                pe.wait_ge(emptied, nth(emptied, l, TILES_BEFORE["qx0"]))
                for k in range(BK):
                    i = k * P // XD
                    for j in range(MT):
                        mm = nc.tensor.matmul(work[:, 3, k * P:(k + 1) * P], vm[:, j, (pair * BK + k) * P:(pair * BK + k + 1) * P],
                                              x_probsT[:, u % 2, (i * MT + j) * P:(i * MT + j + 1) * P],
                                              start=(j == 0), stop=(j == MT - 1))
                mm.then_inc(x_weighed, 1)

            def x_step(l, j):
                if j < XUNITS:
                    x_scores(l, j)
                if 2 <= j < XUNITS + 2:
                    x_weigh(l, j - 2)
                if 1 <= j <= XUNITS:
                    x_turn(l, j - 1)

            def before_tile(l, b, t):
                if b == FIRST_BLOCK["va"]:
                    turned_in(l, ("n1", t))
                if b == FIRST_BLOCK["out0"]:
                    turned_in(l, ("mix", t))
                if b in (FIRST_BLOCK["wo0"], FIRST_BLOCK["wo0"] + 1):
                    pe.wait_ge(x_lo, nth(x_lo, l, (b - FIRST_BLOCK["wo0"]) * T + t + 1))
                    pe.sem_inc(waits_passed, 1)

            def turn_normed(l, phase, t):
                pe.wait_ge(normed, nth(normed, l, NORMED[phase, t] + 1))
                turn(l, (phase, t), hs[:, t % 2])

            def turn_mix(l, t):
                pe.wait_ge(c_out, nth(c_out, l, t + 1))
                if t == 1:
                    pe.wait_ge(c_centred, nth(c_centred, l, T))
                turn(l, ("mix", t), ys[:, t])

            def after_tile(l, b, t):
                if b == FIRST_BLOCK["ka"] + 1 and t == 0:
                    sgu_weights(l)
                j = unit_step(b, t)
                if 0 <= j < UNITS + 2:
                    a_step(l, j)
                if j == UNITS + 2:
                    sgu_mix(l)
                k = (b - FIRST_BLOCK["gc"]) * T + t + 2
                if 0 <= k <= 2 * T:
                    c_slot(l, k)
                if b == FIRST_BLOCK["out0"] - 1 and t >= T - 2:
                    turn_mix(l, t - T + 2)
                if b == FIRST_BLOCK["wo1"] and t == 3:
                    turn_normed(l, "n3", 0)
                if b == FIRST_BLOCK["wo1"] + 1 and t == 2:
                    turn_normed(l, "n3", 1)
                if b == FIRST_BLOCK["out0"] and t < T - 2:
                    turn_mix(l, t + 2)
                if b == FIRST_BLOCK["out0"] + 1 and t < MT:
                    turn_normed(l, "memv", t)
                for phase, fill in FILLED.items():
                    slot, slots = (b - FIRST_BLOCK[fill], t), fill_slots(JOBS[b // KB][5])
                    if slot in slots:
                        turn_normed(l, phase, slots.index(slot))
                if b == FIRST_BLOCK["qx1"] + 1 and t % 2:
                    x_step(l, t // 2)
                if b == FIRST_BLOCK["wo0"]:
                    x_step(l, XUNITS - 2 + t)

            def after_block(l, b):
                if b == FIRST_BLOCK["qx1"] + 1:
                    for j in range(2, XUNITS - 2):
                        x_step(l, j)

            def first_up(l):
                late_slots = ((1, 0), (1, 1))
                for half in range(2):
                    turned_in(l, ("n3", 2 * half + 1))
                    for kb in range(KB):
                        b = HEAD_BLOCKS + kb
                        if half == 0:
                            pe.wait_ge(w_lo_done, nth(w_lo_done, l, b + 1))
                        for t in range(4):
                            if half == 0 and kb == 0:
                                pe.wait_ge(gained, nth(gained, l, GAINED["e2", 1, t] + 1))
                            mm = block_tile(b % WSLOTS, kb, "feat", t, S // 2, hT_hi, hT_lo, 512, at=half * (S // 2))
                            if half:
                                mm.then_inc(tile_done, 1)
                            if half == 0 and (kb, t) in late_slots:
                                turn_normed(l, "n3", 2 + late_slots.index((kb, t)))

            def mlp_group(l, g, jobs=GROUP_JOBS, last=False):
                for name in jobs:
                    i = GROUP_JOBS.index(name)
                    for kb in range(KB):
                        b = HEAD_BLOCKS + KB * i + kb
                        pe.wait_ge(w_lo_done, nth(w_lo_done, l, g * GROUP_BLOCKS + (b + 1)))
                        for t in range(4):
                            if kb == 0:
                                if name == "up0":
                                    pe.wait_ge(added, nth(added, l, g * UP_TILES + (t + 1 - T)))
                                elif name in ("up1", "dn0"):
                                    pe.wait_ge(emptied, nth(emptied, l, g * UP_TILES + (HEAD_TILES + 4 * (i - 1) + t + 1)))
                                else:
                                    pe.wait_ge(added, nth(added, l, g * UP_TILES + (t + 1)))
                            if name == "dn0" and t == 0:
                                pe.wait_ge(hidden_lo, nth(hidden_lo, l, g * UP_TILES + 4 * (kb + 1)))
                            if i < 2:
                                mm = block_tile(b % WSLOTS, kb, "feat", t, S, hT_hi, hT_lo, 512)
                            else:
                                mm = block_tile(b % WSLOTS, kb, "tok", t, 512, uT_hi, uT_lo, 512)
                            mm.then_inc(tile_done, 1)
                            if last and name == "dn0" and kb == 1 and t < MT:
                                turn_normed(l, "memk", t)

            for t in range(MT):
                turn_normed(PROLOGUE, "memk", t)
            with pe.Fori(0, DEPTH) as l:
                for name, _, _, cols, mode, tiles, moving in JOBS:
                    if name == "km0":
                        pe.wait_ge(turned_lo, nth(turned_lo, l, 0))
                        pe.sem_inc(waits_passed, 1)
                    if name == "vm0":
                        turned_in(l, ("memv", MT - 1))
                    if name == "qx0":
                        turned_in(l, ("n2", T - 1))
                    hi, lo = (memT_hi, memT_lo) if name in MEMORY_JOBS else (hT_hi, hT_lo)
                    for kb, t in EARLY_PAIR if name == "wo1" else BY_BLOCK:
                        b = FIRST_BLOCK[name] + kb
                        if t < tiles:
                            before_tile(l, b, t)
                            if t == 0:
                                pe.wait_ge(w_lo_done, nth(w_lo_done, l, b + 1))
                            if kb == 0:
                                user = BANK_USER[name, t]
                                if user is None:
                                    pe.wait_ge(added, nth(added, l, t + 1 - T))
                                elif user[0]:
                                    pe.wait_ge(gained, nth(gained, l, user[1] + 1))
                                else:
                                    pe.wait_ge(emptied, nth(emptied, l, user[1] + 1))
                            mm = block_tile(b % WSLOTS, kb, mode, t, moving, hi, lo, cols)
                            mm.then_inc(tile_done, 1)
                            after_tile(l, b, t)
                        if t == tiles - 1:
                            after_block(l, b)
                first_up(l)
                mlp_group(l, 0, GROUP_JOBS[1:])
                with pe.Fori(1, GROUPS - 1) as g:
                    mlp_group(l, g)
                mlp_group(l, GROUPS - 1, last=True)

        @block.scalar
        def _(act):
            start_counts(act, emptied, hidden_hi, p_copied, c_copied, x_exped, x_copied)
            act.dma_start(ident[:], c_ident).then_inc(first_loaded, 16)
            act.wait_ge(trig_done, 1)
            nc.scalar.activation(sin[:], angle[:], ACT.Sin)
            nc.scalar.activation(cos[:], turns[:], ACT.Sin).then_inc(trig_done, 1)
            nc.scalar.activation(exp_table[:], inv[:, 0:1], ACT.Exp)

            def split_hi(l, b, cols=512, g=0):
                slot = b % WSLOTS
                act.wait_ge(w_loaded[slot], nth(w_loaded[slot], l, g * (16 * GROUP_BLOCKS // WSLOTS) + 16 * (b // WSLOTS + 1)))
                if l is not PROLOGUE:
                    act.wait_ge(tile_done, nth(tile_done, l, g * GROUP_TILES + done(b - WSLOTS)))
                nc.scalar.activation(w_hi[:, slot, :, 0:cols], w_raw[:, slot, :, 0:cols], ACT.Copy).then_inc(w_hi_done, 1)

            def head_split(l, b):
                split_hi(l, b, JOBS[b // KB][3] if b < HEAD_BLOCKS else 512)

            def sum_squares(l, key, src):
                r = STATS[key]
                act.wait_ge(rooted, nth(rooted, l, r - 1))
                nc.scalar.activation(squares[:, r % 2], src, ACT.Square, accum_out=sumsq[:, r % 2]).then_inc(summed, 1)

            def branch_squares(l, e, half, t, src):
                if half == 0:
                    nc.scalar.activation(half_squares[e][:, t], src, ACT.Square, scale=D ** -0.5,
                                         accum_out=half_sum[:, t:t + 1]).then_inc(half_summed, 1)
                    return
                r = STATS[e, t]
                act.wait_ge(rooted, nth(rooted, l, r - 1))
                nc.scalar.activation(squares[:, r % 2, 0:512], src, ACT.Square, scale=D ** -0.5,
                                     accum_out=sumsq[:, r % 2]).then_inc(summed, 1)

            def turn_hi(l, key, dst, t):
                n = TURNED[key]
                for half in range(2):
                    act.wait_ge(turned, nth(turned, l, 2 * n + half + 1))
                    nc.scalar.activation(dst[:, half * BK:(half + 1) * BK, t * P:(t + 1) * P],
                                         work[:, 2 * (n % 2) + half].rearrange("p (k c) -> p k c", k=BK),
                                         ACT.Copy).then_inc(turned_hi, 1)

            def empty(l, b, t):
                name, _, _, cols, _, _, moving = JOBS[b // KB]
                src = proj[:, t, 0:moving]
                act.wait_ge(tile_done, nth(tile_done, l, done(b, t)))
                if name in BRANCH_JOBS:
                    branch_squares(l, "e1" if name[0] == "o" else "e2", int(name[-1]), t, src)
                    return
                func, scale = ACT.Copy, 1.0
                if name == "va":
                    dst = va[:, t]
                elif name == "qa":
                    dst, scale = qaT[:, t], HD ** -0.5
                elif name == "ka":
                    dst = kaT[:, t]
                elif name == "uv":
                    nc.scalar.activation(ys[:, t, AW:AW + BW], proj[:, t, 0:BW], func)
                    src, dst = proj[:, t, BW:2 * BW], vs[:, t]
                elif name in ("qc", "kc"):
                    lo = CW * (name == "kc")
                    dst = qkc[:, t, lo:lo + CW]
                elif name == "vc":
                    dst = vc[:, t]
                elif name == "gc":
                    dst, func = ys[:, t, AW + BW:D], ACT.Silu
                elif name in ("km0", "km1"):
                    dst = kmT[:, 4 * int(name[-1]) + t]
                elif name in ("vm0", "vm1"):
                    lo = 512 * int(name[-1])
                    dst = vm[:, t, lo:lo + 512]
                else:
                    dst, scale = qxT[:, 4 * int(name[-1]) + t], XD ** -0.5
                nc.scalar.activation(dst, src, func, scale=scale).then_inc(emptied, 1)

            def a_step(l, j):
                if j < UNITS:
                    n = (j // NH + 1) * P
                    act.wait_ge(masked, nth(masked, l, j + 1))
                    nc.scalar.activation(probs[:, j % 2, 0:n], probs[:, j % 2, 0:n], ACT.Exp, scale=-1.0,
                                         bias=neg_max[:, j % 2, 0:1], accum_out=den[:, j:j + 1]).then_inc(exped, 1)
                if 1 <= j <= UNITS:
                    u = j - 1
                    n = (u // NH + 1) * P
                    act.wait_ge(p_turned, nth(p_turned, l, u + 1))
                    act.wait_ge(weighed, nth(weighed, l, u - 1))
                    nc.scalar.copy(probsT[:, u % 2, 0:n], work[:, 2, 0:n]).then_inc(p_copied, 1)

            def c_copy(l, c):
                act.wait_ge(c_turned, nth(c_turned, l, c + 1))
                nc.scalar.copy(qkT[:], work[:, 0:2, 0:CW]).then_inc(c_copied, 1)

            def x_step(l, j):
                if j < XUNITS:
                    act.wait_ge(x_max, nth(x_max, l, j + 1))
                    act.wait_ge(x_turned, nth(x_turned, l, j - 1))
                    for i in range(2):
                        last = nc.scalar.activation(x_probs[:, j % 2, i * MEM:(i + 1) * MEM], work[:, j % 2, i * MEM:(i + 1) * MEM],
                                                    ACT.Exp, bias=x_neg[:, j % 2, i:i + 1], accum_out=x_den[:, j, i:i + 1])
                    last.then_inc(x_exped, 1)
                if j >= 2:
                    pair, t = divmod(j - 2, T)
                    act.wait_ge(x_weighed, nth(x_weighed, l, j - 1))
                    nc.scalar.activation(hT_hi[:, pair * BK:(pair + 1) * BK, t * P:(t + 1) * P],
                                         work[:, 3].rearrange("p (k c) -> p k c", k=BK), ACT.Copy).then_inc(x_hi, 1)
                if 1 <= j <= XUNITS:
                    u = j - 1
                    act.wait_ge(x_turned, nth(x_turned, l, u + 1))
                    act.wait_ge(x_weighed, nth(x_weighed, l, u - 1))
                    nc.scalar.copy(x_probsT[:, u % 2], work[:, 2]).then_inc(x_copied, 1)

            def after_tile(l, b, t):
                if b == FIRST_BLOCK["out0"] - 1 and t >= T - 2:
                    turn_hi(l, ("mix", t - T + 2), hT_hi, t - T + 2)
                if b == FIRST_BLOCK["out0"] and t < T - 2:
                    turn_hi(l, ("mix", t + 2), hT_hi, t + 2)
                if b == FIRST_BLOCK["out0"] + 1 and t < MT:
                    turn_hi(l, ("memv", t), memT_hi, t)
                j = unit_step(b, t)
                if 0 <= j < UNITS + 2:
                    a_step(l, j)
                k = (b - FIRST_BLOCK["gc"]) * T + t + 2
                if 0 <= k < 2 * T and k % 2 == 0:
                    c_copy(l, k // 2)
                if b == FIRST_BLOCK["qx1"] + 1 and t % 2:
                    x_step(l, t // 2)
                if b == FIRST_BLOCK["wo0"]:
                    x_step(l, XUNITS - 2 + t)

            def before_block(l, b):
                if b == FIRST_BLOCK["qc"]:
                    act.wait_ge(emptied, nth(emptied, l, TILES_BEFORE["qc"]))
                    nc.scalar.activation(ys[:, :, AW:AW + BW], ys[:, :, AW:AW + BW], ACT.Gelu_apprx_tanh)
                    nc.scalar.activation(vs[:], vs[:], ACT.Gelu_apprx_tanh).then_inc(gelu_done, 1)
                for phase, fill in FILLED.items():
                    k = b - FIRST_BLOCK[fill]
                    for t in FILL_SQUARES.get(k, ()):
                        if phase == "n1":
                            act.wait_ge(x_loaded[t], 16)
                            act.wait_ge(x_ready, nth(x_ready, l, t + 1 - T))
                        else:
                            act.wait_ge(x_ready, nth(x_ready, l, BRANCHED["e1", t] + 1))
                        sum_squares(l, (phase, t), xs[:, t])
                    for t in FILL_HI.get(k, ()):
                        turn_hi(l, (phase, t), hT_hi, t)

            def mlp_group(l, g, last):
                for i in range(GROUP_BLOCKS):
                    b = HEAD_BLOCKS + i
                    if i > 0:
                        split_hi(l, b + 1, g=g)
                    if last and i == 0:
                        act.wait_ge(turned, nth(turned, l, 2 * TURNED["n3", T - 1] + 2))
                        for t in range(MT):
                            act.dma_start(hs[:, t], mem[0, t * P:(t + 1) * P]).then_inc(mem_loaded, 16)
                        act.dma_start(gains[:, GAIN_SLOT["mem"]],
                                      norm_g[DEPTH - 1:DEPTH, GAIN["mem"]].broadcast_to([P, D])).then_inc(gain_loaded["mem"], 16)
                    if last and i == 5:
                        for t in range(MT):
                            turn_hi(l, ("memk", t), memT_hi, t)
                    if last and i in (5, 7):
                        for t in range(T):
                            half = (i - 5) // 2
                            act.wait_ge(added, nth(added, l, g * UP_TILES + (T * half + t + 1)))
                            branch_squares(l, "e3", half, t, ys[:, t, half * 512:(half + 1) * 512])
                    if i in (1, 3):
                        for t in range(5):
                            m = 2 * (i - 1) + t
                            if t < 4:
                                act.wait_ge(tile_done, nth(tile_done, l, g * GROUP_TILES + done(b, t)))
                                act.wait_ge(hidden_lo, nth(hidden_lo, l, g * UP_TILES + (m - 1)))
                                nc.scalar.activation(relu[:, m % 2], proj[:, t], ACT.Relu).then_inc(emptied, 1)
                            if t >= 1:
                                act.wait_ge(hidden_sq, nth(hidden_sq, l, g * UP_TILES + m))
                                nc.scalar.activation(uT_hi[:, m - 1], relu[:, (m - 1) % 2], ACT.Copy).then_inc(hidden_hi, 1)

            for t in range(MT):
                act.wait_ge(mem_loaded, 16 * MT)
                nc.scalar.activation(squares[:, t], hs[:, t], ACT.Square, accum_out=mem_sumsq[:, t:t + 1]).then_inc(mem_summed, 1)
            split_hi(PROLOGUE, BLOCKS)
            for t in range(MT):
                turn_hi(PROLOGUE, ("memk", t), memT_hi, t)
            for dst, src in ((upper, c_upper), (decay, c_decay), (log_count, c_logcount)):
                act.dma_start(dst[:], src).then_inc(const_loaded, 16)

            with act.Fori(0, DEPTH) as l:
                for b in range(HEAD_BLOCKS):
                    if b < HEAD_BLOCKS - 1:
                        head_split(l, b + 1)
                    before_block(l, b)
                    tiles = JOBS[b // KB][5]
                    if b < HEAD_BLOCKS - 1:
                        for t in range(tiles):
                            if b % KB == KB - 1:
                                empty(l, b, t)
                            after_tile(l, b, t)
                    if b == FIRST_BLOCK["qx1"] + 1:
                        for j in range(2, XUNITS - 2):
                            x_step(l, j)
                for what, t in N3_ACT:
                    if what == "e":
                        empty(l, HEAD_BLOCKS - 1, t)
                    elif what == "x":
                        act.wait_ge(x_ready, nth(x_ready, l, BRANCHED["e2", t] + 1))
                        sum_squares(l, ("n3", t), xs[:, t])
                    elif what == "h":
                        turn_hi(l, ("n3", t), hT_hi, t)
                    else:
                        split_hi(l, HEAD_BLOCKS + t)
                with act.Fori(0, GROUPS - 1) as g:
                    mlp_group(l, g, False)
                    split_hi(l, HEAD_BLOCKS + GROUP_BLOCKS + 1, g=g)
                mlp_group(l, GROUPS - 1, True)

        @block.vector
        def _(dve):
            start_counts(dve, w_lo_done, added, gained, hidden_sq, hidden_lo, sgu_ready,
                         masked, a_out, c_masked, c_state, c_centred, x_max, x_lo)
            setup_steps = [0]

            def setup(ins):
                setup_steps[0] += 1
                ins.then_inc(dve_setup, 1)
                dve.wait_ge(dve_setup, setup_steps[0])

            dve.wait_ge(first_loaded, 16 * 3)
            setup(nc.vector.tensor_copy(pos_f[:], pos_i[:]))
            setup(nc.vector.tensor_tensor(angle[:], again(inv[:], T), spread(pos_f[:], HALF), ALU.mult))
            round_up = 1.5 * 2.0 ** 23
            setup(nc.vector.tensor_scalar(turns[:], angle[:], 1.0 / TURN, round_up, ALU.mult, ALU.add))
            setup(nc.vector.tensor_scalar(turns[:], turns[:], -round_up, None, ALU.add))
            for piece in TURN_PIECES:
                setup(nc.vector.scalar_tensor_tensor(out=angle[:], in0=turns[:], scalar=-piece, in1=angle[:],
                                                     op0=ALU.mult, op1=ALU.add))
            pi = float(np.nextafter(np.float32(np.pi), np.float32(0)))
            setup(nc.vector.tensor_scalar(angle[:], angle[:], pi, -pi, ALU.min, ALU.max))
            setup(nc.vector.scalar_tensor_tensor(out=turns[:], in0=angle[:], scalar=-1.0, in1=angle[:],
                                                 op0=ALU.mult, op1=ALU.max))
            setup(nc.vector.tensor_scalar(turns[:], turns[:], -1.0, float(np.float32(np.pi / 2)), ALU.mult, ALU.add))
            dve.sem_inc(trig_done, 1)

            def split_lo(l, b, cols=512, g=0):
                slot = b % WSLOTS
                dve.wait_ge(w_hi_done, nth(w_hi_done, l, g * GROUP_BLOCKS + (b + 1)))
                nc.vector.tensor_tensor(w_lo[:, slot, :, 0:cols], w_raw[:, slot, :, 0:cols],
                                        w_hi[:, slot, :, 0:cols].bitcast(F32), ALU.subtract).then_inc(w_lo_done, 1)

            def head_split(l, b):
                split_lo(l, b, JOBS[b // KB][3] if b < HEAD_BLOCKS else 512)

            def norm(l, key, src):
                n, t = NORMED[key], key[1]
                r = STATS[key]
                before = [k for k in NORMED if NORMED[k] < n and k[1] % 2 == t % 2]
                free = 2 * TURNED[before[-1]] + 2 if before else 0
                at0, at1, at2 = values(dve, nth(rooted, l, r + 1), nth(gain_loaded[key[0]], l, 16), nth(turned, l, free))
                dve.wait_ge(rooted, at0)
                dve.wait_ge(gain_loaded[key[0]], at1)
                dve.wait_ge(turned, at2)
                nc.vector.scalar_tensor_tensor(out=hs[:, t % 2], in0=src, scalar=rstd[:, r],
                                               in1=gains[:, GAIN_SLOT[key[0]]], op0=ALU.mult,
                                               op1=ALU.mult).then_inc(normed, 1)

            def norm_mem(l, phase, t):
                loads = 16 * MT * (1 if phase == "memv" else 2)
                if l is PROLOGUE:
                    dve.wait_ge(mem_loaded, nth(mem_loaded, l, loads))
                    dve.wait_ge(gain_loaded["mem"], nth(gain_loaded["mem"], l, 16))
                    dve.wait_ge(mem_rooted, 1)
                else:
                    at0, at1 = values(dve, nth(mem_loaded, l, loads), nth(gain_loaded["mem"], l, 0 if phase == "memv" else 16))
                    dve.wait_ge(mem_loaded, at0)
                    dve.wait_ge(gain_loaded["mem"], at1)
                nc.vector.scalar_tensor_tensor(out=hs[:, t], in0=hs[:, t], scalar=mem_rstd[:, t:t + 1],
                                               in1=gains[:, GAIN_SLOT["mem"]], op0=ALU.mult,
                                               op1=ALU.mult).then_inc(normed, 1)

            def gain(l, e, half, t):
                h = slice(half * 512, (half + 1) * 512)
                if half:
                    at0, at1 = values(dve, nth(summed, l, STATS[e, t] + 1), nth(gain_loaded[e], l, 16))
                    dve.wait_ge(summed, at0)
                else:
                    at0, at1 = values(dve, nth(half_summed, l, BRANCHED[e, t] + 1), nth(gain_loaded[e], l, 16))
                    dve.wait_ge(half_summed, at0)
                dve.wait_ge(gain_loaded[e], at1)
                nc.vector.tensor_tensor(ys[:, t, h], ys[:, t, h] if e == "e3" else proj[:, t],
                                        gains[:, GAIN_SLOT[e], h], ALU.mult).then_inc(gained, 1)

            def update(l, e, t):
                at0, at1 = values(dve, nth(rooted, l, STATS[e, t] + 1), nth(gained, l, GAINED[e, 1, t] + 1))
                dve.wait_ge(rooted, at0)
                dve.wait_ge(gained, at1)
                nc.vector.scalar_tensor_tensor(out=xs[:, t], in0=ys[:, t], scalar=rstd[:, STATS[e, t]], in1=xs[:, t],
                                               op0=ALU.mult, op1=ALU.add).then_inc(x_ready, 1)

            def turn_lo(l, key, hi, lo, t):
                n = TURNED[key]
                for half in range(2):
                    dve.wait_ge(turned_hi, nth(turned_hi, l, 2 * n + half + 1))
                    at = (slice(None), slice(half * BK, (half + 1) * BK), slice(t * P, (t + 1) * P))
                    nc.vector.tensor_tensor(lo[at], work[:, 2 * (n % 2) + half].rearrange("p (k c) -> p k c", k=BK),
                                            hi[at].bitcast(F32), ALU.subtract).then_inc(turned_lo, 1)

            def a_step(l, links, j):
                if j < UNITS:
                    t = j // NH
                    n = (t + 1) * P
                    at0, at1 = values(dve, nth(scored, l, j + 1), nth(p_turned, l, j - 1))
                    dve.wait_ge(scored, at0)
                    dve.wait_ge(p_turned, at1)
                    dve.sem_inc(waits_passed, 1)
                    nc.vector.tensor_tensor_reduce(out=probs[:, j % 2, 0:n], in0=work[:, j % 2, 0:n],
                                                   in1=log_count[:, S - n:S],
                                                   scale=-1.0, scalar=3e38, op0=ALU.add, op1=ALU.min,
                                                   accum_out=neg_max[:, j % 2, 0:1]).then_inc(masked, 1)
                if j >= 2 and (j - 2) % NH == NH - 1:
                    t = (j - 2) // NH
                    heads = slice(t * NH, (t + 1) * NH)
                    dve.wait_ge(exped, nth(exped, l, (t + 1) * NH))
                    nc.vector.reciprocal(rden[:, heads], den[:, heads]).then_inc(dve_link, 1)
                    dve.wait_ge(dve_link, nth(dve_link, l, next(links)))
                    dve.sem_inc(waits_passed, 1)
                    dve.wait_ge(weighed, nth(weighed, l, (t + 1) * NH))
                    nc.vector.tensor_tensor(ys[:, t, 0:AW].rearrange("p (h e) -> p h e", h=NH),
                                            work[:, 3, 0:AW].rearrange("p (h e) -> p h e", h=NH),
                                            spread(rden[:, heads], HD), ALU.mult).then_inc(a_out, 1)

            def layer_norm(l, links):
                dve.wait_ge(gelu_done, nth(gelu_done, l, 1))
                for t in range(T):
                    last = nc.vector.bn_stats(ln_stats[:, t], vs[:, t])
                last.then_inc(dve_link, 1)
                dve.wait_ge(dve_link, nth(dve_link, l, next(links)))
                dve.sem_inc(waits_passed, 1)
                for t in range(T):
                    last = nc.vector.bn_aggr(ln_mv[:, t], ln_stats[:, t])
                last.then_inc(ln_var, 1)

            def layer_norm_scale(l):
                dve.wait_ge(ln_root, nth(ln_root, l, 1))
                for t in range(T):
                    last = nc.vector.tensor_scalar(vs[:, t], vs[:, t], ln_mv[:, t, 0:1], ln_rstd[:, t:t + 1],
                                                   ALU.subtract, ALU.mult)
                last.then_inc(ln_scaled, 1)

            def gate(l):
                for g in range(G):
                    dve.wait_ge(gated, nth(gated, l, g // 2 + 1))
                    dst = ys[:, :, AW + g * HD:AW + (g + 1) * HD]
                    last = nc.vector.scalar_tensor_tensor(
                        out=dst, in0=work[:, g // 2, (g % 2) * 256:(g % 2 + 1) * 256].rearrange("p (t c) -> p t c", t=T),
                        scalar=sgu_bias[:, g:g + 1], in1=dst, op0=ALU.add, op1=ALU.mult)
                last.then_inc(gate_out, 1)

            def c_mask(l, c):
                dve.wait_ge(c_inner, nth(c_inner, l, c + 1))
                for i in range(2):
                    last = nc.vector.tensor_tensor(innerT[:, i:NH:2],
                                                   work[:, 2 + i, 0:CW].rearrange("p (h c) -> p h c", h=3),
                                                   again(upper[:], 3), ALU.mult)
                last.then_inc(c_masked, 1)
                if c == T - 1:
                    return
                at0, at1 = values(dve, nth(c_kv, l, c + 1), nth(c_state, l, c))
                dve.wait_ge(c_kv, at0)
                dve.wait_ge(c_state, at1)
                if c:
                    dve.wait_ge(c_y, nth(c_y, l, c))
                for lo in (0, HD):
                    at = (slice(lo, lo + HD), slice(None), slice(lo, lo + HD))
                    kv = work[:, 0, 0:CW].rearrange("p (h c) -> p h c", h=PAIRS)[at]
                    new, old = state[:, (c + 1) % 2][at], state[:, c % 2][at]
                    if c == 0:
                        last = nc.vector.tensor_copy(new, kv)
                    else:
                        last = nc.vector.tensor_tensor(new, kv, old, ALU.add)
                last.then_inc(c_state, 1)

            def group_norm(l, links, c):
                dve.wait_ge(c_y, nth(c_y, l, c + 1))
                y = work[:, 2, 0:CW].rearrange("p (h e) -> p h e", h=NH)
                ych = yc[:, c].rearrange("p (h e) -> p h e", h=NH)
                nc.vector.reduce_sum(gn_sum[:], y, AX_X).then_inc(dve_link, 1)
                dve.wait_ge(dve_link, nth(dve_link, l, next(links)))
                dve.sem_inc(waits_passed, 1)
                nc.vector.tensor_scalar(gn_mean[:], gn_sum[:], 1.0 / HD, None, ALU.mult).then_inc(dve_link, 1)
                dve.wait_ge(dve_link, nth(dve_link, l, next(links)))
                dve.sem_inc(waits_passed, 1)
                nc.vector.tensor_tensor(ych, y, spread(gn_mean[:], HD), ALU.subtract).then_inc(c_centred, 1)
                dve.wait_ge(c_centred, nth(c_centred, l, c + 1))
                nc.vector.tensor_tensor(yc2[:], yc[:, c], yc[:, c], ALU.mult).then_inc(dve_link, 1)
                dve.wait_ge(dve_link, nth(dve_link, l, next(links)))
                dve.sem_inc(waits_passed, 1)
                nc.vector.reduce_sum(gn_var[:], yc2[:].rearrange("p (h e) -> p h e", h=NH), AX_X).then_inc(gn_var_done, 1)

            def group_scale(l, links, c):
                ych = yc[:, c].rearrange("p (h e) -> p h e", h=NH)
                dve.wait_ge(gn_root, nth(gn_root, l, c + 1))
                nc.vector.tensor_tensor(ych, ych, spread(gn_rstd[:], HD), ALU.mult).then_inc(dve_link, 1)
                dve.wait_ge(dve_link, nth(dve_link, l, next(links)))
                dve.sem_inc(waits_passed, 1)

            def c_gate(l, c):
                dve.wait_ge(emptied, nth(emptied, l, TILES_BEFORE["gc"] + c + 1))
                nc.vector.tensor_tensor(ys[:, c, AW + BW:D], ys[:, c, AW + BW:D], yc[:, c], ALU.mult).then_inc(c_out, 1)

            def x_step(l, links, j):
                if 1 <= j <= XUNITS:
                    u = j - 1
                    dve.wait_ge(x_exped, nth(x_exped, l, u + 1))
                    nc.vector.reciprocal(x_rden[:, u], x_den[:, u]).then_inc(dve_link, 1)
                    dve.wait_ge(dve_link, nth(dve_link, l, next(links)))
                    dve.sem_inc(waits_passed, 1)
                    two = x_probs[:, u % 2].rearrange("p (h m) -> p h m", h=2)
                    nc.vector.tensor_tensor(two, two, spread(x_rden[:, u], MEM), ALU.mult).then_inc(x_normed, 1)
                if j < XUNITS:
                    dve.wait_ge(x_scored, nth(x_scored, l, j + 1))
                    nc.vector.reduce_max(x_top[:, j % 2], work[:, j % 2].rearrange("p (h m) -> p h m", h=2), AX_X).then_inc(dve_link, 1)
                    dve.wait_ge(dve_link, nth(dve_link, l, next(links)))
                    dve.sem_inc(waits_passed, 1)
                    dve.wait_ge(x_exped, nth(x_exped, l, j - 1))
                    nc.vector.tensor_scalar(x_neg[:, j % 2], x_top[:, j % 2], -1.0, None, ALU.mult).then_inc(x_max, 1)
                if j >= 2:
                    pair, t = divmod(j - 2, T)
                    at = (slice(None), slice(pair * BK, (pair + 1) * BK), slice(t * P, (t + 1) * P))
                    dve.wait_ge(x_hi, nth(x_hi, l, j - 1))
                    nc.vector.tensor_tensor(hT_lo[at], work[:, 3].rearrange("p (k c) -> p k c", k=BK),
                                            hT_hi[at].bitcast(F32), ALU.subtract).then_inc(x_lo, 1)

            def after_tile(l, links, b, t):
                if b == FIRST_BLOCK["out0"] and t < T - 2:
                    turn_lo(l, ("mix", t + 2), hT_hi, hT_lo, t + 2)
                if b == FIRST_BLOCK["out0"] + 1:
                    gain(l, "e1", 0, t)
                    if t < MT:
                        turn_lo(l, ("memv", t), memT_hi, memT_lo, t)
                if b == FIRST_BLOCK["wo0"] + 1:
                    gain(l, "e2", 0, t)
                if b == FIRST_BLOCK["out1"] + 1:
                    gain(l, "e1", 1, t)
                    update(l, "e1", t)
                if b == FIRST_BLOCK["ka"] + 1 and t == 0:
                    dve.wait_ge(const_loaded, 16 * 3)
                    dve.wait_ge(sgu_turned, nth(sgu_turned, l, 1))
                    nc.vector.tensor_tensor(sgu_T[:], work[:, 0].rearrange("p (g i) -> p g i", g=G),
                                            again(upper[:], G),
                                            ALU.mult).then_inc(sgu_ready, 1)
                j = unit_step(b, t)
                if 0 <= j < UNITS + 2:
                    a_step(l, links, j)
                if j == UNITS + 3:
                    gate(l)
                k = (b - FIRST_BLOCK["gc"]) * T + t + 2
                if 0 <= k < 2 * T:
                    if k % 2:
                        c_mask(l, k // 2)
                        if k >= 3:
                            group_scale(l, links, k // 2 - 1)
                    elif k >= 2:
                        group_norm(l, links, k // 2 - 1)
                if k == 2 * T - 1:
                    c_gate(l, 0)
                if k == 2 * T:
                    c_gate(l, 1)
                    group_norm(l, links, T - 1)
                    turn_lo(l, ("mix", 0), hT_hi, hT_lo, 0)
                if k == 2 * T + 1:
                    c_gate(l, 2)
                    turn_lo(l, ("mix", 1), hT_hi, hT_lo, 1)
                    group_scale(l, links, T - 1)
                    c_gate(l, 3)
                if b == FIRST_BLOCK["qx1"] + 1 and t % 2:
                    x_step(l, links, t // 2)
                if b == FIRST_BLOCK["wo0"]:
                    x_step(l, links, XUNITS - 2 + t)

            def before_block(l, links, b):
                if b == FIRST_BLOCK["qc"]:
                    layer_norm(l, links)
                if b == FIRST_BLOCK["qc"] + 1:
                    layer_norm_scale(l)
                for phase, fill in FILLED.items():
                    k = b - FIRST_BLOCK[fill]
                    for t in FILL_HI.get(k, ()):
                        turn_lo(l, (phase, t), hT_hi, hT_lo, t)
                    for t in FILL_SQUARES.get(k, ()):
                        norm(l, (phase, t), xs[:, t])

            def mlp_group(l, g, last):
                for i in range(GROUP_BLOCKS):
                    b = HEAD_BLOCKS + i
                    if i > 0:
                        split_lo(l, b + 1, g=g)
                    if last and i == 4:
                        for t in range(MT):
                            norm_mem(l, "memk", t)
                    if last and i == 5:
                        for t in range(MT):
                            turn_lo(l, ("memk", t), memT_hi, memT_lo, t)
                    if i in (1, 3):
                        for t in range(5):
                            m = 2 * (i - 1) + t
                            if t < 4:
                                dve.wait_ge(emptied, nth(emptied, l, g * UP_TILES + (HEAD_TILES + m + 1)))
                                nc.vector.tensor_tensor(relu[:, m % 2], relu[:, m % 2], relu[:, m % 2],
                                                        ALU.mult).then_inc(hidden_sq, 1)
                            if t >= 1:
                                dve.wait_ge(hidden_hi, nth(hidden_hi, l, g * UP_TILES + m))
                                nc.vector.tensor_tensor(uT_lo[:, m - 1], relu[:, (m - 1) % 2], uT_hi[:, m - 1].bitcast(F32),
                                                        ALU.subtract).then_inc(hidden_lo, 1)
                    if i in (5, 7):
                        for t in range(T):
                            j = (i - 5) // 2
                            at0, at1 = values(dve, nth(tile_done, l, g * GROUP_TILES + done(b, t)), nth(y_zeroed, l, 1))
                            dve.wait_ge(tile_done, at0)
                            dve.wait_ge(y_zeroed, at1)
                            part_y = ys[:, t, j * 512:(j + 1) * 512]
                            nc.vector.tensor_tensor(part_y, proj[:, t], part_y, ALU.add).then_inc(added, 1)
                            if last and j == 1 and t >= 1:
                                gain(l, "e3", 1, t - 1)
                                update(l, "e3", t - 1)
                        if last and j == 1:
                            gain(l, "e3", 1, T - 1)
                            update(l, "e3", T - 1)
                    if last and i == 6:
                        for t in range(T):
                            gain(l, "e3", 0, t)

            for t in range(MT):
                norm_mem(PROLOGUE, "memk", t)
            split_lo(PROLOGUE, BLOCKS)
            for t in range(MT):
                turn_lo(PROLOGUE, ("memk", t), memT_hi, memT_lo, t)

            with dve.Fori(0, DEPTH) as l:
                links = itertools.count(1)
                for b in range(HEAD_BLOCKS):
                    if b < HEAD_BLOCKS - 1:
                        head_split(l, b + 1)
                    before_block(l, links, b)
                    if b == HEAD_BLOCKS - 1:
                        continue
                    for t in range(JOBS[b // KB][5]):
                        after_tile(l, links, b, t)
                    if b == FIRST_BLOCK["out0"]:
                        for t in range(MT):
                            norm_mem(l, "memv", t)
                    if b == FIRST_BLOCK["qx1"] + 1:
                        for j in range(2, XUNITS - 2):
                            x_step(l, links, j)
                for what, t in N3_DVE:
                    if what == "e":
                        gain(l, "e2", 1, t)
                    elif what == "x":
                        update(l, "e2", t)
                    elif what == "n":
                        norm(l, ("n3", t), xs[:, t])
                    elif what == "h":
                        turn_lo(l, ("n3", t), hT_hi, hT_lo, t)
                    else:
                        split_lo(l, HEAD_BLOCKS + t)
                with dve.Fori(0, GROUPS - 1) as g:
                    mlp_group(l, g, False)
                    split_lo(l, HEAD_BLOCKS + GROUP_BLOCKS + 1, g=g)
                mlp_group(l, GROUPS - 1, True)
                assert next(links) == DVE_LINKS + 1

        @block.gpsimd
        def _(pool):
            nc.gpsimd.memset(minus_half[:], -0.5).then_inc(setup_done, 1)
            nc.gpsimd.memset(state[:], 0.0).then_inc(setup_done, 1)
            pool.wait_ge(setup_done, 2)
            start_counts(pool, rooted, x_ready)

            def root(l, links, key):
                r = STATS[key]
                pool.wait_ge(summed, nth(summed, l, r + 1))
                pool.sem_inc(waits_passed, 1)
                nc.gpsimd.tensor_scalar(meansq[:, r % 2], sumsq[:, r % 2], 1.0 / D, EPS, ALU.mult, ALU.add).then_inc(pool_link, 1)
                pool.wait_ge(pool_link, nth(pool_link, l, next(links)))
                pool.sem_inc(waits_passed, 1)
                nc.gpsimd.tensor_tensor(rstd[:, r], meansq[:, r % 2], minus_half[:, 0:1], ALU.pow).then_inc(rooted, 1)

            def branch_halves(l, links, e):
                pool.wait_ge(half_summed, nth(half_summed, l, BRANCHED[e, T - 1] + 1))
                pool.sem_inc(waits_passed, 1)
                nc.gpsimd.tensor_scalar(half_mean[:], half_sum[:], EPS, None, ALU.add).then_inc(pool_link, 1)
                pool.wait_ge(pool_link, nth(pool_link, l, next(links)))
                pool.sem_inc(waits_passed, 1)

            def branch_root(l, links, e, t):
                r = STATS[e, t]
                pool.wait_ge(summed, nth(summed, l, r + 1))
                pool.sem_inc(waits_passed, 1)
                nc.gpsimd.tensor_tensor(meansq[:, r % 2], sumsq[:, r % 2], half_mean[:, t:t + 1], ALU.add).then_inc(pool_link, 1)
                pool.wait_ge(pool_link, nth(pool_link, l, next(links)))
                pool.sem_inc(waits_passed, 1)
                nc.gpsimd.tensor_tensor(rstd[:, r], meansq[:, r % 2], minus_half[:, 0:1], ALU.pow).then_inc(rooted, 1)

            def rotate(l, links, t):
                pool.wait_ge(emptied, nth(emptied, l, TILES_BEFORE["kc"] + t + 1))
                x12 = qkc[:, t].rearrange("p (h s e) -> p h s e", s=2, e=HALF)
                x1, x2 = x12[:, :, 0], x12[:, :, 1]
                a, b_, c = (rot[:, i].rearrange("p (h e) -> p h e", e=HALF) for i in range(3))
                cs = again(cos[:, t], 2 * NH)
                sn = again(sin[:, t], 2 * NH)
                nc.gpsimd.tensor_tensor(a, x1, cs, ALU.mult)
                nc.gpsimd.tensor_tensor(b_, x2, sn, ALU.mult)
                nc.gpsimd.tensor_tensor(c, x1, sn, ALU.mult)
                nc.gpsimd.tensor_tensor(x2, x2, cs, ALU.mult).then_inc(pool_link, 1)
                pool.wait_ge(pool_link, nth(pool_link, l, next(links)))
                nc.gpsimd.tensor_tensor(x1, a, b_, ALU.subtract)
                nc.gpsimd.tensor_tensor(x2, x2, c, ALU.add).then_inc(pool_link, 1)
                pool.wait_ge(pool_link, nth(pool_link, l, next(links)))
                every = qkc[:, t].rearrange("p (h e) -> p h e", e=HD)
                nc.gpsimd.tensor_tensor(every, every, spread(decay[:, t], HD),
                                        ALU.mult).then_inc(rotated, 1)

            pool.wait_ge(mem_summed, MT)
            nc.gpsimd.tensor_scalar(mem_meansq[:], mem_sumsq[:], 1.0 / D, EPS, ALU.mult, ALU.add).then_inc(setup_done, 1)
            pool.wait_ge(setup_done, 3)
            nc.gpsimd.tensor_tensor(mem_rstd[:], mem_meansq[:], minus_half[:, 0:MT], ALU.pow).then_inc(mem_rooted, 1)
            for t in range(1, T):
                pool.dma_start(xs[:, t], x[0, t * P:(t + 1) * P]).then_inc(x_loaded[t], 16)

            with pool.Fori(0, DEPTH) as l:
                links = itertools.count(1)
                for t in range(T):
                    root(l, links, ("n1", t))
                pool.wait_ge(ln_var, nth(ln_var, l, 1))
                pool.sem_inc(waits_passed, 1)
                nc.gpsimd.tensor_scalar(ln_ve[:], ln_mv[:, :, 1], EPS, None, ALU.add).then_inc(pool_link, 1)
                pool.wait_ge(pool_link, nth(pool_link, l, next(links)))
                pool.sem_inc(waits_passed, 1)
                nc.gpsimd.tensor_tensor(ln_rstd[:], ln_ve[:], minus_half[:, 0:T], ALU.pow).then_inc(ln_root, 1)
                pool.wait_ge(ln_scaled, nth(ln_scaled, l, 1))
                pool.wait_ge(sgu_loaded, nth(sgu_loaded, l, 64))
                g4 = again(ln_gain[:], T)
                s4 = again(ln_shift[:], T)
                nc.gpsimd.tensor_tensor(vs[:], vs[:], g4, ALU.mult).then_inc(pool_link, 1)
                pool.wait_ge(pool_link, nth(pool_link, l, next(links)))
                pool.sem_inc(waits_passed, 1)
                nc.gpsimd.tensor_tensor(vs[:], vs[:], s4, ALU.add).then_inc(ln_done, 1)
                pool.wait_ge(trig_done, 2)
                pool.wait_ge(const_loaded, 16 * 3)
                for t in range(T):
                    rotate(l, links, t)
                for c in range(T):
                    pool.wait_ge(gn_var_done, nth(gn_var_done, l, c + 1))
                    pool.sem_inc(waits_passed, 1)
                    nc.gpsimd.tensor_scalar(gn_ve[:], gn_var[:], 1.0 / HD, EPS, ALU.mult, ALU.add).then_inc(pool_link, 1)
                    pool.wait_ge(pool_link, nth(pool_link, l, next(links)))
                    pool.sem_inc(waits_passed, 1)
                    nc.gpsimd.tensor_tensor(gn_rstd[:], gn_ve[:], minus_half[:, 0:NH], ALU.pow).then_inc(gn_root, 1)
                branch_halves(l, links, "e1")
                for t in range(T):
                    branch_root(l, links, "e1", t)
                for t in range(T):
                    root(l, links, ("n2", t))
                branch_halves(l, links, "e2")
                for what, t in N3_ACT:
                    if what == "e":
                        branch_root(l, links, "e2", t)
                    elif what == "x":
                        root(l, links, ("n3", t))
                pool.wait_ge(x_ready, nth(x_ready, l, BRANCHED["e2", T - 1] + 1))
                pool.sem_inc(waits_passed, 1)
                nc.gpsimd.memset(ys[:], 0.0).then_inc(y_zeroed, 1)
                branch_halves(l, links, "e3")
                for t in range(T):
                    branch_root(l, links, "e3", t)
                assert next(links) == POOL_LINKS + 1


NAMES = ["x", "mem", "positions", "norm_g", "w_in", "sgu_w", "sgu_b", "sgu_ln_g", "sgu_ln_b", "w_out",
         "x_wq", "x_wkv", "x_wo", "w_up", "w_down"]


def kernel(**inputs):
    import numpy as _np
    import concourse.bacc as _bacc
    from concourse import mybir as _mybir
    from concourse.bass_utils import run_bass_kernel_spmd as _run

    nc = _bacc.Bacc("TRN2", target_bir_lowering=False, num_devices=1)
    given = {name: _np.ascontiguousarray(inputs[name]) for name in NAMES} | shape_constants()
    given["positions"] = _np.ascontiguousarray(given["positions"].reshape(T, P).T)
    given["sgu_b"] = _np.ascontiguousarray(given["sgu_b"].transpose(0, 2, 1))
    arrays, args = {}, []
    for name, a in given.items():
        arrays[f"in_{name}_dram"] = a
        args.append(nc.dram_tensor(f"in_{name}_dram", a.shape, _mybir.dt.from_np(a.dtype), kind="ExternalInput").ap())
    args.append(nc.dram_tensor("out_dram", (1, S, D), _mybir.dt.float32, kind="ExternalOutput").ap())
    trunk(nc, *args)
    r = _run(nc, [arrays], core_ids=[0])
    return r.results[0]["out_dram"]
```
